# Optimizing a Trainium2 kernel written in Bass

```python
import jax, jax.numpy as jnp
from jax import lax
import numpy as np

D_MODEL = 1024
BATCH = 1
SEQ = 512
DEPTH = 1

ATTN_GROUPS = ((128, 1), (512, 4), (2048, 16))
N_ATTN_GROUPS = len(ATTN_GROUPS)
ATTN_HEADS_PER_GROUP = 4
ATTN_HEAD_DIM = 128
ATTN_WIDTH = N_ATTN_GROUPS * ATTN_HEADS_PER_GROUP * ATTN_HEAD_DIM
ATTN_OUT_WIDTH = ATTN_HEADS_PER_GROUP * ATTN_HEAD_DIM
ROPE_THETA = 500000.0
ROPE_DIM = ATTN_HEAD_DIM // 4
MLSTM_HEADS = 4
MLSTM_WIDTH = D_MODEL
MLSTM_HEAD_DIM = MLSTM_WIDTH // MLSTM_HEADS
MLSTM_CHUNK = 64
CONV_WIDTH = 4
N_EXPERTS = 32
TOP_K = 4
D_FF = D_MODEL
SWIGLU_LIMIT = 7.0
SWIGLU_ALPHA = 1.702
MOE_BLOCK = 128
RMS_EPS = 1e-5
LN_EPS = 1e-5

IN_SPLIT_SIZES = (ATTN_WIDTH, ATTN_WIDTH, ATTN_WIDTH,
                  MLSTM_WIDTH, MLSTM_WIDTH, MLSTM_WIDTH,
                  MLSTM_WIDTH,
                  MLSTM_HEADS, MLSTM_HEADS,
                  D_MODEL, D_MODEL)
D_IN = sum(IN_SPLIT_SIZES)

kernel_name = 'hybrid_dilated_attn_mlstm_moe_block'

def rms_norm(x, g):
    x32 = x.astype(jnp.float32)
    y = x32 * lax.rsqrt(jnp.mean(x32 * x32, axis=-1, keepdims=True) + RMS_EPS)
    return (y * g.astype(jnp.float32)).astype(x.dtype)

def partial_rotary(x, positions):
    half = ROPE_DIM // 2
    inv_freq = ROPE_THETA ** (-jnp.arange(half, dtype=jnp.float32) / half)
    ang = positions.astype(jnp.float32)[..., None] * inv_freq
    ang = ang.reshape(ang.shape[:2] + (1,) * (x.ndim - 3) + (half,))
    cos, sin = jnp.cos(ang), jnp.sin(ang)
    x32 = x.astype(jnp.float32)
    x1, x2 = x32[..., :half], x32[..., half:ROPE_DIM]
    out = jnp.concatenate([x1 * cos - x2 * sin, x2 * cos + x1 * sin, x32[..., ROPE_DIM:]], axis=-1)
    return out.astype(x.dtype)

def dilated_window_attention(q, k, v, window, dilation):
    B_, S_, H, Dh = q.shape
    sub = window // dilation
    L = S_ // dilation
    nblk = -(-L // sub)
    Lp = nblk * sub

    def to_sub(t):
        t = t.reshape(B_, L, dilation, H, Dh).transpose(0, 2, 3, 1, 4)
        t = jnp.pad(t, ((0, 0), (0, 0), (0, 0), (0, Lp - L), (0, 0)))
        return t.reshape(B_, dilation, H, nblk, sub, Dh)

    def with_prev(t):
        prev = jnp.pad(t, ((0, 0), (0, 0), (0, 0), (1, 0), (0, 0), (0, 0)))[:, :, :, :-1]
        return jnp.concatenate([prev, t], axis=-2)

    qb = to_sub(q)
    kk = with_prev(to_sub(k))
    vv = with_prev(to_sub(v))
    s = jnp.einsum('bdhnqe,bdhnke->bdhnqk', qb, kk, preferred_element_type=jnp.float32) * (Dh ** -0.5)
    blk = jnp.arange(nblk)[:, None, None] * sub
    q_pos = blk + jnp.arange(sub)[None, :, None]
    k_pos = blk - sub + jnp.arange(2 * sub)[None, None, :]
    rel = q_pos - k_pos
    valid = (rel >= 0) & (rel <= sub) & (k_pos >= 0)
    s = jnp.where(valid, s, -jnp.inf)
    m = jnp.max(s, axis=-1, keepdims=True)
    p = jnp.exp(s - m)
    den = jnp.sum(p, axis=-1)
    out = jnp.einsum('bdhnqk,bdhnke->bdhnqe', p, vv.astype(jnp.float32)) / den[..., None]
    lse = m[..., 0] + jnp.log(den)
    out = out.reshape(B_, dilation, H, Lp, Dh)[:, :, :, :L].transpose(0, 3, 1, 2, 4).reshape(B_, S_, H, Dh)
    lse = lse.reshape(B_, dilation, H, Lp)[..., :L].transpose(0, 3, 1, 2).reshape(B_, S_, H)
    return out, lse

def dilated_attention_mixer(aq, ak, av, positions):
    B_, S_, _ = aq.shape
    shp = (B_, S_, N_ATTN_GROUPS, ATTN_HEADS_PER_GROUP, ATTN_HEAD_DIM)
    q = partial_rotary(aq.reshape(shp), positions)
    k = partial_rotary(ak.reshape(shp), positions)
    v = av.reshape(shp)
    outs, lses = [], []
    for g, (window, dilation) in enumerate(ATTN_GROUPS):
        o, lse = dilated_window_attention(q[:, :, g], k[:, :, g], v[:, :, g], window, dilation)
        outs.append(o)
        lses.append(lse)
    w = jax.nn.softmax(jnp.stack(lses), axis=0)
    out = jnp.sum(w[..., None] * jnp.stack(outs), axis=0)
    return out.reshape(B_, S_, ATTN_OUT_WIDTH).astype(aq.dtype)

def causal_depthwise_conv(x, w):
    K, C = w.shape
    return lax.conv_general_dilated(x, w[:, None, :].astype(x.dtype), window_strides=(1,),
                                    padding=[(K - 1, 0)], dimension_numbers=('NWC', 'WIO', 'NWC'),
                                    feature_group_count=C)

def mlstm_chunkwise(q, k, v, i_raw, f_raw):
    B_, S_, H, Dk = q.shape
    Dv = v.shape[-1]
    LC = MLSTM_CHUNK
    nC = S_ // LC

    def chunks(t):
        t = t.astype(jnp.float32)
        if t.ndim == 4:
            return t.reshape(B_, nC, LC, H, t.shape[-1]).transpose(1, 0, 3, 2, 4)
        return t.reshape(B_, nC, LC, H).transpose(1, 0, 3, 2)

    logf = jax.nn.log_sigmoid(f_raw.astype(jnp.float32))
    xs = (chunks(q), chunks(k), chunks(v), chunks(i_raw), chunks(logf))
    causal = jnp.tril(jnp.ones((LC, LC), dtype=bool))

    def step(carry, inp):
        C, n, m = carry
        qc, kc, vc, ic, fc = inp
        b = jnp.cumsum(fc, axis=-1)
        Dm = jnp.where(causal, b[..., :, None] - b[..., None, :] + ic[..., None, :], -jnp.inf)
        inter = b + m[..., None]
        m_t = jnp.maximum(inter, jnp.max(Dm, axis=-1))
        w_intra = jnp.exp(Dm - m_t[..., None])
        w_inter = jnp.exp(inter - m_t)
        A = jnp.einsum('bhtd,bhsd->bhts', qc, kc) * w_intra
        num = jnp.einsum('bhts,bhsv->bhtv', A, vc) + w_inter[..., None] * jnp.einsum('bhtd,bhdv->bhtv', qc, C)
        den = jnp.sum(A, axis=-1) + w_inter * jnp.einsum('bhtd,bhd->bht', qc, n)
        h = num / jnp.maximum(jnp.abs(den), jnp.exp(-m_t))[..., None]
        bL = b[..., -1]
        g = bL[..., None] - b + ic
        m_new = jnp.maximum(bL + m, jnp.max(g, axis=-1))
        decay = jnp.exp(bL + m - m_new)
        wk = jnp.exp(g - m_new[..., None])
        kw = kc * wk[..., None]
        C_new = decay[..., None, None] * C + jnp.einsum('bhsd,bhsv->bhdv', kw, vc)
        n_new = decay[..., None] * n + jnp.sum(kw, axis=-2)
        return (C_new, n_new, m_new), h

    init = (jnp.zeros((B_, H, Dk, Dv), jnp.float32), jnp.zeros((B_, H, Dk), jnp.float32),
            jnp.zeros((B_, H), jnp.float32))
    _, hs = lax.scan(step, init, xs)
    return hs.transpose(1, 0, 3, 2, 4).reshape(B_, S_, H, Dv)

def mlstm_mixer(mq, mk, mv, mo, mi, mf, conv_w, b_if, g_norm):
    B_, S_, _ = mq.shape
    H, Dh = MLSTM_HEADS, MLSTM_HEAD_DIM
    qk = jax.nn.silu(causal_depthwise_conv(jnp.concatenate([mq, mk], axis=-1), conv_w))
    q = qk[..., :MLSTM_WIDTH].reshape(B_, S_, H, Dh)
    k = qk[..., MLSTM_WIDTH:].reshape(B_, S_, H, Dh) * (Dh ** -0.5)
    v = mv.reshape(B_, S_, H, Dh)
    i_raw = mi.astype(jnp.float32) + b_if[:H].astype(jnp.float32)
    f_raw = mf.astype(jnp.float32) + b_if[H:].astype(jnp.float32)
    h = mlstm_chunkwise(q, k, v, i_raw, f_raw)
    mu = jnp.mean(h, axis=-1, keepdims=True)
    var = jnp.mean(jnp.square(h - mu), axis=-1, keepdims=True)
    hn = (h - mu) * lax.rsqrt(var + LN_EPS) * g_norm.astype(jnp.float32).reshape(H, Dh)
    out = jax.nn.sigmoid(mo.astype(jnp.float32)) * hn.reshape(B_, S_, MLSTM_WIDTH)
    return out.astype(mq.dtype)

def moe_ffn(xn, w_router, b_router, w_gate_up, b_gate_up, w_down, b_down):
    B_, S_, D = xn.shape
    T = B_ * S_
    A = T * TOP_K
    xf = xn.reshape(T, D)
    logits = (xf @ w_router + b_router).astype(jnp.float32)
    top_logits, top_idx = lax.top_k(logits, TOP_K)
    gates = jax.nn.softmax(top_logits, axis=-1)
    flat_e = top_idx.reshape(A)
    flat_tok = jnp.repeat(jnp.arange(T, dtype=jnp.int32), TOP_K)
    flat_w = gates.reshape(A)
    order = jnp.argsort(flat_e)
    sorted_e = flat_e[order]
    counts = jnp.bincount(flat_e, length=N_EXPERTS)
    starts = jnp.cumsum(counts) - counts
    padded = (counts + MOE_BLOCK - 1) // MOE_BLOCK * MOE_BLOCK
    padded_ends = jnp.cumsum(padded)
    padded_starts = padded_ends - padded
    rank = jnp.arange(A, dtype=jnp.int32) - starts[sorted_e]
    dest = padded_starts[sorted_e] + rank
    n_blocks = -(-A // MOE_BLOCK) + N_EXPERTS
    n_rows = n_blocks * MOE_BLOCK
    row_tok = jnp.zeros((n_rows,), jnp.int32).at[dest].set(flat_tok[order])
    row_w = jnp.zeros((n_rows,), jnp.float32).at[dest].set(flat_w[order])
    block_e = jnp.minimum(jnp.searchsorted(padded_ends, jnp.arange(n_blocks, dtype=jnp.int32) * MOE_BLOCK,
                                           side='right'), N_EXPERTS - 1)
    xs = xf[row_tok].reshape(n_blocks, MOE_BLOCK, D)

    def expert_block(args):
        xb, e = args
        hg = xb @ w_gate_up[e] + b_gate_up[e]
        gate = jnp.minimum(hg[:, 0::2], SWIGLU_LIMIT)
        up = jnp.clip(hg[:, 1::2], -SWIGLU_LIMIT, SWIGLU_LIMIT)
        act = (up + 1.0) * (gate * jax.nn.sigmoid(SWIGLU_ALPHA * gate))
        return act @ w_down[e] + b_down[e]

    ys = lax.map(expert_block, (xs, block_e)).reshape(n_rows, D).astype(jnp.float32) * row_w[:, None]
    out = jnp.zeros((T, D), jnp.float32).at[row_tok].add(ys)
    return out.reshape(B_, S_, D).astype(xn.dtype)

def setup_inputs(seed: int = 0) -> dict:
    key = jax.random.key(seed)
    ks = jax.random.split(key, 20)
    f32 = jnp.float32
    nrm = lambda k, shp: jax.random.normal(k, shp, f32)
    H = MLSTM_HEADS
    b_i = 0.1 * nrm(ks[5], (DEPTH, H))
    b_f = jnp.linspace(3.0, 6.0, H, dtype=f32)[None, :] + 0.1 * nrm(ks[6], (DEPTH, H))
    return {
        'x': nrm(ks[0], (BATCH, SEQ, D_MODEL)),
        'positions': (jnp.arange(SEQ, dtype=jnp.int32)[None, :]
                      + jax.random.randint(ks[1], (BATCH, 1), 0, 4096, dtype=jnp.int32)),
        'g_mix': 1.0 + 0.05 * nrm(ks[2], (DEPTH, D_MODEL)),
        'w_in': nrm(ks[3], (DEPTH, D_MODEL, D_IN)) * D_MODEL ** -0.5,
        'conv_qk': nrm(ks[4], (DEPTH, CONV_WIDTH, 2 * MLSTM_WIDTH)) * CONV_WIDTH ** -0.5,
        'b_if': jnp.concatenate([b_i, b_f], axis=-1),
        'g_mlstm_norm': 1.0 + 0.05 * nrm(ks[7], (DEPTH, MLSTM_WIDTH)),
        'w_attn_out': nrm(ks[8], (DEPTH, ATTN_OUT_WIDTH, D_MODEL)) * ATTN_OUT_WIDTH ** -0.5,
        'w_mlstm_out': nrm(ks[9], (DEPTH, MLSTM_WIDTH, D_MODEL)) * MLSTM_WIDTH ** -0.5,
        'w_mix_out': nrm(ks[10], (DEPTH, D_MODEL, D_MODEL)) * D_MODEL ** -0.5,
        'g_ffn': 1.0 + 0.05 * nrm(ks[11], (DEPTH, D_MODEL)),
        'w_router': nrm(ks[12], (DEPTH, D_MODEL, N_EXPERTS)) * D_MODEL ** -0.5,
        'b_router': 0.01 * nrm(ks[13], (DEPTH, N_EXPERTS)),
        'w_gate_up': nrm(ks[14], (DEPTH, N_EXPERTS, D_MODEL, 2 * D_FF)) * D_MODEL ** -0.5,
        'b_gate_up': 0.02 * nrm(ks[15], (DEPTH, N_EXPERTS, 2 * D_FF)),
        'w_down': nrm(ks[16], (DEPTH, N_EXPERTS, D_FF, D_MODEL)) * D_FF ** -0.5,
        'b_down': 0.02 * nrm(ks[17], (DEPTH, N_EXPERTS, D_MODEL)),
        'g_final': 1.0 + 0.05 * nrm(ks[18], (D_MODEL,)),
    }

def reference(x, positions, g_mix, w_in, conv_qk, b_if, g_mlstm_norm, w_attn_out, w_mlstm_out,
              w_mix_out, g_ffn, w_router, b_router, w_gate_up, b_gate_up, w_down, b_down, g_final):
    offsets = [int(o) for o in np.cumsum(IN_SPLIT_SIZES)[:-1]]
    h = x
    for l in range(DEPTH):
        xn = rms_norm(h, g_mix[l])
        proj = xn @ w_in[l]
        aq, ak, av, mq, mk, mv, mo, mi, mf, ga, gm = jnp.split(proj, offsets, axis=-1)
        attn = dilated_attention_mixer(aq, ak, av, positions)
        mem = mlstm_mixer(mq, mk, mv, mo, mi, mf, conv_qk[l], b_if[l], g_mlstm_norm[l])
        merged = (jax.nn.sigmoid(ga) * (attn @ w_attn_out[l])
                  + jax.nn.sigmoid(gm) * (mem @ w_mlstm_out[l]))
        h = h + merged @ w_mix_out[l]
        h = h + moe_ffn(rms_norm(h, g_ffn[l]), w_router[l], b_router[l], w_gate_up[l],
                        b_gate_up[l], w_down[l], b_down[l])
    return rms_norm(h, g_final)


_drawn_inputs = setup_inputs


def setup_inputs(seed=0):
    import zlib

    import numpy as np

    out = dict(_drawn_inputs(seed))
    spreads = {}
    factors = {'b_gate_up': 5.289, 'b_down': 6.091}
    for name, (base, spread) in spreads.items():
        noise = np.random.default_rng([zlib.crc32(name.encode()), seed]).standard_normal(out[name].shape)
        drawn = base * np.exp(spread * noise) if base else spread * noise
        out[name] = __import__('jax').numpy.asarray(drawn.astype(out[name].dtype))
    for name, factor in factors.items():
        out[name] = (out[name] * factor).astype(out[name].dtype)
    return out
```

```python
from contextlib import ExitStack

import numpy as np

import concourse.bass as bass
from concourse import mybir

F32 = mybir.dt.float32
BF16 = mybir.dt.bfloat16
I32 = mybir.dt.int32
U32 = mybir.dt.uint32
ALU = mybir.AluOpType
ACT = mybir.ActivationFunctionType
AX = mybir.AxisListType

P = 128
BANK = 512
NEG = -1.0e30
RMS_EPS = 1e-5
LN_EPS = 1e-5
ROPE_THETA = 500000.0
WINDOW0 = 128
SWIGLU_LIMIT = 7.0
SWIGLU_ALPHA = 1.702
TOP_K = 4
ABSENT = 4096
DMA = 16


class Chain:

    def __init__(self, eng, sem):
        self.eng, self.sem, self.total, self.base, self.n = eng, sem, 0, 0, 0

    def begin(self, turn, per_turn):
        self.total += self.n
        self.per, self.base, self.n = per_turn, self.total + turn * per_turn, 0

    def end(self, turns):
        assert self.n == self.per, f"{self.n} steps in a turn, not {self.per}"
        self.total += turns * self.per
        self.base, self.n = self.total, 0

    def mark(self, ins):
        self.n += 1
        ins.then_inc(self.sem, 1)

    def settle(self):
        self.eng.wait_ge(self.sem, self.base + self.n)

    def step(self, ins):
        self.mark(ins)
        self.settle()


class Region:

    def __init__(self, nc, start, end):
        self.nc, self.at, self.end = nc, start, end

    def tensor(self, name, shape, dt=F32):
        size = 1
        for n in shape[1:]:
            size *= n
        size = -(-size * (2 if dt == BF16 else 4) // 32) * 32
        assert self.at + size <= self.end, f"{name}: {self.at + size} of {self.end}"
        t = self.nc.alloc_sbuf_tensor_at(name, shape, dt, offset=self.at)
        self.at += size
        return t


def hybrid_block(nc, x, positions, g_mix, w_in, conv_qk, b_if, g_mlstm_norm, w_attn_out, w_mlstm_out, w_mix_out,
                 g_ffn, w_router, b_router, w_gate_up, b_gate_up, w_down, b_down, g_final, out):
    _, T, D = x.shape
    NT = T // P
    KD = D // P
    E = w_router.shape[2]
    F = w_down.shape[2]
    F2 = 2 * F
    H = 4
    G = 3
    DH = 128
    MDH = D // H
    QK_SCALE = float(DH) ** -0.5
    MK_SCALE = float(MDH) ** -0.5
    TAPS = conv_qk.shape[1]
    CT = 2 * D // P
    ROT = DH // 4
    HALF = ROT // 2
    AW = G * H * DH
    AQ, AK, AV = 0, AW, 2 * AW
    MQ = 3 * AW
    MK, MV, MO, MI = MQ + D, MQ + 2 * D, MQ + 3 * D, MQ + 4 * D
    MF = MI + H
    GA = MF + H
    GM = GA + D
    assert T == BANK and DH == P and MDH == 2 * P and w_in.shape[2] == GM + D and F == D and E == 32

    def chunked(w):
        return w.rearrange("(k p) n -> p k n", p=P)

    w_in_v, wa_v, wm_v, wmix_v = chunked(w_in[0]), chunked(w_attn_out[0]), chunked(w_mlstm_out[0]), chunked(w_mix_out[0])
    gu_v = w_gate_up[0].rearrange("e (k p) n -> p e k n", p=P)
    dn_v = w_down[0].rearrange("e (k p) n -> p e k n", p=P)
    x_v = x[0].rearrange("(i p) d -> p i d", p=P)
    out_v = out[0].rearrange("(i p) d -> p i d", p=P)

    xn_rows = nc.dram_tensor("xn_rows", (T, D), F32).ap()
    y_rows = nc.dram_tensor("y_rows", (T * TOP_K, D), F32).ap()
    xn_v = xn_rows.rearrange("(i p) d -> p i d", p=P)
    y_v = y_rows.rearrange("(i p k) d -> p i (k d)", p=P, k=TOP_K)

    keep = Region(nc, -(-nc.sbuf_base // 64) * 64, nc.sbuf_usable_end)
    hres = keep.tensor("hres", [P, NT, D])
    xnT = keep.tensor("xnT", [P, KD, T])
    xw = keep.tensor("xw", [P, 2, D])
    sel = keep.tensor("sel", [P, E, P], BF16)
    bsp = keep.tensor("bsp", [P, F2 + D], BF16)
    ident = keep.tensor("ident", [P, P])
    vecT = keep.tensor("vecT", [P, 88])
    lg = keep.tensor("lg", [P, NT, E])
    brt = keep.tensor("brt", [P, E])
    wr = keep.tensor("wr", [P, KD, E])
    iota_slot = keep.tensor("iota_slot", [P, P])
    ssq = keep.tensor("ssq", [P, 3, NT])
    rstd = keep.tensor("rstd", [P, 3, NT])
    flag = keep.tensor("flag", [P, 1], I32)
    tick = keep.tensor("tick", [P, 1])
    GMIX, GFFN, GMEM = TAPS * CT, TAPS * CT + KD, TAPS * CT + 2 * KD

    RING = 12 * F2 * 4
    mixed = Region(nc, keep.at, keep.at + RING)
    attT = mixed.tensor("attT", [P, H, T])
    memT = mixed.tensor("memT", [P, KD, T])
    mem = Region(nc, mixed.at, mixed.end)
    raw = mem.tensor("raw", [P, 4, T + TAPS - 1])
    cv = mem.tensor("cv", [P, 4, T])
    qkf = mem.tensor("qkf", [P, 4, T])
    mvraw = mem.tensor("mvraw", [P, 2, T])
    VN = MDH + 2
    vN = mem.tensor("vN", [P, NT, VN])
    wexp = mem.tensor("wexp", [P, NT, T])
    AT = mem.tensor("AT", [P, NT, T])
    hh = mem.tensor("hh", [P, NT, MDH])
    sgo = mem.tensor("sgo", [P, 2, T])
    nmb = mem.tensor("nmb", [P, H, T])
    nmd = mem.tensor("nmd", [P, T])
    cmask = mem.tensor("cmask", [P, P])
    ceT = mem.tensor("ceT", [P, NT, 64])
    expE = mem.tensor("expE", [P, NT, H])
    cwh = mem.tensor("cwh", [P, TAPS, 4])
    gmh = mem.tensor("gmh", [P, 2])
    ch = mem.tensor("ch", [P, NT])
    eh = mem.tensor("eh", [P, NT])
    den = mem.tensor("den", [P, 2, NT])
    bst = mem.tensor("bst", [P, NT, 6])
    mv = mem.tensor("mv", [P, NT, 2])
    mrs = mem.tensor("mrs", [P, 2, NT])
    pre = Region(nc, mixed.at, mixed.end)
    pre.tensor("skip_to_wexp", [P, 4 * (T + TAPS - 1) + 8 * T + 2 * T + NT * VN])
    wif = pre.tensor("wif", [P, KD, 64])
    gat = pre.tensor("gat", [64, 3, T])
    ce = pre.tensor("ce", [64, T])
    ones_row = pre.tensor("ones_row", [H, T])
    head_sel = pre.tensor("head_sel", [H, H, P])
    bcol = pre.tensor("bcol", [64, 1])
    brow_at = Region(nc, mixed.at, mixed.end)
    brow_at.tensor("skip_to_qkf", [P, 4 * (T + TAPS - 1) + 4 * T])
    brow = brow_at.tensor("brow", [P, F2 + D])
    att = Region(nc, mixed.at, mixed.end)
    qk = att.tensor("qk", [P, 2 * G, T])
    avraw = att.tensor("avraw", [P, G, T])
    vh = att.tensor("vh", [P, G, NT, P])
    SC = T + 2 * P
    sm = att.tensor("sm", [P, 2, SC])
    pr = att.tensor("pr", [P, 2, SC])
    pT = att.tensor("pT", [P, 6, P])
    rs = att.tensor("rs", [ROT, 2 * G, T])
    smax = att.tensor("smax", [P, 2, 4])
    mrg = Region(nc, mixed.at, mixed.end)
    sgm = mrg.tensor("sgm", [P, 2, 2, T])
    mgt = mrg.tensor("mgt", [P, 2, 2, T])
    tail = Region(nc, keep.at + RING, nc.sbuf_usable_end)
    mergedT = tail.tensor("mergedT", [P, KD, T])
    wring = tail.tensor("wring", [P, 9, D])
    fcol = tail.tensor("fcol", [P, 2])
    masks = Region(nc, keep.at + RING, tail.end)
    amask = masks.tensor("amask", [P, NT, SC])
    rcos = masks.tensor("rcos", [ROT, T])
    rsin = masks.tensor("rsin", [ROT, T])
    start = Region(nc, pre.at, mixed.end)
    vrow = start.tensor("vrow", [88, P])
    frow = start.tensor("frow", [1, 2, P])
    post = start.tensor("post", [ROT, T], I32)
    ang = start.tensor("ang", [ROT, 3, T])
    m4 = start.tensor("m4", [P, P], I32)
    exp_ring = Region(nc, keep.at, keep.at + RING)
    guw = exp_ring.tensor("guw", [P, KD, F2])
    dnw = exp_ring.tensor("dnw", [P, KD, D])
    ex = Region(nc, keep.at + RING, nc.sbuf_usable_end)
    xg = ex.tensor("xg", [P, D])
    xT = ex.tensor("xT", [P, KD, P])
    gt = ex.tensor("gt", [P, F])
    sg = ex.tensor("sg", [P, F])
    up = ex.tensor("up", [P, F])
    act = ex.tensor("act", [P, F])
    actT = ex.tensor("actT", [P, KD, P])
    yw = ex.tensor("yw", [P, D])
    tbl = ex.tensor("tbl", [P, E + 2, NT, 4])
    te = ex.tensor("te", [P, NT, 4])
    sels = ex.tensor("sels", [P, NT, P])
    gate_of = ex.tensor("gate_of", [P, E + 2])
    idx_of = ex.tensor("idx_of", [P, E + 2, 2], I32)
    gcur = ex.tensor("gcur", [P, 1])
    gidx = ex.tensor("gidx", [P, 1], I32)
    sidx = ex.tensor("sidx", [P, 1], I32)
    pool_tick = ex.tensor("pool_tick", [P, 1])
    slot_b = ex.tensor("slot_b", [P, P])
    v8 = ex.tensor("v8", [P, NT, 8])
    i8 = ex.tensor("i8", [P, NT, 8], U32)
    i8f = ex.tensor("i8f", [P, NT, 8])
    gk = ex.tensor("gk", [P, NT, TOP_K])
    gs = ex.tensor("gs", [P, 2, NT])
    iota_e = ex.tensor("iota_e", [P, E])
    iota_k = ex.tensor("iota_k", [P, TOP_K])
    tokf = ex.tensor("tokf", [P, 2, NT])
    i_tmp = ex.tensor("i_tmp", [P, E], I32)
    oh = gt[:, 0:NT * TOP_K * E].rearrange("p (i k e) -> p i k e", i=NT, k=TOP_K)
    oht = sg[:, 0:NT * TOP_K * E].rearrange("p (i k e) -> p i k e", i=NT, k=TOP_K)
    member = up[:, 0:NT * E].rearrange("p (i e) -> p i e", i=NT)
    pos1 = up[:, NT * E:2 * NT * E].rearrange("p (i e) -> p i e", i=NT)
    kth = up[:, 2 * NT * E:3 * NT * E].rearrange("p (i e) -> p i e", i=NT)
    gte = up[:, 3 * NT * E:4 * NT * E].rearrange("p (i e) -> p i e", i=NT)
    memb = ex.tensor("memb", [P, NT, E], BF16)
    tri = ex.tensor("tri", [P, P], BF16)
    onesb = ex.tensor("onesb", [P, P], BF16)
    ovf = ex.tensor("ovf", [P, 1])

    ctx = ExitStack()
    with ctx:
        ps = ctx.enter_context(nc.psum_tensor("ps", [P, 8, BANK], F32))

        def sem(name):
            return ctx.enter_context(nc.semaphore(name))

        x_in = [sem(f"x_in{i}") for i in range(NT)]
        vec_in, pos_in, bif_in, wif_in, brow_in, router_in = (
            sem(n) for n in ("vec_in", "pos_in", "bif_in", "wif_in", "brow_in", "router_in"))
        w_in_slot = [sem(f"w_in_slot{s}") for s in range(9)]
        pool_step, dve_step, act_step = sem("pool_step"), sem("dve_step"), sem("act_step")
        tables = sem("tables")
        x_square, x_var, x_std, xw_ready, xw_used, xnT_ready = (
            sem(n) for n in ("x_square", "x_var", "x_std", "xw_ready", "xw_used", "xnT_ready"))
        vecT_done, angle_ready, sines_ready, m4_ready = (
            sem(n) for n in ("vecT_done", "angle_ready", "sines_ready", "m4_ready"))
        m4_made, sines_done, num_out = sem("m4_made"), sem("sines_done"), sem("num_out")
        gate_mm, gate_abs, gate_ln, gate_rows, gate_T, gate_cols, nmb_mm, nmb_ready = (
            sem(n) for n in ("gate_mm", "gate_abs", "gate_ln", "gate_rows", "gate_T", "gate_cols", "nmb_mm", "nmb_ready"))
        w_used, proj_out = sem("w_used"), sem("proj_out")
        conv_ready, qk_ready, cols_ready, wexp_ready, mv_T, vN_ready, at_mm, at_ready, num_mm, hvar_ready, hstd_ready, hn_ready, hn_T, mem_ready = (
            sem(n) for n in ("conv_ready", "qk_ready", "cols_ready", "wexp_ready", "mv_T", "vN_ready", "at_mm", "at_ready",
                             "num_mm", "hvar_ready", "hstd_ready", "hn_ready", "hn_T", "mem_ready"))
        rot_ready, av_T, vh_ready, s_mm, smax_ready, exp_ready, pr_ready, pr_T, pT_act, pT_dve, pv_mm, att_ready = (
            sem(n) for n in ("rot_ready", "av_T", "vh_ready", "s_mm", "smax_ready", "exp_ready", "pr_ready", "pr_T", "pT_act",
                             "pT_dve", "pv_mm", "att_ready"))
        sg_ready, merged, mix_mm, h_ready = (sem(n) for n in ("sg_ready", "merged", "mix_mm", "h_ready"))
        h_square, h_var, h_std, hw_ready, hw_used, xn2T_ready, lg_mm, top_ready, gk_ready, memb_ready, pos_mm, tbl_ready = (
            sem(n) for n in ("h_square", "h_var", "h_std", "hw_ready", "hw_used", "xn2T_ready", "lg_mm",
                             "top_ready", "gk_ready", "memb_ready", "pos_mm", "tbl_ready"))
        late_tables, bias_ready, flag_ready, slot_ready = (sem(n) for n in ("late_tables", "bias_ready", "flag_ready", "slot_ready"))
        gu_in = [sem(f"gu_in{s}") for s in range(KD)]
        dn_in = [sem(f"dn_in{s}") for s in range(KD // 2)]
        gu_used, dn_used, te_ready, sel_ready, meta_mm, meta_ready, gathered, xg_T, xT_ready, up_read, gt_ready, sg_ready2, act_ready, act_T, actT_ready, gcur_ready, y_ready, y_stored = (
            sem(n) for n in ("gu_used", "dn_used", "te_ready", "sel_ready", "meta_mm", "meta_ready", "gathered", "xg_T", "xT_ready",
                             "up_read", "gt_ready", "sg_ready2", "act_ready", "act_T", "actT_ready", "gcur_ready", "y_ready", "y_stored"))
        all_stored, gfin_in, f_sum, f_square, f_var, f_std, o_ready, o_stored = (
            sem(n) for n in ("all_stored", "gfin_in", "f_sum", "f_square", "f_var", "f_std", "o_ready", "o_stored"))
        pool_over, dve_over, act_over = sem("pool_over"), sem("dve_over"), sem("act_over")
        y_in = [sem(f"y_in{i}") for i in range(NT)]
        xn_stored = [sem(f"xn_stored{i}") for i in range(NT)]

        TABLES = ("ident", "wif", "ce", "rows", "raw", "vN", "amask", "cmask", "slots", "sel")
        made = {name: n + 1 for n, name in enumerate(TABLES)}

        N_MEM, N_ATT, N_MRG = 8, 3 * G, 8
        ATT0 = N_MEM * H
        MRG0 = ATT0 + N_ATT * H
        MIX0 = MRG0 + N_MRG * (KD // 2)

        def mem_cols(h):
            return [c + MDH * h + P * u for c in (MQ, MK, MV, MO) for u in range(2)]

        def att_cols(h):
            return [c + H * DH * g + DH * h for c in (AQ, AK, AV) for g in range(G)]

        def col(expr):
            return bass.ds(expr, P)

        yfin = guw[:].rearrange("p (i a) n -> p i (a n)", i=NT)
        gfin = dnw[:, 0, :]

        def many(eng):
            eng.wait_ge(flag_ready, 1)
            return eng.value_load(flag[0:1, 0:1], min_val=0, max_val=1)

        def extra(b, e):
            return (b - 1) * E + e

        block = ctx.enter_context(nc.Block())

        @block.sync
        def _(sp):
            nc.sync.dma_start(vrow[0:GMIX, :], conv_qk[0].rearrange("j (c p) -> (j c) p", p=P)).then_inc(vec_in, DMA)
            nc.sync.dma_start(vrow[GMIX:GFFN, :], g_mix.rearrange("a (c p) -> (a c) p", p=P)).then_inc(vec_in, DMA)
            nc.sync.dma_start(vrow[GFFN:GMEM, :], g_ffn.rearrange("a (c p) -> (a c) p", p=P)).then_inc(vec_in, DMA)
            nc.sync.dma_start(vrow[GMEM:GMEM + KD, :], g_mlstm_norm.rearrange("a (c p) -> (a c) p", p=P)).then_inc(vec_in, DMA)
            for i in range(NT):
                nc.sync.dma_start(hres[:, i, :], x_v[:, i, :]).then_inc(x_in[i], DMA)
            nc.sync.dma_start(bcol[0:H, :], b_if[:, 0:H].rearrange("a h -> h a")).then_inc(bif_in, DMA)
            nc.sync.dma_start(bcol[32:32 + H, :], b_if[:, H:2 * H].rearrange("a h -> h a")).then_inc(bif_in, DMA)
            sp.wait_ge(tables, made["wif"])
            nc.sync.dma_start(wif[:, :, 0:H], w_in_v[:, :, MI:MI + H]).then_inc(wif_in, DMA)
            nc.sync.dma_start(wif[:, :, 32:32 + H], w_in_v[:, :, MF:MF + H]).then_inc(wif_in, DMA)
            for j, c in enumerate(mem_cols(0)):
                nc.sync.dma_start(wring[:, j, :].rearrange("p (k n) -> p k n", n=P), w_in_v[:, :, c:c + P]).then_inc(w_in_slot[j], DMA)
                if j == 0:
                    nc.sync.dma_start(post[:], positions[0:1, :].to_broadcast([ROT, T])).then_inc(pos_in, DMA)
                    for g in (0, 64, 96):
                        nc.sync.dma_start(brow[g:g + E, 0:F2], b_gate_up[0]).then_inc(brow_in, DMA)
                        nc.sync.dma_start(brow[g:g + E, F2:F2 + D], b_down[0]).then_inc(brow_in, DMA)
            with sp.Fori(1, H) as h:
                for j, c in enumerate([sp.snap(c) for c in mem_cols(h)]):
                    sp.wait_ge(w_used, N_MEM * (h - 1) + j + 1)
                    nc.sync.dma_start(wring[:, j, :].rearrange("p (k n) -> p k n", n=P), w_in_v[:, :, col(c)]).then_inc(w_in_slot[j], DMA)
            nc.sync.dma_start(brt[:], b_router[0:1, :].to_broadcast([P, E])).then_inc(router_in, DMA)
            nc.sync.dma_start(wr[:], chunked(w_router[0])).then_inc(router_in, DMA)
            for j, c in enumerate(att_cols(0)):
                if j < N_MEM:
                    sp.wait_ge(w_used, N_MEM * (H - 1) + j + 1)
                nc.sync.dma_start(wring[:, j, :].rearrange("p (k n) -> p k n", n=P), w_in_v[:, :, c:c + P]).then_inc(w_in_slot[j], DMA)
            with sp.Fori(1, H) as h:
                for j, c in enumerate([sp.snap(c) for c in att_cols(h)]):
                    sp.wait_ge(w_used, ATT0 + N_ATT * (h - 1) + j + 1)
                    nc.sync.dma_start(wring[:, j, :].rearrange("p (k n) -> p k n", n=P), w_in_v[:, :, col(c)]).then_inc(w_in_slot[j], DMA)

            def merge_tiles(b, before):
                at = [P * (2 * b + u) + k0 for u in range(2) for k0 in (GA, GM, 0, 0)]
                if not isinstance(b, int):
                    at = [sp.snap(a) for a in at]
                for u in range(2):
                    for j, w in enumerate((w_in_v, w_in_v, wa_v, wm_v)):
                        s = 4 * u + j
                        if j != 2:
                            sp.wait_ge(w_used, before + s + 1 + (j == 1))
                        nk = w.shape[1]
                        nc.sync.dma_start(wring[:, s, 0:nk * P].rearrange("p (k n) -> p k n", n=P),
                                          w[:, :, col(at[s])]).then_inc(w_in_slot[s], DMA)

            merge_tiles(0, ATT0 + N_ATT * (H - 1))
            with sp.Fori(1, KD // 2) as b:
                merge_tiles(b, MRG0 + N_MRG * (b - 1))
            for k in range(KD):
                sp.wait_ge(w_used, MRG0 + N_MRG * (KD // 2 - 1) + k + 1)
                nc.sync.dma_start(wring[:, k, :], wmix_v[:, k, :]).then_inc(w_in_slot[k], DMA)
            sp.wait_ge(merged, KD)

            def load_gu(e, s):
                nc.sync.dma_start(guw[:, s, :], gu_v[:, bass.ds(e, 1), s, :].rearrange("p a n -> p (a n)")).then_inc(gu_in[s], DMA)

            def load_dn(e, s):
                nc.sync.dma_start(dnw[:, 2 * s:2 * s + 2, :],
                                  dn_v[:, bass.ds(e, 1), 2 * s:2 * s + 2, :].rearrange("p a k n -> p (a k) n")).then_inc(dn_in[s], DMA)

            def store_normed():
                for i in range(NT):
                    sp.wait_ge(hw_ready, i + 1)
                    nc.sync.dma_start(xn_v[:, i, :], xw[:, i % 2, :]).then_inc(xn_stored[i], DMA)

            for s in range(KD):
                load_gu(0, s)
            for s in range(KD // 2):
                load_dn(0, s)
            store_normed()
            for s in range(KD):
                sp.wait_ge(gu_used, s + 1)
                load_gu(1, s)
            with sp.Fori(2, E) as e:
                before = sp.snap(e - 1)
                for s in range(KD):
                    sp.wait_ge(gu_used, KD * (e - 1) + s + 1)
                    load_gu(e, s)
                for s in range(KD // 2):
                    sp.wait_ge(dn_used, (KD // 2) * (e - 2) + s + 1)
                    load_dn(before, s)
            for s in range(KD // 2):
                sp.wait_ge(dn_used, (KD // 2) * (E - 2) + s + 1)
                load_dn(E - 1, s)
            with sp.If(many(sp) > 0):
                with sp.Fori(1, NT) as b:
                    with sp.Fori(0, E) as e:
                        g_idx = extra(b, e) + E
                        for s in range(KD):
                            sp.wait_ge(gu_used, KD * (g_idx - 1) + s + 1)
                            load_gu(e, s)
                        for s in range(KD // 2):
                            sp.wait_ge(dn_used, (KD // 2) * (g_idx - 1) + s + 1)
                            load_dn(e, s)
            sp.wait_ge(all_stored, 1)
            sp.wait_ge(dn_used, KD // 2 * E)
            nc.sync.dma_start(gfin[:], g_final.rearrange("(a d) -> a d", a=1).to_broadcast([P, D])).then_inc(gfin_in, DMA)
            for i in range(NT):
                nc.sync.dma_start(yfin[:, i, :], y_v[:, i, :]).then_inc(y_in[i], DMA)
            for i in range(NT):
                sp.wait_ge(o_ready, i + 1)
                nc.sync.dma_start(out_v[:, i, :], hres[:, i, :]).then_inc(o_stored, DMA)
            sp.wait_ge(o_stored, DMA * NT)

        @block.gpsimd
        def _(pool):
            own = Chain(pool, pool_step)
            g = nc.gpsimd

            def table(name, ins):
                ins.then_inc(tables, 1)
                pool.wait_ge(tables, made[name])

            own.step(g.memset(ident[:], 0.0))
            table("ident", g.affine_select(out=ident[:], in_=ident[:], compare_op=ALU.not_equal, fill=1.0, base=0,
                                  pattern=[[-1, P]], channel_multiplier=1))
            table("wif", g.memset(wif[:], 0.0))
            table("ce", g.memset(ce[:], 0.0))
            own.step(g.memset(ones_row[:], 1.0))
            own.step(g.memset(frow[:], -1.0))
            for j in range(HALF):
                freq = float(np.float32(ROPE_THETA) ** np.float32(-j / HALF))
                own.step(g.memset(frow[0:1, 0, j:j + HALF + 1:HALF], freq))
            own.step(g.memset(frow[0:1, 1, HALF:ROT], 1.0))
            own.step(g.memset(head_sel[:], 0.0))
            table("rows", g.affine_select(out=head_sel[:], in_=head_sel[:], compare_op=ALU.not_equal, fill=1.0, base=0,
                                  pattern=[[-1, H], [0, P]], channel_multiplier=1))
            table("raw", g.memset(raw[:, :, 0:TAPS - 1], 0.0))
            table("vN", g.memset(vN[:, :, MDH:VN], 1.0))
            g.iota(m4[:], pattern=[[-1, P]], base=P, channel_multiplier=1).then_inc(m4_made, 1)
            pool.wait_ge(m4_made, 1)
            own.step(g.memset(bsp[32:64], 0.0))
            pool.wait_ge(brow_in, 6 * DMA)
            hi, lo = slice(64, P), slice(96, P)
            own.step(g.tensor_copy(bsp[0:E], brow[0:E]))
            own.step(g.tensor_copy(bsp[hi], brow[hi]))
            own.step(g.tensor_tensor(brow[hi], brow[hi], bsp[hi], ALU.subtract))
            own.step(g.tensor_copy(bsp[hi], brow[hi]))
            own.step(g.tensor_tensor(brow[lo], brow[lo], bsp[lo], ALU.subtract))
            g.tensor_copy(bsp[lo], brow[lo]).then_inc(bias_ready, 1)
            pool.wait_ge(bias_ready, 1)
            own.step(g.memset(amask[:, :, 0:T + P], 0.0))
            m0, m1, m2 = amask[:, :, 0:T], amask[:, :, T:T + P], amask[:, :, T + P:SC]
            own.step(g.affine_select(out=m0, in_=m0, compare_op=ALU.is_ge, fill=NEG, base=0,
                                     pattern=[[1, NT], [-1, T]], channel_multiplier=NT))
            own.step(g.affine_select(out=m0, in_=m0, compare_op=ALU.is_ge, fill=NEG, base=WINDOW0,
                                     pattern=[[-1, NT], [1, T]], channel_multiplier=-NT))
            own.step(g.affine_select(out=m1, in_=m1, compare_op=ALU.is_ge, fill=NEG, base=0,
                                     pattern=[[0, NT], [-1, P]], channel_multiplier=1))
            pool.wait_ge(m4_ready, 1)
            table("amask", g.affine_select(out=m2, in_=m2, compare_op=ALU.is_ge, fill=NEG, base=0,
                                  pattern=[[0, NT], [-1, P]], channel_multiplier=1))
            own.step(g.memset(cmask[:], 0.0))
            table("cmask", g.affine_select(out=cmask[:], in_=cmask[:], compare_op=ALU.is_ge, fill=NEG, base=0,
                                  pattern=[[1, P]], channel_multiplier=-1))
            table("slots", g.iota(iota_slot[:], pattern=[[1, P]], base=0, channel_multiplier=0, allow_small_or_imprecise_dtypes=True))
            own.step(g.memset(sel[:], 0.0))
            for q in (0, 64):
                own.step(g.affine_select(out=sel[q:q + E], in_=sel[q:q + E], compare_op=ALU.not_equal, fill=1.0, base=0,
                                         pattern=[[-1, E], [0, P]], channel_multiplier=1))
            table("sel", g.affine_select(out=sel[96:P], in_=sel[96:P], compare_op=ALU.not_equal, fill=1.0, base=0,
                                  pattern=[[-1, E], [0, P]], channel_multiplier=1))
            own.settle()
            pool.wait_ge(mix_mm, 2 * NT)
            own.step(g.memset(xg[:], 0.0))
            own.step(g.iota(iota_e[:], pattern=[[1, E]], base=0, channel_multiplier=0, allow_small_or_imprecise_dtypes=True))
            own.step(g.iota(iota_k[:], pattern=[[1, TOP_K]], base=0, channel_multiplier=0, allow_small_or_imprecise_dtypes=True))
            own.step(g.iota(tokf[:, 0, :], pattern=[[P, NT]], base=-ABSENT, channel_multiplier=1,
                            allow_small_or_imprecise_dtypes=True))
            own.step(g.iota(tokf[:, 1, :], pattern=[[TOP_K * P, NT]], base=-ABSENT, channel_multiplier=TOP_K,
                            allow_small_or_imprecise_dtypes=True))
            own.step(g.memset(tbl[:, E:E + 2, :, 0], -1.0))
            own.step(g.memset(pool_tick[:], 0.0))
            own.step(g.memset(tbl[:, E:E + 2, :, 1:4], 0.0))
            own.step(g.memset(onesb[:], 1.0))
            g.affine_select(out=tri[:], in_=onesb[:], compare_op=ALU.is_gt, fill=0.0, base=0,
                            pattern=[[1, P]], channel_multiplier=-1).then_inc(late_tables, 1)
            pool.wait_ge(tbl_ready, 4)
            for i in range(NT):
                pool.wait_ge(xn_stored[i], DMA)

            def table_of(e, m):
                pool.wait_ge(meta_mm, m)
                g.tensor_copy(te[:], tbl[:, bass.ds(e, 1), :, :].rearrange("p a i v -> p (a i) v")).then_inc(te_ready, 1)

            def gather(e, m, xi):
                pool.wait_ge(meta_ready, 2 * (m + 1))
                pool.wait_ge(gathered, DMA * xi)
                pool.wait_ge(xg_T, 2 * xi)
                own.step(g.tensor_copy(gidx[:], idx_of[:, bass.ds(e, 1), 0]))
                g.tensor_tensor(pool_tick[:], pool_tick[:], pool_tick[:], ALU.mult)
                g.indirect_dma_start(out=xg[:], out_offset=None, in_=xn_rows,
                                     in_offset=bass.IndirectOffsetOnAxis(ap=gidx[:, 0:1], axis=0),
                                     bounds_check=T - 1, oob_is_err=False).then_inc(gathered, DMA)

            def scatter(e, gi):
                pool.wait_ge(y_ready, 2 * (gi + 1))
                pool.wait_ge(y_stored, DMA * gi)
                own.step(g.tensor_copy(sidx[:], idx_of[:, bass.ds(e, 1), 1]))
                g.tensor_tensor(pool_tick[:], pool_tick[:], pool_tick[:], ALU.mult)
                g.indirect_dma_start(out=y_rows, out_offset=bass.IndirectOffsetOnAxis(ap=sidx[:, 0:1], axis=0),
                                     in_=yw[:], in_offset=None,
                                     bounds_check=T * TOP_K - 1, oob_is_err=False).then_inc(y_stored, DMA)

            table_of(0, 0)
            gather(0, 0, 0)
            table_of(1, 1)
            gather(1, 1, 1)
            table_of(2, 2)

            def expert_turn(e):
                gather(e + 1, e + 1, e + 1)
                table_of(e + 2, e + 2)
                scatter(e - 1, e - 1)

            expert_turn(1)
            with pool.Fori(2, E) as e:
                own.begin(e - 2, 2)
                expert_turn(e)
                own.end(E - 2)
            scatter(E - 1, E - 1)
            pool.wait_ge(y_stored, DMA * E)
            with pool.If(many(pool) > 0):
                common, own = own, Chain(pool, pool_over)
                with pool.Fori(1, NT) as b:
                    with pool.Fori(0, E) as e:
                        n = extra(b, e)
                        own.begin(n, 2)
                        table_of(e, E + 2 + n)
                        gather(e, E + 2 + n, E + 1 + n)
                        scatter(e, E + n)
                        pool.wait_ge(y_stored, DMA * (E + 1 + n))
                        own.end((NT - 1) * E)
                own = common
            g.engine_nop().then_inc(all_stored, 1)

        @block.tensor
        def _(pe):
            mm, tr = nc.tensor.matmul, nc.tensor.transpose

            pe.wait_ge(tables, made["ident"])
            pe.wait_ge(vec_in, 4 * DMA)
            tr(ps[:, 7, 0:88], vrow[:, :], ident[0:88, 0:88]).then_inc(vecT_done, 1)
            pe.wait_ge(tables, made["rows"])
            tr(ps[:, 6, 0:1], frow[0:1, 0, :], ident[0:1, 0:1])
            tr(ps[:, 6, 1:2], frow[0:1, 1, :], ident[0:1, 0:1]).then_inc(vecT_done, 1)

            def transpose_rows(ready, used, done, i):
                pe.wait_ge(ready, i + 1)
                for b in range(2):
                    if i >= 2:
                        pe.wait_ge(done, 2 * (i - 2) + b + 1)
                    for k in range(4):
                        last = tr(ps[:, 2 * (i % 2) + b, k * P:(k + 1) * P], xw[:, i % 2, (4 * b + k) * P:(4 * b + k + 1) * P], ident[:])
                    last.then_inc(used, 1)

            for i in range(NT):
                transpose_rows(xw_ready, xw_used, xnT_ready, i)
            pe.wait_ge(wif_in, 2 * DMA)
            pe.wait_ge(xnT_ready, 2 * NT)
            for k in range(KD):
                last = mm(ps[0:64, 4, :], wif[:, k, :], xnT[:, k, :], start=(k == 0), stop=(k == KD - 1))
            last.then_inc(gate_mm, 1)

            def project(slot, uses, bank, rhs=xnT, nk=KD):
                pe.wait_ge(w_in_slot[slot], DMA * uses)
                for k in range(nk):
                    last = mm(ps[:, bank, :], wring[:, slot, k * P:(k + 1) * P], rhs[:, k, :], start=(k == 0), stop=(k == nk - 1))
                last.then_inc(w_used, 1)

            def mem_tile(h, j):
                n = N_MEM * h + j
                if not isinstance(h, int) or n >= 2:
                    pe.wait_ge(proj_out, n - 1)
                project(j, h + 1, j % 2)

            def mem_gates():
                pe.wait_ge(tables, made["ce"])
                pe.wait_ge(gate_rows, 2)
                for i in range(NT):
                    last = tr(ps[:, 5, i * 64:(i + 1) * 64], ce[:, i * P:(i + 1) * P], ident[0:64, 0:64])
                last.then_inc(gate_T, 1)
                for h in range(H):
                    if h >= 2:
                        pe.wait_ge(nmb_ready, h - 1)
                    mm(ps[:, 6 + h % 2, :], head_sel[:, h, :], gat[0:H, 1, :], start=True, stop=True).then_inc(nmb_mm, 1)

            def mem_core(h):
                pe.wait_ge(proj_out, N_MEM * h + 6)
                pe.wait_ge(mem_ready, 2 * h)
                for i in range(NT):
                    for u in range(2):
                        last = tr(ps[:, 2 + i // 2, (i % 2) * MDH + u * P:(i % 2) * MDH + (u + 1) * P],
                                  mvraw[:, u, i * P:(i + 1) * P], ident[:])
                    if i % 2:
                        last.then_inc(mv_T, 1)
                pe.wait_ge(qk_ready, h + 1)
                for j in range(NT):
                    pe.wait_ge(at_ready, NT * h + j - 1 if j > 0 else NT * h)
                    for c in range(2):
                        last = mm(ps[:, 4 + j % 2, j * P:T], qkf[:, 2 + c, j * P:(j + 1) * P], qkf[:, c, j * P:T],
                                  start=(c == 0), stop=(c == 1))
                    last.then_inc(at_mm, 1)
                pe.wait_ge(vN_ready, 2 * (h + 1))
                for i in range(NT):
                    pe.wait_ge(at_ready, NT * h + i + 1)
                    if i >= 2:
                        pe.wait_ge(num_out, NT * h + i - 1)
                    for j in range(i + 1):
                        last = mm(ps[:, 6 + i % 2, 0:VN], AT[:, j, i * P:(i + 1) * P], vN[:, j, :], start=(j == 0), stop=(j == i))
                    last.then_inc(num_mm, 1)
                for i in range(NT):
                    pe.wait_ge(hn_ready, NT * h + i + 1)
                    for c in range(2):
                        last = tr(ps[:, 2 + c, i * P:(i + 1) * P], hh[:, i, c * P:(c + 1) * P], ident[:])
                last.then_inc(hn_T, 1)

            for j in range(4):
                mem_tile(0, j)
            mem_gates()
            for j in range(4, N_MEM):
                mem_tile(0, j)
            pe.wait_ge(nmb_ready, H)
            pe.wait_ge(gate_cols, 2)
            mem_core(0)
            with pe.Fori(1, H) as h:
                for j in range(N_MEM):
                    mem_tile(h, j)
                mem_core(h)

            def att_head(h):
                for j in range(N_ATT):
                    pe.wait_ge(proj_out, ATT0 + N_ATT * h + j - (1 if j else 0))
                    if j < 2:
                        pe.wait_ge(att_ready, NT * h)
                    project(j, h + 1 + (H if j < N_MEM else 0), j % 2)
                for g in range(G):
                    pe.wait_ge(proj_out, ATT0 + N_ATT * h + 2 * G + g + 1)
                    for i in range(NT):
                        src = avraw[:, g, i * P:(i + 1) * P] if g == 0 else avraw[:, g, i:T:NT]
                        last = tr(ps[:, (6, 7, 5)[g], i * P:(i + 1) * P], src, ident[:])
                    last.then_inc(av_T, 1)

                def scores(r):
                    b = 2 + 2 * (r % 2)
                    if r >= 2:
                        pe.wait_ge(smax_ready, NT * h + r - 1)
                    q = lambda g: qk[:, g, r:T:NT]
                    mm(ps[:, b, :], q(0), qk[:, G, :], start=True, stop=True)
                    mm(ps[:, b + 1, 0:P], q(1), qk[:, G + 1, r:T:NT], start=True, stop=True)
                    mm(ps[:, b + 1, P:2 * P], q(2), qk[:, G + 2, r:T:NT], start=True, stop=True).then_inc(s_mm, 1)

                pe.wait_ge(rot_ready, h + 1)
                scores(0)
                pe.wait_ge(vh_ready, G * (h + 1))
                scores(1)
                for r in range(NT):
                    pe.wait_ge(pr_ready, NT * h + r + 1)
                    pe.wait_ge(pT_dve, NT * h + r)
                    pe.wait_ge(pT_act, NT * h + r)
                    for m in range(6):
                        last = tr(ps[:, 6 + m // 4, (m % 4) * P:(m % 4 + 1) * P], pr[:, r % 2, m * P:(m + 1) * P], ident[:])
                        if m == 3:
                            last.then_inc(pr_T, 1)
                    last.then_inc(pr_T, 1)
                    if r + 2 < NT:
                        scores(r + 2)
                    pe.wait_ge(pT_act, NT * h + r + 1)
                    pe.wait_ge(pT_dve, NT * h + r + 1)
                    if r >= 2:
                        pe.wait_ge(att_ready, NT * h + r - 1)
                    for m in range(6):
                        v = vh[:, 0, m, :] if m < NT else vh[:, m - NT + 1, r, :]
                        last = mm(ps[:, r % 2, 0:P], v, pT[:, m, :], start=(m == 0), stop=(m == 5))
                    last.then_inc(pv_mm, 1)

            att_head(0)
            with pe.Fori(1, H) as h:
                att_head(h)

            def merge_step(b):
                for u in range(2):
                    for j, (rhs, nk) in enumerate(((xnT, KD), (xnT, KD), (attT, H), (memT, KD))):
                        if j < 2:
                            pe.wait_ge(sg_ready, 4 * b)
                        else:
                            pe.wait_ge(merged, 2 * b)
                        project(4 * u + j, 2 * H + b + 1, 4 * u + j, rhs, nk)

            pe.wait_ge(att_ready, NT * H)
            pe.wait_ge(mem_ready, 2 * H)
            merge_step(0)
            with pe.Fori(1, KD // 2) as b:
                merge_step(b)
            pe.wait_ge(merged, KD)
            for i in range(NT):
                for n in range(2):
                    if i >= 2:
                        pe.wait_ge(h_ready, 2 * (i - 2) + n + 1)
                    for k in range(KD):
                        if i == 0 and n == 0:
                            pe.wait_ge(w_in_slot[k], DMA * (2 * H + KD // 2 + 1))
                        last = mm(ps[:, 4 + 2 * (i % 2) + n, :], mergedT[:, k, i * P:(i + 1) * P], wring[:, k, n * BANK:(n + 1) * BANK],
                                  start=(k == 0), stop=(k == KD - 1))
                    last.then_inc(mix_mm, 1)

            for i in range(NT):
                transpose_rows(hw_ready, hw_used, xn2T_ready, i)
            pe.wait_ge(router_in, 2 * DMA)
            for i in range(NT):
                pe.wait_ge(xn2T_ready, 2 * (i + 1))
                if i == 0:
                    pe.wait_ge(h_ready, 2 * NT)
                for k in range(KD):
                    last = mm(ps[:, 4, i * E:(i + 1) * E], xnT[:, k, i * P:(i + 1) * P], wr[:, k, :], start=(k == 0), stop=(k == KD - 1))
                last.then_inc(lg_mm, 1)
            pe.wait_ge(late_tables, 1)
            pe.wait_ge(memb_ready, 1)
            for i in range(NT):
                for j in range(i):
                    mm(ps[:, 5, i * E:(i + 1) * E], onesb[:], memb[:, j, :], start=(j == 0), stop=False)
                mm(ps[:, 5, i * E:(i + 1) * E], tri[:], memb[:, i, :], start=(i == 0), stop=True)
            for j in range(NT):
                last = mm(ps[:, 5, NT * E:(NT + 1) * E], onesb[:], memb[:, j, :], start=(j == 0), stop=(j == NT - 1))
            last.then_inc(pos_mm, 1)

            GUB, DNB, TB0, TB1 = 0, 4, 7, 6

            def slots_of(m):
                pe.wait_ge(sel_ready, NT * (m + 1))
                for i in range(NT):
                    last = mm(ps[:, TB1, 0:4], sels[:, i, :], te[:, i, :], start=(i == 0), stop=(i == NT - 1))
                last.then_inc(meta_mm, 1)

            def rows_T(m, xi):
                pe.wait_ge(gathered, DMA * (xi + 1))
                for b, bank in enumerate((TB0, TB1)):
                    if b == 1:
                        pe.wait_ge(meta_ready, 2 * (m + 1))
                    for k in range(4):
                        last = tr(ps[:, bank, k * P:(k + 1) * P], xg[:, (4 * b + k) * P:(4 * b + k + 1) * P], ident[:])
                    last.then_inc(xg_T, 1)

            def gate_up(e, xi, gi):
                pe.wait_ge(xT_ready, 2 * (xi + 1))
                pe.wait_ge(up_read, gi)
                for n in range(4):
                    mm(ps[:, GUB + n, :], sel[:, bass.ds(e, 1), :].rearrange("p a s -> p (a s)"), bsp[:, n * BANK:(n + 1) * BANK],
                       start=True, stop=False)
                for k in range(KD):
                    pe.wait_ge(gu_in[k], DMA * (gi + 1))
                    for n in range(4):
                        last = mm(ps[:, GUB + n, :], xT[:, k, :], guw[:, k, n * BANK:(n + 1) * BANK], start=False, stop=(k == KD - 1))
                    last.then_inc(gu_used, 1)

            def down(e, gi):
                pe.wait_ge(actT_ready, 2 * (gi + 1))
                pe.wait_ge(y_ready, 2 * gi)
                for n in range(2):
                    mm(ps[:, DNB + n, :], sel[:, bass.ds(e, 1), :].rearrange("p a s -> p (a s)"),
                       bsp[:, F2 + n * BANK:F2 + (n + 1) * BANK], start=True, stop=False)
                for k in range(KD):
                    if k % 2 == 0:
                        pe.wait_ge(dn_in[k // 2], DMA * (gi + 1))
                    for n in range(2):
                        last = mm(ps[:, DNB + n, :], actT[:, k, :], dnw[:, k, n * BANK:(n + 1) * BANK], start=False, stop=(k == KD - 1))
                    if k % 2:
                        last.then_inc(dn_used, 1)

            def act_rows_T(gi, xi):
                pe.wait_ge(act_ready, gi + 1)
                pe.wait_ge(xT_ready, 2 * (xi + 1))
                for b, bank in enumerate((TB0, TB1)):
                    for k in range(4):
                        last = tr(ps[:, bank, k * P:(k + 1) * P], act[:, (4 * b + k) * P:(4 * b + k + 1) * P], ident[:])
                    last.then_inc(act_T, 1)

            pe.wait_ge(bias_ready, 1)
            slots_of(0)
            rows_T(0, 0)
            pe.wait_ge(xT_ready, 2)
            slots_of(1)
            gate_up(0, 0, 0)
            pe.wait_ge(meta_ready, 4)
            slots_of(2)
            rows_T(2, 1)
            act_rows_T(0, 1)

            def expert_turn(e):
                gate_up(e, e, e)
                pe.wait_ge(actT_ready, 2 * e)
                slots_of(e + 2)
                rows_T(e + 2, e + 1)
                down(e - 1, e - 1)
                act_rows_T(e, e + 1)

            expert_turn(1)
            with pe.Fori(2, E) as e:
                expert_turn(e)
            down(E - 1, E - 1)
            with pe.If(many(pe) > 0):
                with pe.Fori(1, NT) as b:
                    with pe.Fori(0, E) as e:
                        n = extra(b, e)
                        slots_of(E + 2 + n)
                        rows_T(E + 2 + n, E + 1 + n)
                        gate_up(e, E + 1 + n, E + n)
                        act_rows_T(E + n, E + 1 + n)
                        down(e, E + n)

        @block.scalar
        def _(sc):
            own = Chain(sc, act_step)
            a = nc.scalar.activation

            def squares(i, ready, count, n, done):
                sc.wait_ge(ready, count)
                a(ps[:, 0:2, :].rearrange("p b n -> p (b n)"), hres[:, i, :], ACT.Square, accum_out=ssq[:, n, i:i + 1]).then_inc(done, 1)

            def std(n, ready, done):
                sc.wait_ge(ready, 1)
                a(ssq[:, n, :], ssq[:, n, :], ACT.Sqrt).then_inc(done, 1)

            for i in range(NT):
                if i:
                    sc.wait_ge(x_square, i)
                squares(i, x_in[i], DMA, 0, x_square)
            std(0, x_var, x_std)
            sc.wait_ge(angle_ready, 2)
            a(rcos[:], ang[:, 1, :], ACT.Sin).then_inc(sines_ready, 1)
            a(rsin[:], ang[:, 2, :], ACT.Sin).then_inc(sines_ready, 1)
            sc.wait_ge(gate_abs, 1)
            own.step(a(gat[0:H, 2, :], gat[0:H, 2, :], ACT.Exp))
            a(gat[0:H, 2, :], gat[0:H, 2, :], ACT.Ln, bias=1.0).then_inc(gate_ln, 1)

            sc.wait_ge(bias_ready, 1)
            def mem_head(h, first=False):
                sc.wait_ge(conv_ready, 4 * h)
                for j in range(4):
                    sc.wait_ge(w_used, N_MEM * h + j + 1)
                    nc.scalar.copy(raw[:, j, TAPS - 1:], ps[:, j % 2, :]).then_inc(proj_out, 1)
                if first:
                    sc.wait_ge(gate_cols, 1)
                    a(expE[:], ceT[:, :, 32:32 + H], ACT.Exp).then_inc(gate_cols, 1)
                    sc.wait_ge(sines_done, 1)
                    for n in range(H):
                        sc.wait_ge(nmb_mm, n + 1)
                        nc.scalar.copy(nmb[:, n, :], ps[:, 6 + n % 2, :]).then_inc(nmb_ready, 1)
                for u in range(2):
                    sc.wait_ge(w_used, N_MEM * h + 4 + u + 1)
                    sc.wait_ge(mv_T, 2 * h)
                    nc.scalar.copy(mvraw[:, u, :], ps[:, u, :]).then_inc(proj_out, 1)
                sc.wait_ge(conv_ready, 4 * (h + 1))
                sc.wait_ge(at_mm, NT * h)
                a(qkf[:], cv[:], ACT.Silu).then_inc(qk_ready, 1)
                for u in range(2):
                    sc.wait_ge(w_used, N_MEM * h + 6 + u + 1)
                    sc.wait_ge(mem_ready, 2 * h)
                    a(sgo[:, u, :], ps[:, u, :], ACT.Sigmoid).then_inc(proj_out, 1)
                sc.wait_ge(cols_ready, 3 * (h + 1))
                sc.wait_ge(at_ready, NT * h)
                for j in range(NT):
                    a(wexp[:, j, j * P:(j + 1) * P], nmd[:, j * P:(j + 1) * P], ACT.Exp, bias=ch[:, j:j + 1]).then_inc(wexp_ready, 1)
                    if j < NT - 1:
                        a(wexp[:, j, (j + 1) * P:T], nmb[:, bass.ds(h, 1), (j + 1) * P:T].rearrange("p a t -> p (a t)"),
                          ACT.Exp, bias=ch[:, j:j + 1]).then_inc(wexp_ready, 1)
                for b in range(2):
                    sc.wait_ge(mv_T, 2 * h + b + 1)
                    sc.wait_ge(num_mm, NT * h)
                    nc.scalar.copy(vN[:, 2 * b:2 * b + 2, 0:MDH], ps[:, 2 + b, :].rearrange("p (i c) -> p i c", i=2)).then_inc(vN_ready, 1)
                sc.wait_ge(hvar_ready, h + 1)
                a(mrs[:, 0, :], mrs[:, 0, :], ACT.Sqrt).then_inc(hstd_ready, 1)

            mem_head(0, first=True)
            with sc.Fori(1, H) as h:
                mem_head(h)

            def att_head(h):
                for j in range(2 * G):
                    sc.wait_ge(w_used, ATT0 + N_ATT * h + j + 1)
                    nc.scalar.copy(qk[:, j, :], ps[:, j % 2, :]).then_inc(proj_out, 1)
                for g in range(G):
                    sc.wait_ge(w_used, ATT0 + N_ATT * h + 2 * G + g + 1)
                    nc.scalar.copy(avraw[:, g, :], ps[:, g % 2, :]).then_inc(proj_out, 1)
                for g in range(G):
                    sc.wait_ge(av_T, G * h + g + 1)
                    nc.scalar.copy(vh[:, g, :, :].rearrange("p i c -> p (i c)"), ps[:, (6, 7, 5)[g], :]).then_inc(vh_ready, 1)
                def weights(r):
                    sc.wait_ge(smax_ready, NT * h + r + 1)
                    a(pr[:, r % 2, :], sm[:, r % 2, :], ACT.Exp, bias=smax[:, r % 2, 1:2], scale=QK_SCALE,
                      accum_out=smax[:, r % 2, 2:3]).then_inc(exp_ready, 1)

                weights(0)
                for r in range(NT):
                    if r + 1 < NT:
                        weights(r + 1)
                    sc.wait_ge(pr_T, 2 * (NT * h + r) + 1)
                    nc.scalar.copy(pT[:, 0:4, :].rearrange("p m c -> p (m c)"), ps[:, 6, :]).then_inc(pT_act, 1)

            att_head(0)
            with sc.Fori(1, H) as h:
                att_head(h)

            def merge_step(b):
                for u in range(2):
                    for j in range(2):
                        sc.wait_ge(w_used, MRG0 + N_MRG * b + 4 * u + j + 1)
                        sc.wait_ge(merged, 2 * b)
                        a(sgm[:, u, j, :], ps[:, 4 * u + j, :], ACT.Sigmoid).then_inc(sg_ready, 1)

            sc.wait_ge(att_ready, NT * H)
            merge_step(0)
            with sc.Fori(1, KD // 2) as b:
                merge_step(b)

            for i in range(NT):
                if i:
                    sc.wait_ge(h_square, i)
                squares(i, h_ready, 2 * (i + 1), 1, h_square)
            std(1, h_var, h_std)
            sc.wait_ge(top_ready, 1)
            a(gk[:], gk[:], ACT.Exp).then_inc(gk_ready, 1)

            def sigmoid(gi):
                sc.wait_ge(gt_ready, gi + 1)
                a(sg[:], gt[:], ACT.Sigmoid, scale=SWIGLU_ALPHA).then_inc(sg_ready2, 1)

            def weighted(e, gi):
                sc.wait_ge(y_ready, 2 * gi)
                own.step(nc.scalar.copy(gcur[:], gate_of[:, bass.ds(e, 1)]))
                sc.wait_ge(dn_used, (KD // 2) * (gi + 1))
                sc.wait_ge(y_stored, DMA * gi)
                for n in range(2):
                    nc.scalar.mul(yw[:, n * BANK:(n + 1) * BANK], ps[:, 4 + n, :], gcur[:, 0:1]).then_inc(y_ready, 1)

            def act_rows(gi):
                for b, bank in enumerate((7, 6)):
                    sc.wait_ge(act_T, 2 * gi + b + 1)
                    nc.scalar.copy(actT[:, 4 * b:4 * b + 4, :].rearrange("p k c -> p (k c)"), ps[:, bank, :]).then_inc(actT_ready, 1)

            sigmoid(0)
            act_rows(0)

            def expert_turn(e):
                sigmoid(e)
                weighted(e - 1, e - 1)
                act_rows(e)

            expert_turn(1)
            with sc.Fori(2, E) as e:
                own.begin(e - 2, 1)
                expert_turn(e)
                own.end(E - 2)
            weighted(E - 1, E - 1)
            with sc.If(many(sc) > 0):
                common, own = own, Chain(sc, act_over)
                with sc.Fori(1, NT) as b:
                    with sc.Fori(0, E) as e:
                        n = extra(b, e)
                        own.begin(n, 1)
                        sigmoid(E + n)
                        act_rows(E + n)
                        weighted(e, E + n)
                        own.end((NT - 1) * E)
                own = common
            for i in range(NT):
                if i:
                    sc.wait_ge(f_square, i)
                squares(i, f_sum, i + 1, 2, f_square)
            std(2, f_var, f_std)

        @block.vector
        def _(dve):
            own = Chain(dve, dve_step)
            v = nc.vector
            tt, ts, stt = v.tensor_tensor, v.tensor_scalar, v.scalar_tensor_tensor

            def variance(n, ready, done):
                dve.wait_ge(ready, NT)
                ts(ssq[:, n, :], ssq[:, n, :], 1.0 / D, RMS_EPS, ALU.mult, ALU.add).then_inc(done, 1)

            def scaled_chunks(count, gain, ready, at):
                for b in range(2):
                    dve.wait_ge(count[0], count[1] + b + 1)
                    bank, dst = at(b)
                    tt(dst, ps[:, bank, :].rearrange("p (k c) -> p k c", k=4),
                       vecT[:, gain + 4 * b:gain + 4 * b + 4].unsqueeze(2).to_broadcast([P, 4, P]), ALU.mult).then_inc(ready, 1)

            dve.wait_ge(vecT_done, 2)
            own.mark(v.tensor_copy(vecT[:], ps[:, 7, 0:88]))
            own.mark(v.tensor_copy(fcol[:], ps[:, 6, 0:2]))
            own.settle()
            variance(0, x_square, x_var)
            dve.wait_ge(x_std, 1)
            own.step(v.reciprocal(rstd[:, 0, :], ssq[:, 0, :]))
            for i in range(NT):
                if i >= 2:
                    dve.wait_ge(xw_used, 2 * (i - 1))
                ts(xw[:, i % 2, :], hres[:, i, :], rstd[:, 0, i:i + 1], None, ALU.mult).then_inc(xw_ready, 1)
                if i:
                    scaled_chunks((xw_used, 2 * (i - 1)), GMIX, xnT_ready,
                                  lambda b, i=i - 1: (2 * (i % 2) + b, xnT[:, 4 * b:4 * b + 4, i * P:(i + 1) * P]))
            scaled_chunks((xw_used, 2 * (NT - 1)), GMIX, xnT_ready,
                          lambda b, i=NT - 1: (2 * (i % 2) + b, xnT[:, 4 * b:4 * b + 4, i * P:(i + 1) * P]))
            TWO_PI = 2.0 * float(np.pi)
            C1 = 6.28125
            C2 = float(np.float32(np.round((TWO_PI - C1) * 2 ** 21) / 2 ** 21))
            C3 = TWO_PI - C1 - C2
            MAGIC = 1.5 * 2 ** 23
            TOP = 3.1415925
            dve.wait_ge(pos_in, DMA)
            own.step(ts(ang[:, 0, :], post[:], fcol[0:ROT, 0:1], None, ALU.mult))
            turns = rcos
            for n, (shift, offset) in enumerate(((0.25, float(np.pi) / 2), (0.0, 0.0))):
                a1 = ang[:, n + 1, :]
                own.step(ts(turns[:], ang[:, 0, :], 1.0 / TWO_PI, shift, ALU.mult, ALU.add))
                own.step(ts(turns[:], turns[:], MAGIC, None, ALU.add))
                own.step(ts(turns[:], turns[:], MAGIC, None, ALU.subtract))
                own.step(stt(a1, turns[:], -C1, ang[:, 0, :], ALU.mult, ALU.add))
                own.step(stt(a1, turns[:], -C2, a1, ALU.mult, ALU.add))
                own.step(stt(a1, turns[:], -C3, a1, ALU.mult, ALU.add))
                own.step(ts(a1, a1, offset, TOP, ALU.add, ALU.min))
                ts(a1, a1, -TOP, None, ALU.max).then_inc(angle_ready, 1)

            R = slice(0, H)
            R2 = slice(32, 32 + H)
            dve.wait_ge(gate_mm, 1)
            dve.wait_ge(bif_in, 2 * DMA)
            own.mark(ts(gat[R, 0, :], ps[R, 4, :], bcol[R, 0:1], None, ALU.add))
            own.step(ts(gat[R, 1, :], ps[R2, 4, :], bcol[R2, 0:1], None, ALU.add))
            stt(gat[R, 2, :], gat[R, 1, :], -1.0, gat[R, 1, :], ALU.mult, ALU.min).then_inc(gate_abs, 1)
            dve.wait_ge(gate_ln, 1)
            own.step(stt(gat[R, 1, :], gat[R, 1, :], 0.0, gat[R, 2, :], ALU.min, ALU.subtract))
            own.step(v.tensor_tensor_scan(gat[R, 2, :], ones_row[:], gat[R, 1, :], 0.0, ALU.mult, ALU.add))
            dve.wait_ge(tables, made["ce"])
            own.step(tt(ce[R, :], gat[R, 0, :], gat[R, 2, :], ALU.subtract))
            own.step(v.tensor_tensor_scan(gat[R, 0, :], ones_row[:], ce[R, :], 0.0, ALU.mult, ALU.max))
            stt(ce[R2, :], gat[R, 2, :], -1.0, gat[R, 0, :], ALU.mult, ALU.subtract).then_inc(gate_rows, 1)
            ts(gat[R, 1, :], gat[R, 0, :], -1.0, None, ALU.mult).then_inc(gate_rows, 1)
            dve.wait_ge(sines_ready, 2)
            ts(rsin[:], rsin[:], fcol[0:ROT, 1:2], None, ALU.mult).then_inc(sines_done, 1)

            dve.wait_ge(m4_made, 1)
            own.step(ts(m4[:], m4[:], 3, None, ALU.bitwise_and))
            ts(amask[:, :, T + P:SC], m4[:].unsqueeze(1).to_broadcast([P, NT, P]), NEG, None, ALU.mult).then_inc(m4_ready, 1)
            WEXPS = 2 * NT - 1

            def mem_head(h, first=False):
                dve.wait_ge(wexp_ready, WEXPS * h)
                dve.wait_ge(mem_ready, 2 * h)
                cols = vecT[:, 0:GMIX].rearrange("p (t c) -> p t c", t=TAPS)
                own.mark(v.tensor_copy(cwh[:, :, 0:2], cols[:, :, bass.ds(2 * h, 2)]))
                own.mark(v.tensor_copy(cwh[:, :, 2:4], cols[:, :, bass.ds(KD + 2 * h, 2)]))
                own.mark(v.tensor_copy(gmh[:], vecT[:, bass.ds(GMEM + 2 * h, 2)]))
                own.settle()
                dve.wait_ge(qk_ready, h)
                for j in range(4):
                    dve.wait_ge(proj_out, N_MEM * h + j + 1)
                    own.step(ts(cv[:, j, :], raw[:, j, 0:T], cwh[:, 0, j:j + 1], None, ALU.mult))
                    for t in range(1, TAPS):
                        ins = stt(cv[:, j, :], raw[:, j, t:t + T], cwh[:, t, j:j + 1], cv[:, j, :], ALU.mult, ALU.add)
                        if t < TAPS - 1:
                            own.step(ins)
                        else:
                            ins.then_inc(conv_ready, 1)
                if first:
                    dve.wait_ge(gate_T, 1)
                    v.tensor_copy(ceT[:].rearrange("p i c -> p (i c)"), ps[:, 5, 0:NT * 64]).then_inc(gate_cols, 1)
                    dve.wait_ge(gate_cols, 2)
                    dve.wait_ge(nmb_ready, H)
                    dve.wait_ge(tables, made["cmask"])
                v.tensor_copy(ch[:], ceT[:, :, bass.ds(h, 1)].rearrange("p i a -> p (i a)")).then_inc(cols_ready, 1)
                v.tensor_copy(eh[:], expE[:, :, bass.ds(h, 1)].rearrange("p i a -> p (i a)")).then_inc(cols_ready, 1)
                tt(nmd[:].rearrange("p (i t) -> p i t", i=NT), nmb[:, bass.ds(h, 1), :].rearrange("p a (i t) -> p (a i) t", i=NT),
                   cmask[:].unsqueeze(1).to_broadcast([P, NT, P]), ALU.add).then_inc(cols_ready, 1)
                dve.wait_ge(cols_ready, 3 * (h + 1))
                dve.wait_ge(wexp_ready, WEXPS * (h + 1))
                for j in range(NT):
                    dve.wait_ge(at_mm, NT * h + j + 1)
                    stt(AT[:, j, j * P:T], ps[:, 4 + j % 2, j * P:T], MK_SCALE, wexp[:, j, j * P:T],
                        ALU.mult, ALU.mult).then_inc(at_ready, 1)
                for i in range(NT):
                    dve.wait_ge(num_mm, NT * h + i + 1)
                    num = ps[:, 6 + i % 2, :]
                    own.step(ts(den[:, 0, i:i + 1], num[:, MDH:MDH + 1], eh[:, i:i + 1], None, ALU.max))
                    own.step(stt(den[:, 0, i:i + 1], num[:, MDH:MDH + 1], -1.0, den[:, 0, i:i + 1], ALU.mult, ALU.max))
                    own.step(v.reciprocal(den[:, 1, i:i + 1], den[:, 0, i:i + 1]))
                    ts(hh[:, i, :], num[:, 0:MDH], den[:, 1, i:i + 1], None, ALU.mult).then_inc(num_out, 1)
                    dve.wait_ge(num_out, NT * h + i + 1)
                    own.mark(v.bn_stats(bst[:, i, :], hh[:, i, :]))
                own.settle()
                v.memset(mrs[:], 0.0)
                for i in range(NT):
                    own.mark(v.bn_aggr(mv[:, i, :], bst[:, i, :]))
                own.settle()
                ts(mrs[:, 0, :], mv[:, :, 1], LN_EPS, None, ALU.add).then_inc(hvar_ready, 1)
                dve.wait_ge(hstd_ready, h + 1)
                own.step(v.reciprocal(mrs[:, 1, :], mrs[:, 0, :]))
                for i in range(NT):
                    ts(hh[:, i, :], hh[:, i, :], mv[:, i, 0:1], mrs[:, 1, i:i + 1], ALU.subtract, ALU.mult).then_inc(hn_ready, 1)
                dve.wait_ge(hn_T, h + 1)
                for c in range(2):
                    stt(memT[:, bass.ds(2 * h + c, 1), :].rearrange("p a t -> p (a t)"), ps[:, 2 + c, :], gmh[:, c:c + 1], sgo[:, c, :],
                        ALU.mult, ALU.mult).then_inc(mem_ready, 1)

            own.begin(0, 36)
            mem_head(0, first=True)
            own.end(1)
            with dve.Fori(1, H) as h:
                own.begin(h - 1, 36)
                mem_head(h)
                own.end(H - 1)

            def att_head(h):
                dve.wait_ge(proj_out, ATT0 + N_ATT * h + 2 * G)
                swap = [(i + HALF) % ROT for i in range(ROT)]
                rows = qk[0:ROT, :, :]
                flat = lambda t: t.rearrange("p g t -> p (g t)")
                v.memset(tick[:], 0.0)
                own.step(v.stream_shuffle(flat(rs[:]), flat(rows), swap))
                own.mark(tt(rs[:], rs[:], rsin[:].unsqueeze(1).to_broadcast([ROT, 2 * G, T]), ALU.mult))
                own.step(tt(rows, rows, rcos[:].unsqueeze(1).to_broadcast([ROT, 2 * G, T]), ALU.mult))
                tt(rows, rows, rs[:], ALU.add).then_inc(rot_ready, 1)

                def masked(r):
                    dve.wait_ge(s_mm, NT * h + r + 1)
                    b = 2 + 2 * (r % 2)
                    v.memset(tick[:], 0.0)
                    own.step(v.tensor_tensor_reduce(out=sm[:, r % 2, :], in0=ps[:, b:b + 2, :].rearrange("p b t -> p (b t)")[:, 0:SC],
                                                    in1=amask[:, r, :], scale=1.0, scalar=NEG, op0=ALU.add, op1=ALU.max,
                                                    accum_out=smax[:, r % 2, 0:1]))
                    ts(smax[:, r % 2, 1:2], smax[:, r % 2, 0:1], -QK_SCALE, None, ALU.mult).then_inc(smax_ready, 1)

                def weights(r):
                    dve.wait_ge(exp_ready, NT * h + r + 1)
                    own.step(v.reciprocal(smax[:, r % 2, 3:4], smax[:, r % 2, 2:3]))
                    ts(pr[:, r % 2, :], pr[:, r % 2, :], smax[:, r % 2, 3:4], None, ALU.mult).then_inc(pr_ready, 1)

                masked(0)
                masked(1)
                weights(0)
                for r in range(NT):
                    if r + 2 < NT:
                        masked(r + 2)
                    dve.wait_ge(pr_T, 2 * (NT * h + r + 1))
                    v.tensor_copy(pT[:, 4:6, :].rearrange("p m c -> p (m c)"), ps[:, 7, 0:2 * P]).then_inc(pT_dve, 1)
                    if r + 1 < NT:
                        weights(r + 1)
                    dve.wait_ge(pv_mm, NT * h + r + 1)
                    v.tensor_copy(attT[:, bass.ds(h, 1), r:T:NT].rearrange("p a t -> p (a t)"), ps[:, r % 2, 0:P]).then_inc(att_ready, 1)

            dve.wait_ge(tables, made["amask"])
            own.begin(0, 11)
            att_head(0)
            own.end(1)
            with dve.Fori(1, H) as h:
                own.begin(h - 1, 11)
                att_head(h)
                own.end(H - 1)

            def merge_step(b):
                for u in range(2):
                    for j in range(2):
                        dve.wait_ge(w_used, MRG0 + N_MRG * b + 4 * u + 2 + j + 1)
                        dve.wait_ge(sg_ready, 4 * b + 2 * u + j + 1)
                        own.mark(tt(mgt[:, u, j, :], ps[:, 4 * u + 2 + j, :], sgm[:, u, j, :], ALU.mult))
                    own.settle()
                    tt(mergedT[:, bass.ds(2 * b + u, 1), :].rearrange("p a t -> p (a t)"), mgt[:, u, 0, :], mgt[:, u, 1, :],
                       ALU.add).then_inc(merged, 1)

            own.begin(0, 4)
            merge_step(0)
            own.end(1)
            with dve.Fori(1, KD // 2) as b:
                own.begin(b - 1, 4)
                merge_step(b)
                own.end(KD // 2 - 1)
            for i in range(NT):
                for n in range(2):
                    dve.wait_ge(mix_mm, 2 * i + n + 1)
                    hn = hres[:, i, n * BANK:(n + 1) * BANK]
                    tt(hn, hn, ps[:, 4 + 2 * (i % 2) + n, :], ALU.add).then_inc(h_ready, 1)

            variance(1, h_square, h_var)
            dve.wait_ge(h_std, 1)
            own.step(v.reciprocal(rstd[:, 1, :], ssq[:, 1, :]))
            for i in range(NT):
                if i >= 2:
                    dve.wait_ge(hw_used, 2 * (i - 1))
                    dve.wait_ge(xn_stored[i - 2], DMA)
                ts(xw[:, i % 2, :], hres[:, i, :], rstd[:, 1, i:i + 1], None, ALU.mult).then_inc(hw_ready, 1)
                if i:
                    scaled_chunks((hw_used, 2 * (i - 1)), GFFN, xn2T_ready,
                                  lambda b, i=i - 1: (2 * (i % 2) + b, xnT[:, 4 * b:4 * b + 4, i * P:(i + 1) * P]))
            scaled_chunks((hw_used, 2 * (NT - 1)), GFFN, xn2T_ready,
                          lambda b, i=NT - 1: (2 * (i % 2) + b, xnT[:, 4 * b:4 * b + 4, i * P:(i + 1) * P]))
            dve.wait_ge(lg_mm, NT)
            own.step(tt(lg[:], ps[:, 4, 0:NT * E].rearrange("p (i e) -> p i e", i=NT), brt[:].unsqueeze(1).to_broadcast([P, NT, E]), ALU.add))
            for i in range(NT):
                own.step(v.max(v8[:, i, :], lg[:, i, :]))
                own.mark(v.max_index(i8[:, i, :], v8[:, i, :], lg[:, i, :]))
            own.settle()
            own.mark(v.tensor_copy(i8f[:], i8[:]))
            tt(gk[:], v8[:, :, 0:TOP_K], v8[:, :, 0:1].to_broadcast([P, NT, TOP_K]), ALU.subtract).then_inc(top_ready, 1)
            own.settle()
            dve.wait_ge(late_tables, 1)
            full = [P, NT, TOP_K, E]
            own.step(tt(oh, iota_e[:].unsqueeze(1).unsqueeze(1).to_broadcast(full), i8f[:, :, 0:TOP_K].unsqueeze(3).to_broadcast(full),
                        ALU.is_equal))
            over_k = lambda t: t.rearrange("p i k e -> p i e k")
            own.step(v.tensor_reduce(member, over_k(oh), AX.X, ALU.add))
            v.tensor_copy(memb[:], member).then_inc(memb_ready, 1)
            own.step(tt(oht, oh, iota_k[:].unsqueeze(1).unsqueeze(3).to_broadcast(full), ALU.mult))
            own.step(v.tensor_reduce(kth, over_k(oht), AX.X, ALU.add))
            dve.wait_ge(gk_ready, 1)
            own.step(v.tensor_reduce(gs[:, 0, :], gk[:], AX.X, ALU.add))
            own.step(v.reciprocal(gs[:, 1, :], gs[:, 0, :]))
            own.step(tt(gk[:], gk[:], gs[:, 1, :].unsqueeze(2).to_broadcast([P, NT, TOP_K]), ALU.mult))
            own.step(tt(oht, oh, gk[:].unsqueeze(3).to_broadcast(full), ALU.mult))
            own.step(v.tensor_reduce(gte, over_k(oht), AX.X, ALU.add))
            entry = lambda n: tbl[:, 0:E, :, n].rearrange("p e i -> p i e")
            per_tok = lambda n: tokf[:, n, :].unsqueeze(2).to_broadcast([P, NT, E])
            v.tensor_copy(entry(3), gte).then_inc(tbl_ready, 1)
            tt(entry(1), member, per_tok(0), ALU.mult).then_inc(tbl_ready, 1)
            own.step(tt(oht[:, :, 0, :], member, per_tok(1), ALU.mult))
            tt(entry(2), oht[:, :, 0, :], kth, ALU.add).then_inc(tbl_ready, 1)
            dve.wait_ge(pos_mm, 1)
            own.step(ts(pos1, ps[:, 5, 0:NT * E].rearrange("p (i e) -> p i e", i=NT), 1.0, None, ALU.add))
            own.step(tt(pos1, pos1, member, ALU.mult))
            ts(entry(0), pos1, -1.0, None, ALU.add).then_inc(tbl_ready, 1)
            own.step(v.tensor_reduce(ovf[:], ps[:, 5, NT * E:(NT + 1) * E], AX.X, ALU.max))
            ts(flag[:], ovf[:], float(P), None, ALU.is_gt).then_inc(flag_ready, 1)

            def select(m, slots):
                dve.wait_ge(te_ready, m + 1)
                dve.wait_ge(meta_mm, m)
                for i in range(NT):
                    ts(sels[:, i, :], slots[:], te[:, i, 0:1], None, ALU.is_equal).then_inc(sel_ready, 1)

            def selected(e, m):
                dve.wait_ge(meta_mm, m + 1)
                ts(idx_of[:, bass.ds(e, 1), :].rearrange("p a c -> p (a c)"), ps[:, 6, 1:3], float(ABSENT), None, ALU.add).then_inc(meta_ready, 1)
                v.tensor_copy(gate_of[:, bass.ds(e, 1)], ps[:, 6, 3:4]).then_inc(meta_ready, 1)

            def rows(xi):
                scaled_chunks((xg_T, 2 * xi), GFFN, xT_ready, lambda b: ((7, 6)[b], xT[:, 4 * b:4 * b + 4, :]))

            def swiglu(gi):
                dve.wait_ge(gu_used, KD * (gi + 1))
                hg = ps[:, 0:4, :].rearrange("p b (n c) -> p c (b n)", c=2)
                ts(gt[:], hg[:, 0, :], SWIGLU_LIMIT, None, ALU.min).then_inc(gt_ready, 1)
                ts(up[:], hg[:, 1, :], SWIGLU_LIMIT, -SWIGLU_LIMIT, ALU.min, ALU.max).then_inc(up_read, 1)
                dve.wait_ge(sg_ready2, gi + 1)
                own.step(tt(gt[:], gt[:], sg[:], ALU.mult))
                dve.wait_ge(act_T, 2 * gi)
                stt(act[:], up[:], 1.0, gt[:], ALU.add, ALU.mult).then_inc(act_ready, 1)

            own.begin(0, 1)
            select(0, iota_slot)
            selected(0, 0)
            select(1, iota_slot)
            rows(0)
            selected(1, 1)
            select(2, iota_slot)
            selected(2, 2)
            rows(1)
            swiglu(0)
            own.end(1)
            with dve.Fori(1, E) as e:
                own.begin(e - 1, 1)
                select(e + 2, iota_slot)
                selected(e + 2, e + 2)
                rows(e + 1)
                swiglu(e)
                own.end(E - 1)
            with dve.If(many(dve) > 0):
                common, own = own, Chain(dve, dve_over)
                v.tensor_copy(slot_b[:], iota_slot[:]).then_inc(slot_ready, 1)
                with dve.Fori(1, NT) as b:
                    dve.wait_ge(slot_ready, b)
                    ts(slot_b[:], slot_b[:], float(P), None, ALU.add).then_inc(slot_ready, 1)
                    dve.wait_ge(slot_ready, b + 1)
                    v.memset(tick[:], 0.0)
                    with dve.Fori(0, E) as e:
                        n = extra(b, e)
                        own.begin(n, 1)
                        select(E + 2 + n, slot_b)
                        selected(e, E + 2 + n)
                        rows(E + 1 + n)
                        swiglu(E + n)
                        own.end((NT - 1) * E)
                own = common

            for i in range(NT):
                dve.wait_ge(y_in[i], DMA)
                y = yfin[:, i, :]
                own.mark(tt(y[:, 0:D], y[:, 0:D], y[:, D:2 * D], ALU.add))
                own.step(tt(y[:, 2 * D:3 * D], y[:, 2 * D:3 * D], y[:, 3 * D:4 * D], ALU.add))
                own.mark(tt(hres[:, i, :], hres[:, i, :], y[:, 0:D], ALU.add))
                own.settle()
                tt(hres[:, i, :], hres[:, i, :], y[:, 2 * D:3 * D], ALU.add).then_inc(f_sum, 1)
            variance(2, f_square, f_var)
            dve.wait_ge(f_std, 1)
            own.step(v.reciprocal(rstd[:, 2, :], ssq[:, 2, :]))
            dve.wait_ge(gfin_in, DMA)
            for i in range(NT):
                stt(hres[:, i, :], hres[:, i, :], rstd[:, 2, i:i + 1], gfin, ALU.mult, ALU.mult).then_inc(o_ready, 1)


_INS = ['x', 'positions', 'g_mix', 'w_in', 'conv_qk', 'b_if', 'g_mlstm_norm', 'w_attn_out', 'w_mlstm_out', 'w_mix_out', 'g_ffn',
        'w_router', 'b_router', 'w_gate_up', 'b_gate_up', 'w_down', 'b_down', 'g_final']


def kernel(**inputs):
    import concourse.bacc as _bacc
    from concourse.bass_utils import run_bass_kernel_spmd as _run

    nc = _bacc.Bacc("TRN2", target_bir_lowering=False, num_devices=1)
    arrays, args = {}, []
    for name in _INS:
        a = np.ascontiguousarray(inputs[name])
        arrays[f"in_{name}"] = a
        args.append(nc.dram_tensor(f"in_{name}", a.shape, mybir.dt.from_np(a.dtype), kind="ExternalInput").ap())
    shape = arrays["in_x"].shape
    args.append(nc.dram_tensor("out_0", shape, F32, kind="ExternalOutput").ap())
    hybrid_block(nc, *args)
    r = _run(nc, [arrays], core_ids=[0])
    return r.results[0]["out_0"]
```

```python
from contextlib import ExitStack

import numpy as np

import concourse.bass as bass
from concourse import mybir

F32 = mybir.dt.float32
F32R = mybir.dt.float32r
BF16 = mybir.dt.bfloat16
I32 = mybir.dt.int32
U32 = mybir.dt.uint32
ALU = mybir.AluOpType
ACT = mybir.ActivationFunctionType
AX = mybir.AxisListType

P = 128
BANK = 512
NEG = -1.0e30
RMS_EPS = 1e-5
LN_EPS = 1e-5
ROPE_THETA = 500000.0
WINDOW0 = 128
SWIGLU_LIMIT = 7.0
SWIGLU_ALPHA = 1.702
TOP_K = 4
ABSENT = 4096
DMA = 16


class Chain:

    def __init__(self, eng, sem):
        self.eng, self.sem, self.total, self.base, self.n = eng, sem, 0, 0, 0

    def begin(self, turn, per_turn):
        self.total += self.n
        self.per, self.base, self.n = per_turn, self.total + turn * per_turn, 0

    def end(self, turns):
        assert self.n == self.per, f"{self.n} steps in a turn, not {self.per}"
        self.total += turns * self.per
        self.base, self.n = self.total, 0

    def mark(self, ins):
        self.n += 1
        ins.then_inc(self.sem, 1)

    def settle(self):
        self.eng.wait_ge(self.sem, self.base + self.n)

    def step(self, ins):
        self.mark(ins)
        self.settle()


class Region:

    def __init__(self, nc, start, end):
        self.nc, self.at, self.end = nc, start, end

    def tensor(self, name, shape, dt=F32):
        size = 1
        for n in shape[1:]:
            size *= n
        size = -(-size * (2 if dt == BF16 else 4) // 32) * 32
        assert self.at + size <= self.end, f"{name}: {self.at + size} of {self.end}"
        t = self.nc.alloc_sbuf_tensor_at(name, shape, dt, offset=self.at)
        self.at += size
        return t


def hybrid_block(nc, x, positions, g_mix, w_in, conv_qk, b_if, g_mlstm_norm, w_attn_out, w_mlstm_out, w_mix_out,
                 g_ffn, w_router, b_router, w_gate_up, b_gate_up, w_down, b_down, g_final, out):
    _, T, D = x.shape
    NT = T // P
    KD = D // P
    E = w_router.shape[2]
    F = w_down.shape[2]
    F2 = 2 * F
    H = 4
    G = 3
    DH = 128
    MDH = D // H
    QK_SCALE = float(DH) ** -0.5
    MK_SCALE = float(MDH) ** -0.5
    TAPS = conv_qk.shape[1]
    CT = 2 * D // P
    ROT = DH // 4
    HALF = ROT // 2
    AW = G * H * DH
    AQ, AK, AV = 0, AW, 2 * AW
    MQ = 3 * AW
    MK, MV, MO, MI = MQ + D, MQ + 2 * D, MQ + 3 * D, MQ + 4 * D
    MF = MI + H
    GA = MF + H
    GM = GA + D
    assert T == BANK and DH == P and MDH == 2 * P and w_in.shape[2] == GM + D and F == D and E == 32

    def chunked(w):
        return w.rearrange("(k p) n -> p k n", p=P)

    w_in_v, wa_v, wm_v, wmix_v = chunked(w_in[0]), chunked(w_attn_out[0]), chunked(w_mlstm_out[0]), chunked(w_mix_out[0])
    gu_v = w_gate_up[0].rearrange("e (k p) n -> p e k n", p=P)
    dn_v = w_down[0].rearrange("e (k p) n -> p e k n", p=P)
    x_v = x[0].rearrange("(i p) d -> p i d", p=P)
    out_v = out[0].rearrange("(i p) d -> p i d", p=P)

    xn_rows = nc.dram_tensor("xn_rows", (T, D), F32).ap()
    y_rows = nc.dram_tensor("y_rows", (T * TOP_K, D), F32).ap()
    xn_v = xn_rows.rearrange("(i p) d -> p i d", p=P)
    y_v = y_rows.rearrange("(i p k) d -> p i (k d)", p=P, k=TOP_K)

    keep = Region(nc, -(-nc.sbuf_base // 64) * 64, nc.sbuf_usable_end)
    late_split = Region(nc, keep.at, keep.at + 4 * D * 4)
    hres = keep.tensor("hres", [P, NT, D])
    router_xT = Region(nc, keep.at, keep.at + KD * T * 4)
    xh = keep.tensor("xh", [P, KD, T], F32R)
    router = Region(nc, keep.at, keep.at + KD * T * 4)
    xl = keep.tensor("xl", [P, KD, T], F32R)
    sel = keep.tensor("sel", [P, E, P], BF16)
    bsp = keep.tensor("bsp", [P, F2 + D], BF16)
    ident = keep.tensor("ident", [P, P])
    vecT = keep.tensor("vecT", [P, 88])
    ssq = keep.tensor("ssq", [P, 3, NT])
    rstd = keep.tensor("rstd", [P, 3, NT])
    flag = keep.tensor("flag", [P, 1], I32)
    tick = keep.tensor("tick", [P, 1])
    xn2T = router_xT.tensor("xn2T", [P, KD, T])
    xw2 = router.tensor("xw2", [P, 2, D])
    lg = router.tensor("lg", [P, NT, E])
    brt = router.tensor("brt", [P, E])
    wr = router.tensor("wr", [P, KD, E])
    iota_slot = router.tensor("iota_slot", [P, P])
    gffn = router.tensor("gffn", [P, D])
    chunk_a = Region(nc, router_xT.at - KD * T * 4, router_xT.at)
    chunk_b = Region(nc, router_xT.at, router_xT.at + 2 * D * 4)
    GMIX, GFFN, GMEM = TAPS * CT, TAPS * CT + KD, TAPS * CT + 2 * KD

    RING = 12 * F2 * 4
    mixed = Region(nc, keep.at, keep.at + RING)
    attT = mixed.tensor("attT", [P, H, T])
    memT = mixed.tensor("memT", [P, KD, T])
    mem = Region(nc, mixed.at, mixed.end)
    raw = mem.tensor("raw", [P, 4, T + TAPS - 1])
    cv = mem.tensor("cv", [P, 4, T])
    qkf = mem.tensor("qkf", [P, 4, T])
    mvraw = mem.tensor("mvraw", [P, 2, T])
    VN = MDH + 2
    vN = mem.tensor("vN", [P, NT, VN])
    wexp = mem.tensor("wexp", [P, NT, T])
    AT = mem.tensor("AT", [P, NT, T])
    hh = mem.tensor("hh", [P, NT, MDH])
    sgo = mem.tensor("sgo", [P, 2, T])
    nmb = mem.tensor("nmb", [P, H, T])
    nmd = mem.tensor("nmd", [P, T])
    cmask = mem.tensor("cmask", [P, P])
    ceT = mem.tensor("ceT", [P, NT, 64])
    expE = mem.tensor("expE", [P, NT, H])
    cwh = mem.tensor("cwh", [P, TAPS, 4])
    gmh = mem.tensor("gmh", [P, 2])
    ch = mem.tensor("ch", [P, NT])
    eh = mem.tensor("eh", [P, NT])
    den = mem.tensor("den", [P, 2, NT])
    bst = mem.tensor("bst", [P, NT, 6])
    mv = mem.tensor("mv", [P, NT, 2])
    mrs = mem.tensor("mrs", [P, 2, NT])
    pre = Region(nc, mixed.at, mixed.end)
    pre.tensor("skip_to_wexp", [P, 4 * (T + TAPS - 1) + 8 * T + 2 * T + NT * VN])
    wif = pre.tensor("wif", [P, KD, 64])
    gat = pre.tensor("gat", [64, 3, T])
    ce = pre.tensor("ce", [64, T])
    ones_row = pre.tensor("ones_row", [H, T])
    head_sel = pre.tensor("head_sel", [H, H, P])
    bcol = pre.tensor("bcol", [64, 1])
    norm = Region(nc, mixed.at, mixed.end)
    norm.tensor("skip_to_qkf", [P, 4 * (T + TAPS - 1) + 4 * T])
    xw = norm.tensor("xw", [P, 2, D])
    xt = norm.tensor("xt", [P, 2, 4 * P])
    att = Region(nc, mixed.at, mixed.end)
    qk = att.tensor("qk", [P, 2 * G, T])
    avraw = att.tensor("avraw", [P, G, T])
    vh = att.tensor("vh", [P, G, NT, P])
    SC = T + 2 * P
    sm = att.tensor("sm", [P, 2, SC])
    pr = att.tensor("pr", [P, 2, SC])
    pT = att.tensor("pT", [P, 6, P])
    rs = att.tensor("rs", [ROT, 2 * G, T])
    smax = att.tensor("smax", [P, 2, 4])
    brow = att.tensor("brow", [P, F2 + D])
    mrg = Region(nc, mixed.at, mixed.end)
    attR = mrg.tensor("attR", [P, H, T], F32R)
    attL = mrg.tensor("attL", [P, H, T], F32R)
    memR = mrg.tensor("memR", [P, KD, T], F32R)
    memL = mrg.tensor("memL", [P, KD, T], F32R)
    sgm = mrg.tensor("sgm", [P, 2, 2, T])
    mgt = mrg.tensor("mgt", [P, 2, 2, T])
    wmix1 = mrg.tensor("wmix1", [P, 2, D])
    mixw = Region(nc, keep.at, mixed.at)
    wmix0 = mixw.tensor("wmix0", [P, KD - 2, D])
    tail = Region(nc, keep.at + RING, nc.sbuf_usable_end)
    mergedT = tail.tensor("mergedT", [P, KD, T])
    wraw = tail.tensor("wraw", [P, 4, D])
    split0 = tail.tensor("split0", [P, 2, 2, D], F32R)
    split1 = late_split.tensor("split1", [P, 2, 2, D], F32R)
    fcol = tail.tensor("fcol", [P, 2])
    masks = Region(nc, keep.at + RING, tail.end)
    amask = masks.tensor("amask", [P, NT, SC])
    rcos = masks.tensor("rcos", [ROT, T])
    rsin = masks.tensor("rsin", [ROT, T])
    start = Region(nc, pre.at, mixed.end)
    vrow = start.tensor("vrow", [88, P])
    frow = start.tensor("frow", [1, 2, P])
    post = start.tensor("post", [ROT, T], I32)
    ang = start.tensor("ang", [ROT, 3, T])
    m4 = start.tensor("m4", [P, P], I32)
    wifh = start.tensor("wifh", [P, KD, 64], F32R)
    wifl = start.tensor("wifl", [P, KD, 64], F32R)
    exp_ring = Region(nc, keep.at, keep.at + RING)
    rests = Region(nc, exp_ring.at, exp_ring.end)
    guw = exp_ring.tensor("guw", [P, KD, F2])
    gul = rests.tensor("gul", [P, KD, F2], F32R)
    dnw = exp_ring.tensor("dnw", [P, KD, D])
    ex = Region(nc, keep.at + RING, nc.sbuf_usable_end)
    xg = ex.tensor("xg", [P, D])
    xTh = ex.tensor("xTh", [P, KD, P], F32R)
    xTl = ex.tensor("xTl", [P, KD, P], F32R)
    gt = ex.tensor("gt", [P, F])
    sg = ex.tensor("sg", [P, F])
    up = ex.tensor("up", [P, F])
    actT = ex.tensor("actT", [P, KD, P])
    yw = ex.tensor("yw", [P, D])
    tbl = ex.tensor("tbl", [P, E + 2, NT, 4])
    te = ex.tensor("te", [P, NT, 4])
    sels = ex.tensor("sels", [P, NT, P])
    gate_of = ex.tensor("gate_of", [P, E + 2])
    idx_of = ex.tensor("idx_of", [P, E + 2, 2], I32)
    gcur = ex.tensor("gcur", [P, 1])
    gidx = ex.tensor("gidx", [P, 1], I32)
    sidx = ex.tensor("sidx", [P, 1], I32)
    pool_tick = ex.tensor("pool_tick", [P, 1])
    slot_b = ex.tensor("slot_b", [P, P])
    v8 = ex.tensor("v8", [P, NT, 8])
    i8 = ex.tensor("i8", [P, NT, 8], U32)
    i8f = ex.tensor("i8f", [P, NT, 8])
    gk = ex.tensor("gk", [P, NT, TOP_K])
    gs = ex.tensor("gs", [P, 2, NT])
    iota_e = ex.tensor("iota_e", [P, E])
    iota_k = ex.tensor("iota_k", [P, TOP_K])
    tokf = ex.tensor("tokf", [P, 2, NT])
    i_tmp = ex.tensor("i_tmp", [P, E], I32)
    oh = gt[:, 0:NT * TOP_K * E].rearrange("p (i k e) -> p i k e", i=NT, k=TOP_K)
    oht = sg[:, 0:NT * TOP_K * E].rearrange("p (i k e) -> p i k e", i=NT, k=TOP_K)
    member = up[:, 0:NT * E].rearrange("p (i e) -> p i e", i=NT)
    pos1 = up[:, NT * E:2 * NT * E].rearrange("p (i e) -> p i e", i=NT)
    kth = up[:, 2 * NT * E:3 * NT * E].rearrange("p (i e) -> p i e", i=NT)
    gte = up[:, 3 * NT * E:4 * NT * E].rearrange("p (i e) -> p i e", i=NT)
    memb = ex.tensor("memb", [P, NT, E], BF16)
    tri = ex.tensor("tri", [P, P], BF16)
    onesb = ex.tensor("onesb", [P, P], BF16)
    ovf = ex.tensor("ovf", [P, 1])
    act = sg
    guh = [chunk_a.tensor("guh0", [P, F2], F32R), chunk_a.tensor("guh1", [P, F2], F32R),
           chunk_b.tensor("guh2", [P, F2], F32R), ex.tensor("guh3", [P, F2], F32R)]

    ctx = ExitStack()
    with ctx:
        ps = ctx.enter_context(nc.psum_tensor("ps", [P, 8, BANK], F32))

        def sem(name):
            return ctx.enter_context(nc.semaphore(name))

        x_in = [sem(f"x_in{i}") for i in range(NT)]
        vec_in, pos_in, bif_in, wif_in, brow_in, router_in = (
            sem(n) for n in ("vec_in", "pos_in", "bif_in", "wif_in", "brow_in", "router_in"))
        w_in_slot = [sem(f"w_in_slot{s}") for s in range(4)]
        wmix_in = [sem(f"wmix_in{k}") for k in range(KD)]
        rounded, w_split, xt_ready, xh_ready, wif_round, wif_split, am_round, am_split = (
            sem(n) for n in ("rounded", "w_split", "xt_ready", "xh_ready", "wif_round", "wif_split", "am_round", "am_split"))
        pool_step, dve_step, act_step = sem("pool_step"), sem("dve_step"), sem("act_step")
        tables = sem("tables")
        x_square, x_var, x_std, xw_ready, xw_used, xnT_ready = (
            sem(n) for n in ("x_square", "x_var", "x_std", "xw_ready", "xw_used", "xnT_ready"))
        vecT_done, angle_ready, sines_ready, m4_ready = (
            sem(n) for n in ("vecT_done", "angle_ready", "sines_ready", "m4_ready"))
        m4_made, sines_done, num_out = sem("m4_made"), sem("sines_done"), sem("num_out")
        gate_mm, gate_abs, gate_ln, gate_rows, gate_T, gate_cols, nmb_mm, nmb_ready = (
            sem(n) for n in ("gate_mm", "gate_abs", "gate_ln", "gate_rows", "gate_T", "gate_cols", "nmb_mm", "nmb_ready"))
        w_used, proj_out = sem("w_used"), sem("proj_out")
        conv_ready, qk_ready, cols_ready, wexp_ready, mv_T, vN_ready, at_mm, at_ready, num_mm, hvar_ready, hstd_ready, hn_ready, hn_T, mem_ready = (
            sem(n) for n in ("conv_ready", "qk_ready", "cols_ready", "wexp_ready", "mv_T", "vN_ready", "at_mm", "at_ready",
                             "num_mm", "hvar_ready", "hstd_ready", "hn_ready", "hn_T", "mem_ready"))
        rot_ready, av_T, vh_ready, s_mm, smax_ready, exp_ready, pr_ready, pr_T, pT_act, pT_dve, pv_mm, att_ready = (
            sem(n) for n in ("rot_ready", "av_T", "vh_ready", "s_mm", "smax_ready", "exp_ready", "pr_ready", "pr_T", "pT_act",
                             "pT_dve", "pv_mm", "att_ready"))
        sg_ready, merged, mix_mm, h_ready = (sem(n) for n in ("sg_ready", "merged", "mix_mm", "h_ready"))
        h_square, h_var, h_std, hw_ready, hw_used, xn2T_ready, lg_mm, top_ready, gk_ready, memb_ready, pos_mm, tbl_ready = (
            sem(n) for n in ("h_square", "h_var", "h_std", "hw_ready", "hw_used", "xn2T_ready", "lg_mm",
                             "top_ready", "gk_ready", "memb_ready", "pos_mm", "tbl_ready"))
        late_tables, bias_ready, flag_ready, slot_ready = (sem(n) for n in ("late_tables", "bias_ready", "flag_ready", "slot_ready"))
        gu_rounded, gu_split, xTh_ready = sem("gu_rounded"), sem("gu_split"), sem("xTh_ready")
        gu_in = [sem(f"gu_in{s}") for s in range(KD)]
        dn_in = [sem(f"dn_in{s}") for s in range(KD // 2)]
        gu_used, dn_used, te_ready, sel_ready, meta_mm, meta_ready, gathered, xg_T, xT_ready, up_read, gt_ready, sg_ready2, act_ready, act_T, actT_ready, gcur_ready, y_ready, y_stored = (
            sem(n) for n in ("gu_used", "dn_used", "te_ready", "sel_ready", "meta_mm", "meta_ready", "gathered", "xg_T", "xT_ready",
                             "up_read", "gt_ready", "sg_ready2", "act_ready", "act_T", "actT_ready", "gcur_ready", "y_ready", "y_stored"))
        all_stored, gfin_in, f_sum, f_square, f_var, f_std, o_ready, o_stored = (
            sem(n) for n in ("all_stored", "gfin_in", "f_sum", "f_square", "f_var", "f_std", "o_ready", "o_stored"))
        pool_over, dve_over, act_over = sem("pool_over"), sem("dve_over"), sem("act_over")
        y_in = [sem(f"y_in{i}") for i in range(NT)]
        xn_stored = [sem(f"xn_stored{i}") for i in range(NT)]

        TABLES = ("ident", "wif", "ce", "rows", "raw", "vN", "cmask", "amask", "sel")
        made = {name: n + 1 for n, name in enumerate(TABLES)}

        N_MEM, N_ATT, N_MRG = 8, 3 * G, 8
        ATT0 = N_MEM * H
        MRG0 = ATT0 + N_ATT * H
        MIX0 = MRG0 + N_MRG * (KD // 2)

        def mem_cols(h):
            return [c + MDH * h + P * u for c in (MQ, MK, MV, MO) for u in range(2)]

        def att_cols(h):
            return [c + H * DH * g + DH * h for c in (AQ, AK, AV) for g in range(G)]

        def split(slot):
            return (split0, split1)[slot // 2][:, slot % 2]

        def col(expr):
            return bass.ds(expr, P)

        yfin = guw[:].rearrange("p (i a) n -> p i (a n)", i=NT)
        gfin = dnw[:, 0, :]

        def many(eng):
            eng.wait_ge(flag_ready, 1)
            return eng.value_load(flag[0:1, 0:1], min_val=0, max_val=1)

        def extra(b, e):
            return (b - 1) * E + e

        block = ctx.enter_context(nc.Block())

        @block.sync
        def _(sp):
            nc.sync.dma_start(vrow[0:GMIX, :], conv_qk[0].rearrange("j (c p) -> (j c) p", p=P)).then_inc(vec_in, DMA)
            nc.sync.dma_start(vrow[GMIX:GFFN, :], g_mix.rearrange("a (c p) -> (a c) p", p=P)).then_inc(vec_in, DMA)
            nc.sync.dma_start(vrow[GFFN:GMEM, :], g_ffn.rearrange("a (c p) -> (a c) p", p=P)).then_inc(vec_in, DMA)
            nc.sync.dma_start(vrow[GMEM:GMEM + KD, :], g_mlstm_norm.rearrange("a (c p) -> (a c) p", p=P)).then_inc(vec_in, DMA)
            for i in range(NT):
                nc.sync.dma_start(hres[:, i, :], x_v[:, i, :]).then_inc(x_in[i], DMA)
            nc.sync.dma_start(bcol[0:H, :], b_if[:, 0:H].rearrange("a h -> h a")).then_inc(bif_in, DMA)
            nc.sync.dma_start(bcol[32:32 + H, :], b_if[:, H:2 * H].rearrange("a h -> h a")).then_inc(bif_in, DMA)
            sp.wait_ge(tables, made["wif"])
            nc.sync.dma_start(wif[:, :, 0:H], w_in_v[:, :, MI:MI + H]).then_inc(wif_in, DMA)
            nc.sync.dma_start(wif[:, :, 32:32 + H], w_in_v[:, :, MF:MF + H]).then_inc(wif_in, DMA)
            def load_tile(slot, c, w=w_in_v):
                nk = w.shape[1]
                nc.sync.dma_start(wraw[:, slot, 0:nk * P].rearrange("p (k n) -> p k n", n=P), w[:, :, col(c)]).then_inc(w_in_slot[slot], DMA)

            for j, c in enumerate(mem_cols(0)):
                if j >= 4:
                    sp.wait_ge(w_split, j - 3)
                load_tile(j % 4, c)
                if j == 0:
                    nc.sync.dma_start(post[:], positions[0:1, :].to_broadcast([ROT, T])).then_inc(pos_in, DMA)
            with sp.Fori(1, H) as h:
                for j, c in enumerate([sp.snap(c) for c in mem_cols(h)]):
                    sp.wait_ge(w_split, N_MEM * h + j - 3)
                    load_tile(j % 4, c)
            for j, c in enumerate(att_cols(0)):
                sp.wait_ge(w_split, ATT0 + j - (3 if j < 3 else 2))
                load_tile(j % 3, c)
            sp.wait_ge(mem_ready, 2 * H)
            for g in (0, 64, 96):
                nc.sync.dma_start(brow[g:g + E, 0:F2], b_gate_up[0]).then_inc(brow_in, DMA)
                nc.sync.dma_start(brow[g:g + E, F2:F2 + D], b_down[0]).then_inc(brow_in, DMA)
            with sp.Fori(1, H) as h:
                for j, c in enumerate([sp.snap(c) for c in att_cols(h)]):
                    sp.wait_ge(w_split, ATT0 + N_ATT * h + j - 2)
                    load_tile(j % 3, c)

            def merge_tiles(b, first=False):
                at = [P * (2 * b + u) + k0 for u in range(2) for k0 in (GA, GM, 0, 0)]
                if not first:
                    at = [sp.snap(a) for a in at]
                for u in range(2):
                    for j, w in enumerate((w_in_v, w_in_v, wa_v, wm_v)):
                        if j == 0:
                            sp.wait_ge(w_split, MRG0 + N_MRG * b + 4 * u - (2 if first and u == 0 else 3))
                        if j == 1:
                            sp.wait_ge(w_split, MRG0 + N_MRG * b + 4 * u)
                        load_tile(j, at[4 * u + j], w)

            merge_tiles(0, first=True)
            sp.wait_ge(am_split, 3)
            for k in range(KD):
                nc.sync.dma_start(wmix0[:, k, :] if k < KD - 2 else wmix1[:, k - KD + 2, :], wmix_v[:, k, :]).then_inc(wmix_in[k], DMA)
            with sp.Fori(1, KD // 2) as b:
                merge_tiles(b)
            sp.wait_ge(w_used, MIX0)
            for i in range(NT):
                nc.sync.dma_start(hres[:, i, :], x_v[:, i, :]).then_inc(x_in[i], DMA)
            nc.sync.dma_start(brt[:], b_router[0:1, :].to_broadcast([P, E])).then_inc(router_in, DMA)
            nc.sync.dma_start(wr[:], chunked(w_router[0])).then_inc(router_in, DMA)
            nc.sync.dma_start(gffn[:], g_ffn[0:1, :].to_broadcast([P, D])).then_inc(router_in, DMA)
            sp.wait_ge(merged, KD)

            def load_gu(e, s):
                nc.sync.dma_start(guw[:, s, :], gu_v[:, bass.ds(e, 1), s, :].rearrange("p a n -> p (a n)")).then_inc(gu_in[s], DMA)

            def load_dn(e, s):
                nc.sync.dma_start(dnw[:, 2 * s:2 * s + 2, :],
                                  dn_v[:, bass.ds(e, 1), 2 * s:2 * s + 2, :].rearrange("p a k n -> p (a k) n")).then_inc(dn_in[s], DMA)

            def store_normed():
                for i in range(NT):
                    sp.wait_ge(hw_ready, i + 1)
                    nc.sync.dma_start(xn_v[:, i, :], xw2[:, i % 2, :]).then_inc(xn_stored[i], DMA)

            for s in range(3, KD):
                load_gu(0, s)
            for s in range(KD // 2 - 1):
                load_dn(0, s)
            sp.wait_ge(mix_mm, 2 * NT)
            for s in range(3):
                load_gu(0, s)
            load_dn(0, KD // 2 - 1)
            store_normed()
            for s in range(KD):
                sp.wait_ge(gu_used, s + 1)
                load_gu(1, s)
            with sp.Fori(2, E) as e:
                before = sp.snap(e - 1)
                for s in range(KD):
                    sp.wait_ge(gu_used, KD * (e - 1) + s + 1)
                    load_gu(e, s)
                for s in range(KD // 2):
                    sp.wait_ge(dn_used, (KD // 2) * (e - 2) + s + 1)
                    load_dn(before, s)
            for s in range(KD // 2):
                sp.wait_ge(dn_used, (KD // 2) * (E - 2) + s + 1)
                load_dn(E - 1, s)
            with sp.If(many(sp) > 0):
                with sp.Fori(1, NT) as b:
                    with sp.Fori(0, E) as e:
                        g_idx = extra(b, e) + E
                        for s in range(KD):
                            sp.wait_ge(gu_used, KD * (g_idx - 1) + s + 1)
                            load_gu(e, s)
                        for s in range(KD // 2):
                            sp.wait_ge(dn_used, (KD // 2) * (g_idx - 1) + s + 1)
                            load_dn(e, s)
            sp.wait_ge(all_stored, 1)
            sp.wait_ge(dn_used, KD // 2 * E)
            nc.sync.dma_start(gfin[:], g_final.rearrange("(a d) -> a d", a=1).to_broadcast([P, D])).then_inc(gfin_in, DMA)
            for i in range(NT):
                nc.sync.dma_start(yfin[:, i, :], y_v[:, i, :]).then_inc(y_in[i], DMA)
            for i in range(NT):
                sp.wait_ge(o_ready, i + 1)
                nc.sync.dma_start(out_v[:, i, :], hres[:, i, :]).then_inc(o_stored, DMA)
            sp.wait_ge(o_stored, DMA * NT)

        @block.gpsimd
        def _(pool):
            own = Chain(pool, pool_step)
            g = nc.gpsimd

            def table(name, ins):
                ins.then_inc(tables, 1)
                pool.wait_ge(tables, made[name])

            own.step(g.memset(ident[:], 0.0))
            table("ident", g.affine_select(out=ident[:], in_=ident[:], compare_op=ALU.not_equal, fill=1.0, base=0,
                                  pattern=[[-1, P]], channel_multiplier=1))
            table("wif", g.memset(wif[:], 0.0))
            table("ce", g.memset(ce[:], 0.0))
            own.step(g.memset(ones_row[:], 1.0))
            own.step(g.memset(frow[:], -1.0))
            for j in range(HALF):
                freq = float(np.float32(ROPE_THETA) ** np.float32(-j / HALF))
                own.step(g.memset(frow[0:1, 0, j:j + HALF + 1:HALF], freq))
            own.step(g.memset(frow[0:1, 1, HALF:ROT], 1.0))
            own.step(g.memset(head_sel[:], 0.0))
            table("rows", g.affine_select(out=head_sel[:], in_=head_sel[:], compare_op=ALU.not_equal, fill=1.0, base=0,
                                  pattern=[[-1, H], [0, P]], channel_multiplier=1))
            table("raw", g.memset(raw[:, :, 0:TAPS - 1], 0.0))
            table("vN", g.memset(vN[:, :, MDH:VN], 1.0))
            g.iota(m4[:], pattern=[[-1, P]], base=P, channel_multiplier=1).then_inc(m4_made, 1)
            pool.wait_ge(m4_made, 1)
            own.step(g.memset(cmask[:], 0.0))
            table("cmask", g.affine_select(out=cmask[:], in_=cmask[:], compare_op=ALU.is_ge, fill=NEG, base=0,
                                  pattern=[[1, P]], channel_multiplier=-1))

            def rest(n, slot, nk=KD):
                pool.wait_ge(rounded, n + 1)
                g.tensor_tensor(split(slot)[:, 1, 0:nk * P], wraw[:, slot, 0:nk * P], split(slot)[:, 0, 0:nk * P], ALU.subtract).then_inc(w_split, 1)

            for j in range(N_MEM):
                rest(j, j % 4)
            pool.wait_ge(w_split, N_MEM)
            own.step(g.memset(amask[:, :, 0:T + P], 0.0))
            m0, m1, m2 = amask[:, :, 0:T], amask[:, :, T:T + P], amask[:, :, T + P:SC]
            own.step(g.affine_select(out=m0, in_=m0, compare_op=ALU.is_ge, fill=NEG, base=0,
                                     pattern=[[1, NT], [-1, T]], channel_multiplier=NT))
            own.step(g.affine_select(out=m0, in_=m0, compare_op=ALU.is_ge, fill=NEG, base=WINDOW0,
                                     pattern=[[-1, NT], [1, T]], channel_multiplier=-NT))
            own.step(g.affine_select(out=m1, in_=m1, compare_op=ALU.is_ge, fill=NEG, base=0,
                                     pattern=[[0, NT], [-1, P]], channel_multiplier=1))
            pool.wait_ge(m4_ready, 1)
            table("amask", g.affine_select(out=m2, in_=m2, compare_op=ALU.is_ge, fill=NEG, base=0,
                                  pattern=[[0, NT], [-1, P]], channel_multiplier=1))
            with pool.Fori(1, H) as h:
                for j in range(N_MEM):
                    rest(N_MEM * h + j, j % 4)
            for j in range(N_ATT):
                rest(ATT0 + j, j % 3)
            pool.wait_ge(w_split, ATT0 + N_ATT)
            own.step(g.memset(bsp[32:64], 0.0))
            own.step(g.memset(sel[:], 0.0))
            for q in (0, 64):
                own.step(g.affine_select(out=sel[q:q + E], in_=sel[q:q + E], compare_op=ALU.not_equal, fill=1.0, base=0,
                                         pattern=[[-1, E], [0, P]], channel_multiplier=1))
            table("sel", g.affine_select(out=sel[96:P], in_=sel[96:P], compare_op=ALU.not_equal, fill=1.0, base=0,
                                  pattern=[[-1, E], [0, P]], channel_multiplier=1))
            own.settle()
            with pool.Fori(1, H) as h:
                for j in range(N_ATT):
                    rest(ATT0 + N_ATT * h + j, j % 3)
            with pool.Fori(0, KD // 2) as b:
                for u in range(2):
                    for j in range(4):
                        rest(MRG0 + N_MRG * b + 4 * u + j, j, H if j == 2 else KD)
            pool.wait_ge(mix_mm, 2 * NT)
            own.step(g.iota(iota_slot[:], pattern=[[1, P]], base=0, channel_multiplier=0, allow_small_or_imprecise_dtypes=True))
            own.step(g.memset(xg[:], 0.0))
            own.step(g.iota(iota_e[:], pattern=[[1, E]], base=0, channel_multiplier=0, allow_small_or_imprecise_dtypes=True))
            own.step(g.iota(iota_k[:], pattern=[[1, TOP_K]], base=0, channel_multiplier=0, allow_small_or_imprecise_dtypes=True))
            own.step(g.iota(tokf[:, 0, :], pattern=[[P, NT]], base=-ABSENT, channel_multiplier=1,
                            allow_small_or_imprecise_dtypes=True))
            own.step(g.iota(tokf[:, 1, :], pattern=[[TOP_K * P, NT]], base=-ABSENT, channel_multiplier=TOP_K,
                            allow_small_or_imprecise_dtypes=True))
            own.step(g.memset(tbl[:, E:E + 2, :, 0], -1.0))
            own.step(g.memset(pool_tick[:], 0.0))
            own.step(g.memset(tbl[:, E:E + 2, :, 1:4], 0.0))
            own.step(g.memset(onesb[:], 1.0))
            g.affine_select(out=tri[:], in_=onesb[:], compare_op=ALU.is_gt, fill=0.0, base=0,
                            pattern=[[1, P]], channel_multiplier=-1).then_inc(late_tables, 1)
            pool.wait_ge(tbl_ready, 4)
            for i in range(NT):
                pool.wait_ge(xn_stored[i], DMA)

            def table_of(e, m):
                pool.wait_ge(meta_mm, m)
                g.tensor_copy(te[:], tbl[:, bass.ds(e, 1), :, :].rearrange("p a i v -> p (a i) v")).then_inc(te_ready, 1)

            def gather(e, m, xi):
                pool.wait_ge(meta_ready, 2 * (m + 1))
                pool.wait_ge(gathered, DMA * xi)
                pool.wait_ge(xg_T, 2 * xi)
                own.step(g.tensor_copy(gidx[:], idx_of[:, bass.ds(e, 1), 0]))
                g.tensor_tensor(pool_tick[:], pool_tick[:], pool_tick[:], ALU.mult)
                g.indirect_dma_start(out=xg[:], out_offset=None, in_=xn_rows,
                                     in_offset=bass.IndirectOffsetOnAxis(ap=gidx[:, 0:1], axis=0),
                                     bounds_check=T - 1, oob_is_err=False).then_inc(gathered, DMA)

            def scatter(e, gi):
                pool.wait_ge(y_ready, 2 * (gi + 1))
                pool.wait_ge(y_stored, DMA * gi)
                own.step(g.tensor_copy(sidx[:], idx_of[:, bass.ds(e, 1), 1]))
                g.tensor_tensor(pool_tick[:], pool_tick[:], pool_tick[:], ALU.mult)
                g.indirect_dma_start(out=y_rows, out_offset=bass.IndirectOffsetOnAxis(ap=sidx[:, 0:1], axis=0),
                                     in_=yw[:], in_offset=None,
                                     bounds_check=T * TOP_K - 1, oob_is_err=False).then_inc(y_stored, DMA)

            table_of(0, 0)
            gather(0, 0, 0)
            table_of(1, 1)
            gather(1, 1, 1)
            table_of(2, 2)

            def expert_turn(e):
                gather(e + 1, e + 1, e + 1)
                table_of(e + 2, e + 2)
                scatter(e - 1, e - 1)

            expert_turn(1)
            with pool.Fori(2, E) as e:
                own.begin(e - 2, 2)
                expert_turn(e)
                own.end(E - 2)
            scatter(E - 1, E - 1)
            pool.wait_ge(y_stored, DMA * E)
            with pool.If(many(pool) > 0):
                common, own = own, Chain(pool, pool_over)
                with pool.Fori(1, NT) as b:
                    with pool.Fori(0, E) as e:
                        n = extra(b, e)
                        own.begin(n, 2)
                        table_of(e, E + 2 + n)
                        gather(e, E + 2 + n, E + 1 + n)
                        scatter(e, E + n)
                        pool.wait_ge(y_stored, DMA * (E + 1 + n))
                        own.end((NT - 1) * E)
                own = common
            g.engine_nop().then_inc(all_stored, 1)

        @block.tensor
        def _(pe):
            mm, tr = nc.tensor.matmul, nc.tensor.transpose

            pe.wait_ge(tables, made["ident"])
            pe.wait_ge(vec_in, 4 * DMA)
            tr(ps[:, 7, 0:88], vrow[:, :], ident[0:88, 0:88]).then_inc(vecT_done, 1)
            pe.wait_ge(tables, made["rows"])
            tr(ps[:, 6, 0:1], frow[0:1, 0, :], ident[0:1, 0:1])
            tr(ps[:, 6, 1:2], frow[0:1, 1, :], ident[0:1, 0:1]).then_inc(vecT_done, 1)

            def transpose_rows(xw, ready, used, done, i):
                pe.wait_ge(ready, i + 1)
                for b in range(2):
                    if i >= 2:
                        pe.wait_ge(done, 2 * (i - 2) + b + 1)
                    for k in range(4):
                        last = tr(ps[:, 2 * (i % 2) + b, k * P:(k + 1) * P], xw[:, i % 2, (4 * b + k) * P:(4 * b + k + 1) * P], ident[:])
                    last.then_inc(used, 1)

            for i in range(NT):
                transpose_rows(xw, xw_ready, xw_used, xnT_ready, i)
            def product(out, wh, wl, rh, rl, nk):
                for k in range(nk):
                    mm(out, wh(k), rh[:, k, :], start=(k == 0), stop=False)
                    mm(out, wh(k), rl[:, k, :], start=False, stop=False)
                    last = mm(out, wl(k), rh[:, k, :], start=False, stop=(k == nk - 1))
                return last

            pe.wait_ge(wif_split, 1)
            pe.wait_ge(xnT_ready, 2 * NT)
            product(ps[0:64, 4, :], lambda k: wifh[:, k, :], lambda k: wifl[:, k, :], xh, xl, KD).then_inc(gate_mm, 1)

            def project(n, slot, bank, rh=xh, rl=xl, nk=KD):
                pe.wait_ge(w_split, n + 1)
                product(ps[:, bank, :], lambda k: split(slot)[:, 0, k * P:(k + 1) * P], lambda k: split(slot)[:, 1, k * P:(k + 1) * P],
                        rh, rl, nk).then_inc(w_used, 1)

            def mem_tile(h, j):
                n = N_MEM * h + j
                if not isinstance(h, int) or n >= 2:
                    pe.wait_ge(proj_out, n - 1)
                project(n, j % 4, j % 2)

            def mem_gates():
                pe.wait_ge(tables, made["ce"])
                pe.wait_ge(gate_rows, 2)
                for i in range(NT):
                    last = tr(ps[:, 5, i * 64:(i + 1) * 64], ce[:, i * P:(i + 1) * P], ident[0:64, 0:64])
                last.then_inc(gate_T, 1)
                for h in range(H):
                    if h >= 2:
                        pe.wait_ge(nmb_ready, h - 1)
                    mm(ps[:, 6 + h % 2, :], head_sel[:, h, :], gat[0:H, 1, :], start=True, stop=True).then_inc(nmb_mm, 1)

            def mem_core(h):
                pe.wait_ge(proj_out, N_MEM * h + 6)
                pe.wait_ge(mem_ready, 2 * h)
                for i in range(NT):
                    for u in range(2):
                        last = tr(ps[:, 2 + i // 2, (i % 2) * MDH + u * P:(i % 2) * MDH + (u + 1) * P],
                                  mvraw[:, u, i * P:(i + 1) * P], ident[:])
                    if i % 2:
                        last.then_inc(mv_T, 1)
                pe.wait_ge(qk_ready, h + 1)
                for j in range(NT):
                    pe.wait_ge(at_ready, NT * h + j - 1 if j > 0 else NT * h)
                    for c in range(2):
                        last = mm(ps[:, 4 + j % 2, j * P:T], qkf[:, 2 + c, j * P:(j + 1) * P], qkf[:, c, j * P:T],
                                  start=(c == 0), stop=(c == 1))
                    last.then_inc(at_mm, 1)
                pe.wait_ge(vN_ready, 2 * (h + 1))
                for i in range(NT):
                    pe.wait_ge(at_ready, NT * h + i + 1)
                    if i >= 2:
                        pe.wait_ge(num_out, NT * h + i - 1)
                    for j in range(i + 1):
                        last = mm(ps[:, 6 + i % 2, 0:VN], AT[:, j, i * P:(i + 1) * P], vN[:, j, :], start=(j == 0), stop=(j == i))
                    last.then_inc(num_mm, 1)
                for i in range(NT):
                    pe.wait_ge(hn_ready, NT * h + i + 1)
                    for c in range(2):
                        last = tr(ps[:, 2 + c, i * P:(i + 1) * P], hh[:, i, c * P:(c + 1) * P], ident[:])
                last.then_inc(hn_T, 1)

            for j in range(4):
                mem_tile(0, j)
            mem_gates()
            for j in range(4, N_MEM):
                mem_tile(0, j)
            pe.wait_ge(nmb_ready, H)
            pe.wait_ge(gate_cols, 2)
            mem_core(0)
            with pe.Fori(1, H) as h:
                for j in range(N_MEM):
                    mem_tile(h, j)
                mem_core(h)

            def att_head(h):
                for j in range(N_ATT):
                    pe.wait_ge(proj_out, ATT0 + N_ATT * h + j - (1 if j else 0))
                    if j < 2:
                        pe.wait_ge(att_ready, NT * h)
                    project(ATT0 + N_ATT * h + j, j % 3, j % 2)
                for g in range(G):
                    pe.wait_ge(proj_out, ATT0 + N_ATT * h + 2 * G + g + 1)
                    for i in range(NT):
                        src = avraw[:, g, i * P:(i + 1) * P] if g == 0 else avraw[:, g, i:T:NT]
                        last = tr(ps[:, (6, 7, 5)[g], i * P:(i + 1) * P], src, ident[:])
                    last.then_inc(av_T, 1)

                def scores(r):
                    b = 2 + 2 * (r % 2)
                    if r >= 2:
                        pe.wait_ge(smax_ready, NT * h + r - 1)
                    q = lambda g: qk[:, g, r:T:NT]
                    mm(ps[:, b, :], q(0), qk[:, G, :], start=True, stop=True)
                    mm(ps[:, b + 1, 0:P], q(1), qk[:, G + 1, r:T:NT], start=True, stop=True)
                    mm(ps[:, b + 1, P:2 * P], q(2), qk[:, G + 2, r:T:NT], start=True, stop=True).then_inc(s_mm, 1)

                pe.wait_ge(rot_ready, h + 1)
                scores(0)
                pe.wait_ge(vh_ready, G * (h + 1))
                scores(1)
                for r in range(NT):
                    pe.wait_ge(pr_ready, NT * h + r + 1)
                    pe.wait_ge(pT_dve, NT * h + r)
                    pe.wait_ge(pT_act, NT * h + r)
                    for m in range(6):
                        last = tr(ps[:, 6 + m // 4, (m % 4) * P:(m % 4 + 1) * P], pr[:, r % 2, m * P:(m + 1) * P], ident[:])
                        if m == 3:
                            last.then_inc(pr_T, 1)
                    last.then_inc(pr_T, 1)
                    if r + 2 < NT:
                        scores(r + 2)
                    pe.wait_ge(pT_act, NT * h + r + 1)
                    pe.wait_ge(pT_dve, NT * h + r + 1)
                    if r >= 2:
                        pe.wait_ge(att_ready, NT * h + r - 1)
                    for m in range(6):
                        v = vh[:, 0, m, :] if m < NT else vh[:, m - NT + 1, r, :]
                        last = mm(ps[:, r % 2, 0:P], v, pT[:, m, :], start=(m == 0), stop=(m == 5))
                    last.then_inc(pv_mm, 1)

            att_head(0)
            with pe.Fori(1, H) as h:
                att_head(h)

            def merge_step(b):
                for u in range(2):
                    for j, (rh, rl, nk) in enumerate(((xh, xl, KD), (xh, xl, KD), (attR, attL, H), (memR, memL, KD))):
                        if j < 2:
                            pe.wait_ge(sg_ready, 4 * b)
                        else:
                            pe.wait_ge(merged, 2 * b)
                            pe.wait_ge(am_split, 1 if j == 2 else 3)
                        project(MRG0 + N_MRG * b + 4 * u + j, j, 4 * u + j, rh, rl, nk)

            pe.wait_ge(att_ready, NT * H)
            pe.wait_ge(mem_ready, 2 * H)
            merge_step(0)
            with pe.Fori(1, KD // 2) as b:
                merge_step(b)
            pe.wait_ge(merged, KD)
            for i in range(NT):
                for n in range(2):
                    if i >= 2:
                        pe.wait_ge(h_ready, 2 * (i - 2) + n + 1)
                    for k in range(KD):
                        if i == 0 and n == 0:
                            pe.wait_ge(wmix_in[k], DMA)
                        last = mm(ps[:, 4 + 2 * (i % 2) + n, :], mergedT[:, k, i * P:(i + 1) * P], (wmix0[:, k, n * BANK:(n + 1) * BANK] if k < KD - 2 else wmix1[:, k - KD + 2, n * BANK:(n + 1) * BANK]),
                                  start=(k == 0), stop=(k == KD - 1))
                    last.then_inc(mix_mm, 1)

            for i in range(NT):
                transpose_rows(xw2, hw_ready, hw_used, xn2T_ready, i)
            pe.wait_ge(router_in, 3 * DMA)
            for i in range(NT):
                pe.wait_ge(xn2T_ready, 2 * (i + 1))
                if i == 0:
                    pe.wait_ge(h_ready, 2 * NT)
                for k in range(KD):
                    last = mm(ps[:, 4, i * E:(i + 1) * E], xn2T[:, k, i * P:(i + 1) * P], wr[:, k, :], start=(k == 0), stop=(k == KD - 1))
                last.then_inc(lg_mm, 1)
            pe.wait_ge(late_tables, 1)
            pe.wait_ge(memb_ready, 1)
            for i in range(NT):
                for j in range(i):
                    mm(ps[:, 5, i * E:(i + 1) * E], onesb[:], memb[:, j, :], start=(j == 0), stop=False)
                mm(ps[:, 5, i * E:(i + 1) * E], tri[:], memb[:, i, :], start=(i == 0), stop=True)
            for j in range(NT):
                last = mm(ps[:, 5, NT * E:(NT + 1) * E], onesb[:], memb[:, j, :], start=(j == 0), stop=(j == NT - 1))
            last.then_inc(pos_mm, 1)

            GUB, DNB, TB0, TB1 = 0, 4, 7, 6

            def slots_of(m):
                pe.wait_ge(sel_ready, NT * (m + 1))
                for i in range(NT):
                    last = mm(ps[:, TB1, 0:4], sels[:, i, :], te[:, i, :], start=(i == 0), stop=(i == NT - 1))
                last.then_inc(meta_mm, 1)

            def rows_T(m, xi):
                pe.wait_ge(gathered, DMA * (xi + 1))
                for b, bank in enumerate((TB0, TB1)):
                    if b == 1:
                        pe.wait_ge(meta_ready, 2 * (m + 1))
                    for k in range(4):
                        last = tr(ps[:, bank, k * P:(k + 1) * P], xg[:, (4 * b + k) * P:(4 * b + k + 1) * P], ident[:])
                    last.then_inc(xg_T, 1)

            def gate_up(e, xi, gi):
                pe.wait_ge(xT_ready, 2 * (xi + 1))
                pe.wait_ge(up_read, gi)
                for n in range(4):
                    mm(ps[:, GUB + n, :], sel[:, bass.ds(e, 1), :].rearrange("p a s -> p (a s)"), bsp[:, n * BANK:(n + 1) * BANK],
                       start=True, stop=False)
                for k in range(KD):
                    pe.wait_ge(gu_split, KD * gi + k + 1)
                    for n in range(4):
                        cols = slice(n * BANK, (n + 1) * BANK)
                        mm(ps[:, GUB + n, :], xTh[:, k, :], guh[k % 4][:, cols], start=False, stop=False)
                        mm(ps[:, GUB + n, :], xTh[:, k, :], gul[:, k, cols], start=False, stop=False)
                    for n in range(4):
                        last = mm(ps[:, GUB + n, :], xTl[:, k, :], guh[k % 4][:, n * BANK:(n + 1) * BANK], start=False, stop=(k == KD - 1))
                    last.then_inc(gu_used, 1)

            def down(e, gi):
                pe.wait_ge(actT_ready, 2 * (gi + 1))
                pe.wait_ge(y_ready, 2 * gi)
                for n in range(2):
                    mm(ps[:, DNB + n, :], sel[:, bass.ds(e, 1), :].rearrange("p a s -> p (a s)"),
                       bsp[:, F2 + n * BANK:F2 + (n + 1) * BANK], start=True, stop=False)
                for k in range(KD):
                    if k % 2 == 0:
                        pe.wait_ge(dn_in[k // 2], DMA * (gi + 1))
                    for n in range(2):
                        last = mm(ps[:, DNB + n, :], actT[:, k, :], dnw[:, k, n * BANK:(n + 1) * BANK], start=False, stop=(k == KD - 1))
                    if k % 2:
                        last.then_inc(dn_used, 1)

            def act_rows_T(gi, xi):
                pe.wait_ge(act_ready, gi + 1)
                pe.wait_ge(xT_ready, 2 * (xi + 1))
                for b, bank in enumerate((TB0, TB1)):
                    for k in range(4):
                        last = tr(ps[:, bank, k * P:(k + 1) * P], act[:, (4 * b + k) * P:(4 * b + k + 1) * P], ident[:])
                    last.then_inc(act_T, 1)

            pe.wait_ge(bias_ready, 1)
            slots_of(0)
            rows_T(0, 0)
            pe.wait_ge(xT_ready, 2)
            slots_of(1)
            gate_up(0, 0, 0)
            pe.wait_ge(meta_ready, 4)
            slots_of(2)
            rows_T(2, 1)
            act_rows_T(0, 1)

            def expert_turn(e):
                gate_up(e, e, e)
                pe.wait_ge(actT_ready, 2 * e)
                slots_of(e + 2)
                rows_T(e + 2, e + 1)
                down(e - 1, e - 1)
                act_rows_T(e, e + 1)

            expert_turn(1)
            with pe.Fori(2, E) as e:
                expert_turn(e)
            down(E - 1, E - 1)
            with pe.If(many(pe) > 0):
                with pe.Fori(1, NT) as b:
                    with pe.Fori(0, E) as e:
                        n = extra(b, e)
                        slots_of(E + 2 + n)
                        rows_T(E + 2 + n, E + 1 + n)
                        gate_up(e, E + 1 + n, E + n)
                        act_rows_T(E + n, E + 1 + n)
                        down(e, E + n)

        @block.scalar
        def _(sc):
            own = Chain(sc, act_step)
            a = nc.scalar.activation

            def squares(i, ready, count, n, done):
                sc.wait_ge(ready, count)
                a(ps[:, 0:2, :].rearrange("p b n -> p (b n)"), hres[:, i, :], ACT.Square, accum_out=ssq[:, n, i:i + 1]).then_inc(done, 1)

            def std(n, ready, done):
                sc.wait_ge(ready, 1)
                a(ssq[:, n, :], ssq[:, n, :], ACT.Sqrt).then_inc(done, 1)

            for i in range(NT):
                if i:
                    sc.wait_ge(x_square, i)
                squares(i, x_in[i], DMA, 0, x_square)
            std(0, x_var, x_std)
            sc.wait_ge(wif_in, 2 * DMA)
            nc.scalar.copy(wifh[:], wif[:]).then_inc(wif_round, 1)
            for n in range(2 * NT):
                sc.wait_ge(xt_ready, n + 1)
                nc.scalar.copy(xh[:, 4 * (n % 2):4 * (n % 2) + 4, (n // 2) * P:(n // 2 + 1) * P],
                               xt[:, n % 2, :].rearrange("p (k c) -> p k c", k=4)).then_inc(xh_ready, 1)

            def round_tile(slot, uses):
                sc.wait_ge(w_in_slot[slot], DMA * uses)
                nc.scalar.copy(split(slot)[:, 0, :], wraw[:, slot, :]).then_inc(rounded, 1)

            def next_of_mem(h, j):
                j = j + 3
                if j < N_MEM:
                    round_tile(j % 4, 2 * h + j // 4 + 1)
                else:
                    round_tile(j - N_MEM, 2 * h + 3)

            def next_of_att(h, j):
                j = j + 3
                if j < N_ATT:
                    round_tile(j % 3, 2 * H + 3 * h + j // 3 + 1)
                else:
                    round_tile(j - N_ATT, 2 * H + 3 * h + 4)

            def next_of_merge(b, t, last):
                t = t + 3
                if t >= N_MRG and last:
                    return
                if t >= N_MRG:
                    b, t = b + 1, t - N_MRG
                s = t % 4
                round_tile(s, (2 * H if s == 3 else 5 * H) + 2 * b + t // 4 + 1)

            round_tile(0, 1)
            round_tile(1, 1)
            sc.wait_ge(xw_ready, NT)
            round_tile(2, 1)
            sc.wait_ge(angle_ready, 2)
            a(rcos[:], ang[:, 1, :], ACT.Sin).then_inc(sines_ready, 1)
            a(rsin[:], ang[:, 2, :], ACT.Sin).then_inc(sines_ready, 1)
            sc.wait_ge(gate_abs, 1)
            own.step(a(gat[0:H, 2, :], gat[0:H, 2, :], ACT.Exp))
            a(gat[0:H, 2, :], gat[0:H, 2, :], ACT.Ln, bias=1.0).then_inc(gate_ln, 1)

            def mem_head(h, first=False):
                sc.wait_ge(conv_ready, 4 * h)
                for j in range(4):
                    sc.wait_ge(w_used, N_MEM * h + j + 1)
                    nc.scalar.copy(raw[:, j, TAPS - 1:], ps[:, j % 2, :]).then_inc(proj_out, 1)
                    next_of_mem(h, j)
                if first:
                    sc.wait_ge(gate_cols, 1)
                    a(expE[:], ceT[:, :, 32:32 + H], ACT.Exp).then_inc(gate_cols, 1)
                    sc.wait_ge(sines_done, 1)
                    for n in range(H):
                        sc.wait_ge(nmb_mm, n + 1)
                        nc.scalar.copy(nmb[:, n, :], ps[:, 6 + n % 2, :]).then_inc(nmb_ready, 1)
                for u in range(2):
                    sc.wait_ge(w_used, N_MEM * h + 4 + u + 1)
                    sc.wait_ge(mv_T, 2 * h)
                    nc.scalar.copy(mvraw[:, u, :], ps[:, u, :]).then_inc(proj_out, 1)
                    next_of_mem(h, 4 + u)
                sc.wait_ge(conv_ready, 4 * (h + 1))
                sc.wait_ge(at_mm, NT * h)
                a(qkf[:], cv[:], ACT.Silu).then_inc(qk_ready, 1)
                for u in range(2):
                    sc.wait_ge(w_used, N_MEM * h + 6 + u + 1)
                    sc.wait_ge(mem_ready, 2 * h)
                    a(sgo[:, u, :], ps[:, u, :], ACT.Sigmoid).then_inc(proj_out, 1)
                    next_of_mem(h, 6 + u)
                sc.wait_ge(cols_ready, 3 * (h + 1))
                sc.wait_ge(at_ready, NT * h)
                for j in range(NT):
                    a(wexp[:, j, j * P:(j + 1) * P], nmd[:, j * P:(j + 1) * P], ACT.Exp, bias=ch[:, j:j + 1]).then_inc(wexp_ready, 1)
                    if j < NT - 1:
                        a(wexp[:, j, (j + 1) * P:T], nmb[:, bass.ds(h, 1), (j + 1) * P:T].rearrange("p a t -> p (a t)"),
                          ACT.Exp, bias=ch[:, j:j + 1]).then_inc(wexp_ready, 1)
                for b in range(2):
                    sc.wait_ge(mv_T, 2 * h + b + 1)
                    sc.wait_ge(num_mm, NT * h)
                    nc.scalar.copy(vN[:, 2 * b:2 * b + 2, 0:MDH], ps[:, 2 + b, :].rearrange("p (i c) -> p i c", i=2)).then_inc(vN_ready, 1)
                sc.wait_ge(hvar_ready, h + 1)
                a(mrs[:, 0, :], mrs[:, 0, :], ACT.Sqrt).then_inc(hstd_ready, 1)

            mem_head(0, first=True)
            with sc.Fori(1, H) as h:
                mem_head(h)

            def att_head(h):
                for j in range(2 * G):
                    sc.wait_ge(w_used, ATT0 + N_ATT * h + j + 1)
                    nc.scalar.copy(qk[:, j, :], ps[:, j % 2, :]).then_inc(proj_out, 1)
                    next_of_att(h, j)
                for g in range(G):
                    sc.wait_ge(w_used, ATT0 + N_ATT * h + 2 * G + g + 1)
                    nc.scalar.copy(avraw[:, g, :], ps[:, g % 2, :]).then_inc(proj_out, 1)
                    next_of_att(h, 2 * G + g)
                for g in range(G):
                    sc.wait_ge(av_T, G * h + g + 1)
                    nc.scalar.copy(vh[:, g, :, :].rearrange("p i c -> p (i c)"), ps[:, (6, 7, 5)[g], :]).then_inc(vh_ready, 1)
                def weights(r):
                    sc.wait_ge(smax_ready, NT * h + r + 1)
                    a(pr[:, r % 2, :], sm[:, r % 2, :], ACT.Exp, bias=smax[:, r % 2, 1:2], scale=QK_SCALE,
                      accum_out=smax[:, r % 2, 2:3]).then_inc(exp_ready, 1)

                weights(0)
                for r in range(NT):
                    if r + 1 < NT:
                        weights(r + 1)
                    sc.wait_ge(pr_T, 2 * (NT * h + r) + 1)
                    nc.scalar.copy(pT[:, 0:4, :].rearrange("p m c -> p (m c)"), ps[:, 6, :]).then_inc(pT_act, 1)

            att_head(0)
            with sc.Fori(1, H) as h:
                att_head(h)

            def merge_step(b, last=False):
                for u in range(2):
                    for j in range(2):
                        sc.wait_ge(w_used, MRG0 + N_MRG * b + 4 * u + j + 1)
                        sc.wait_ge(merged, 2 * b)
                        a(sgm[:, u, j, :], ps[:, 4 * u + j, :], ACT.Sigmoid).then_inc(sg_ready, 1)
                        next_of_merge(b, 4 * u + j, last)
                    for j in range(2, 4):
                        sc.wait_ge(w_used, MRG0 + N_MRG * b + 4 * u + j)
                        next_of_merge(b, 4 * u + j, last)

            sc.wait_ge(att_ready, NT * H)
            nc.scalar.copy(attR[:], attT[:]).then_inc(am_round, 1)
            for c in range(2):
                nc.scalar.copy(memR[:, 4 * c:4 * c + 4, :], memT[:, 4 * c:4 * c + 4, :]).then_inc(am_round, 1)
            merge_step(0)
            with sc.Fori(1, KD // 2 - 1) as b:
                merge_step(b)
            merge_step(KD // 2 - 1, last=True)

            for i in range(NT):
                if i:
                    sc.wait_ge(h_square, i)
                squares(i, h_ready, 2 * (i + 1), 1, h_square)
            std(1, h_var, h_std)
            sc.wait_ge(top_ready, 1)
            a(gk[:], gk[:], ACT.Exp).then_inc(gk_ready, 1)

            def round_chunk(gi, k):
                sc.wait_ge(gu_in[k], DMA * (gi + 1))
                if not isinstance(gi, int) or gi or k >= 4:
                    sc.wait_ge(gu_used, KD * gi + k - 3)
                nc.scalar.copy(guh[k % 4][:], guw[:, k, :]).then_inc(gu_rounded, 1)

            def rows(xi):
                for b, bank in enumerate((7, 6)):
                    sc.wait_ge(xg_T, 2 * xi + b + 1)
                    nc.scalar.copy(xTh[:, 4 * b:4 * b + 4, :].rearrange("p k c -> p (k c)"), ps[:, bank, :]).then_inc(xTh_ready, 1)

            def sigmoid(gi):
                sc.wait_ge(gt_ready, gi + 1)
                a(sg[:], gt[:], ACT.Sigmoid, scale=SWIGLU_ALPHA).then_inc(sg_ready2, 1)

            def weighted(e, gi):
                sc.wait_ge(y_ready, 2 * gi)
                own.step(nc.scalar.copy(gcur[:], gate_of[:, bass.ds(e, 1)]))
                sc.wait_ge(dn_used, (KD // 2) * (gi + 1))
                sc.wait_ge(y_stored, DMA * gi)
                for n in range(2):
                    nc.scalar.mul(yw[:, n * BANK:(n + 1) * BANK], ps[:, 4 + n, :], gcur[:, 0:1]).then_inc(y_ready, 1)

            def act_rows(gi):
                for b, bank in enumerate((7, 6)):
                    sc.wait_ge(act_T, 2 * gi + b + 1)
                    nc.scalar.copy(actT[:, 4 * b:4 * b + 4, :].rearrange("p k c -> p (k c)"), ps[:, bank, :]).then_inc(actT_ready, 1)

            def expert_turn(e, first=False, last=False):
                for k in range(4, KD):
                    round_chunk(e, k)
                if not last:
                    for k in range(3):
                        round_chunk(e + 1, k)
                sigmoid(e)
                rows(e + 1)
                if not last:
                    round_chunk(e + 1, 3)
                if not first:
                    weighted(e - 1, e - 1)
                act_rows(e)

            sc.wait_ge(lg_mm, NT)
            for i in range(NT):
                sc.wait_ge(xn_stored[i], DMA)
            for k in range(4):
                round_chunk(0, k)
            rows(0)
            expert_turn(0, first=True)
            expert_turn(1)
            with sc.Fori(2, E - 1) as e:
                own.begin(e - 2, 1)
                expert_turn(e)
                own.end(E - 3)
            expert_turn(E - 1, last=True)
            weighted(E - 1, E - 1)
            with sc.If(many(sc) > 0):
                common, own = own, Chain(sc, act_over)
                with sc.Fori(1, NT) as b:
                    with sc.Fori(0, E) as e:
                        n = extra(b, e)
                        own.begin(n, 1)
                        rows(E + 1 + n)
                        for k in range(KD):
                            round_chunk(E + n, k)
                        sigmoid(E + n)
                        act_rows(E + n)
                        weighted(e, E + n)
                        own.end((NT - 1) * E)
                own = common
            for i in range(NT):
                if i:
                    sc.wait_ge(f_square, i)
                squares(i, f_sum, i + 1, 2, f_square)
            std(2, f_var, f_std)

        @block.vector
        def _(dve):
            own = Chain(dve, dve_step)
            v = nc.vector
            tt, ts, stt = v.tensor_tensor, v.tensor_scalar, v.scalar_tensor_tensor

            def variance(n, ready, done):
                dve.wait_ge(ready, NT)
                ts(ssq[:, n, :], ssq[:, n, :], 1.0 / D, RMS_EPS, ALU.mult, ALU.add).then_inc(done, 1)

            dve.wait_ge(vecT_done, 2)
            own.mark(v.tensor_copy(vecT[:], ps[:, 7, 0:88]))
            own.mark(v.tensor_copy(fcol[:], ps[:, 6, 0:2]))
            own.settle()
            variance(0, x_square, x_var)
            dve.wait_ge(x_std, 1)
            own.step(v.reciprocal(rstd[:, 0, :], ssq[:, 0, :]))
            four = lambda t: t.rearrange("p (k c) -> p k c", k=4)

            def x_rest(n):
                dve.wait_ge(xh_ready, n + 1)
                at = (slice(None), slice(4 * (n % 2), 4 * (n % 2) + 4), slice((n // 2) * P, (n // 2 + 1) * P))
                tt(xl[at], four(xt[:, n % 2, :]), xh[at], ALU.subtract).then_inc(xnT_ready, 1)

            for i in range(NT + 1):
                if i >= 2:
                    dve.wait_ge(xw_used, 2 * (i - 1))
                if i < NT:
                    ts(xw[:, i % 2, :], hres[:, i, :], rstd[:, 0, i:i + 1], None, ALU.mult).then_inc(xw_ready, 1)
                if i == 0:
                    continue
                for n in (2 * i - 2, 2 * i - 1):
                    dve.wait_ge(xw_used, n + 1)
                    if n >= 2:
                        dve.wait_ge(xnT_ready, n - 1)
                    tt(four(xt[:, n % 2, :]), ps[:, n % 4, :].rearrange("p (k c) -> p k c", k=4),
                       vecT[:, GMIX + 4 * (n % 2):GMIX + 4 * (n % 2) + 4].unsqueeze(2).to_broadcast([P, 4, P]), ALU.mult).then_inc(xt_ready, 1)
                    if n == 0:
                        dve.wait_ge(wif_round, 1)
                        tt(wifl[:], wif[:], wifh[:], ALU.subtract).then_inc(wif_split, 1)
                    else:
                        x_rest(n - 1)
            x_rest(2 * NT - 1)
            TWO_PI = 2.0 * float(np.pi)
            C1 = 6.28125
            C2 = float(np.float32(np.round((TWO_PI - C1) * 2 ** 21) / 2 ** 21))
            C3 = TWO_PI - C1 - C2
            MAGIC = 1.5 * 2 ** 23
            TOP = 3.1415925
            dve.wait_ge(pos_in, DMA)
            own.step(ts(ang[:, 0, :], post[:], fcol[0:ROT, 0:1], None, ALU.mult))
            turns = rcos
            for n, (shift, offset) in enumerate(((0.25, float(np.pi) / 2), (0.0, 0.0))):
                a1 = ang[:, n + 1, :]
                own.step(ts(turns[:], ang[:, 0, :], 1.0 / TWO_PI, shift, ALU.mult, ALU.add))
                own.step(ts(turns[:], turns[:], MAGIC, None, ALU.add))
                own.step(ts(turns[:], turns[:], MAGIC, None, ALU.subtract))
                own.step(stt(a1, turns[:], -C1, ang[:, 0, :], ALU.mult, ALU.add))
                own.step(stt(a1, turns[:], -C2, a1, ALU.mult, ALU.add))
                own.step(stt(a1, turns[:], -C3, a1, ALU.mult, ALU.add))
                own.step(ts(a1, a1, offset, TOP, ALU.add, ALU.min))
                ts(a1, a1, -TOP, None, ALU.max).then_inc(angle_ready, 1)

            R = slice(0, H)
            R2 = slice(32, 32 + H)
            dve.wait_ge(gate_mm, 1)
            dve.wait_ge(bif_in, 2 * DMA)
            own.mark(ts(gat[R, 0, :], ps[R, 4, :], bcol[R, 0:1], None, ALU.add))
            own.step(ts(gat[R, 1, :], ps[R2, 4, :], bcol[R2, 0:1], None, ALU.add))
            stt(gat[R, 2, :], gat[R, 1, :], -1.0, gat[R, 1, :], ALU.mult, ALU.min).then_inc(gate_abs, 1)
            dve.wait_ge(gate_ln, 1)
            own.step(stt(gat[R, 1, :], gat[R, 1, :], 0.0, gat[R, 2, :], ALU.min, ALU.subtract))
            own.step(v.tensor_tensor_scan(gat[R, 2, :], ones_row[:], gat[R, 1, :], 0.0, ALU.mult, ALU.add))
            dve.wait_ge(tables, made["ce"])
            own.step(tt(ce[R, :], gat[R, 0, :], gat[R, 2, :], ALU.subtract))
            own.step(v.tensor_tensor_scan(gat[R, 0, :], ones_row[:], ce[R, :], 0.0, ALU.mult, ALU.max))
            stt(ce[R2, :], gat[R, 2, :], -1.0, gat[R, 0, :], ALU.mult, ALU.subtract).then_inc(gate_rows, 1)
            ts(gat[R, 1, :], gat[R, 0, :], -1.0, None, ALU.mult).then_inc(gate_rows, 1)
            dve.wait_ge(sines_ready, 2)
            ts(rsin[:], rsin[:], fcol[0:ROT, 1:2], None, ALU.mult).then_inc(sines_done, 1)

            dve.wait_ge(m4_made, 1)
            own.step(ts(m4[:], m4[:], 3, None, ALU.bitwise_and))
            ts(amask[:, :, T + P:SC], m4[:].unsqueeze(1).to_broadcast([P, NT, P]), NEG, None, ALU.mult).then_inc(m4_ready, 1)
            WEXPS = 2 * NT - 1

            def mem_head(h, first=False):
                dve.wait_ge(wexp_ready, WEXPS * h)
                dve.wait_ge(mem_ready, 2 * h)
                cols = vecT[:, 0:GMIX].rearrange("p (t c) -> p t c", t=TAPS)
                own.mark(v.tensor_copy(cwh[:, :, 0:2], cols[:, :, bass.ds(2 * h, 2)]))
                own.mark(v.tensor_copy(cwh[:, :, 2:4], cols[:, :, bass.ds(KD + 2 * h, 2)]))
                own.mark(v.tensor_copy(gmh[:], vecT[:, bass.ds(GMEM + 2 * h, 2)]))
                own.settle()
                dve.wait_ge(qk_ready, h)
                for j in range(4):
                    dve.wait_ge(proj_out, N_MEM * h + j + 1)
                    own.step(ts(cv[:, j, :], raw[:, j, 0:T], cwh[:, 0, j:j + 1], None, ALU.mult))
                    for t in range(1, TAPS):
                        ins = stt(cv[:, j, :], raw[:, j, t:t + T], cwh[:, t, j:j + 1], cv[:, j, :], ALU.mult, ALU.add)
                        if t < TAPS - 1:
                            own.step(ins)
                        else:
                            ins.then_inc(conv_ready, 1)
                if first:
                    dve.wait_ge(gate_T, 1)
                    v.tensor_copy(ceT[:].rearrange("p i c -> p (i c)"), ps[:, 5, 0:NT * 64]).then_inc(gate_cols, 1)
                    dve.wait_ge(gate_cols, 2)
                    dve.wait_ge(nmb_ready, H)
                    dve.wait_ge(tables, made["cmask"])
                v.tensor_copy(ch[:], ceT[:, :, bass.ds(h, 1)].rearrange("p i a -> p (i a)")).then_inc(cols_ready, 1)
                v.tensor_copy(eh[:], expE[:, :, bass.ds(h, 1)].rearrange("p i a -> p (i a)")).then_inc(cols_ready, 1)
                tt(nmd[:].rearrange("p (i t) -> p i t", i=NT), nmb[:, bass.ds(h, 1), :].rearrange("p a (i t) -> p (a i) t", i=NT),
                   cmask[:].unsqueeze(1).to_broadcast([P, NT, P]), ALU.add).then_inc(cols_ready, 1)
                dve.wait_ge(cols_ready, 3 * (h + 1))
                dve.wait_ge(wexp_ready, WEXPS * (h + 1))
                for j in range(NT):
                    dve.wait_ge(at_mm, NT * h + j + 1)
                    stt(AT[:, j, j * P:T], ps[:, 4 + j % 2, j * P:T], MK_SCALE, wexp[:, j, j * P:T],
                        ALU.mult, ALU.mult).then_inc(at_ready, 1)
                for i in range(NT):
                    dve.wait_ge(num_mm, NT * h + i + 1)
                    num = ps[:, 6 + i % 2, :]
                    own.step(ts(den[:, 0, i:i + 1], num[:, MDH:MDH + 1], eh[:, i:i + 1], None, ALU.max))
                    own.step(stt(den[:, 0, i:i + 1], num[:, MDH:MDH + 1], -1.0, den[:, 0, i:i + 1], ALU.mult, ALU.max))
                    own.step(v.reciprocal(den[:, 1, i:i + 1], den[:, 0, i:i + 1]))
                    ts(hh[:, i, :], num[:, 0:MDH], den[:, 1, i:i + 1], None, ALU.mult).then_inc(num_out, 1)
                    dve.wait_ge(num_out, NT * h + i + 1)
                    own.mark(v.bn_stats(bst[:, i, :], hh[:, i, :]))
                own.settle()
                v.memset(mrs[:], 0.0)
                for i in range(NT):
                    own.mark(v.bn_aggr(mv[:, i, :], bst[:, i, :]))
                own.settle()
                ts(mrs[:, 0, :], mv[:, :, 1], LN_EPS, None, ALU.add).then_inc(hvar_ready, 1)
                dve.wait_ge(hstd_ready, h + 1)
                own.step(v.reciprocal(mrs[:, 1, :], mrs[:, 0, :]))
                for i in range(NT):
                    ts(hh[:, i, :], hh[:, i, :], mv[:, i, 0:1], mrs[:, 1, i:i + 1], ALU.subtract, ALU.mult).then_inc(hn_ready, 1)
                dve.wait_ge(hn_T, h + 1)
                for c in range(2):
                    stt(memT[:, bass.ds(2 * h + c, 1), :].rearrange("p a t -> p (a t)"), ps[:, 2 + c, :], gmh[:, c:c + 1], sgo[:, c, :],
                        ALU.mult, ALU.mult).then_inc(mem_ready, 1)

            own.begin(0, 36)
            mem_head(0, first=True)
            own.end(1)
            with dve.Fori(1, H) as h:
                own.begin(h - 1, 36)
                mem_head(h)
                own.end(H - 1)

            def att_head(h):
                dve.wait_ge(proj_out, ATT0 + N_ATT * h + 2 * G)
                swap = [(i + HALF) % ROT for i in range(ROT)]
                rows = qk[0:ROT, :, :]
                flat = lambda t: t.rearrange("p g t -> p (g t)")
                v.memset(tick[:], 0.0)
                own.step(v.stream_shuffle(flat(rs[:]), flat(rows), swap))
                own.mark(tt(rs[:], rs[:], rsin[:].unsqueeze(1).to_broadcast([ROT, 2 * G, T]), ALU.mult))
                own.step(tt(rows, rows, rcos[:].unsqueeze(1).to_broadcast([ROT, 2 * G, T]), ALU.mult))
                tt(rows, rows, rs[:], ALU.add).then_inc(rot_ready, 1)

                def masked(r):
                    dve.wait_ge(s_mm, NT * h + r + 1)
                    b = 2 + 2 * (r % 2)
                    v.memset(tick[:], 0.0)
                    own.step(v.tensor_tensor_reduce(out=sm[:, r % 2, :], in0=ps[:, b:b + 2, :].rearrange("p b t -> p (b t)")[:, 0:SC],
                                                    in1=amask[:, r, :], scale=1.0, scalar=NEG, op0=ALU.add, op1=ALU.max,
                                                    accum_out=smax[:, r % 2, 0:1]))
                    ts(smax[:, r % 2, 1:2], smax[:, r % 2, 0:1], -QK_SCALE, None, ALU.mult).then_inc(smax_ready, 1)

                def weights(r):
                    dve.wait_ge(exp_ready, NT * h + r + 1)
                    own.step(v.reciprocal(smax[:, r % 2, 3:4], smax[:, r % 2, 2:3]))
                    ts(pr[:, r % 2, :], pr[:, r % 2, :], smax[:, r % 2, 3:4], None, ALU.mult).then_inc(pr_ready, 1)

                masked(0)
                masked(1)
                weights(0)
                for r in range(NT):
                    if r + 2 < NT:
                        masked(r + 2)
                    dve.wait_ge(pr_T, 2 * (NT * h + r + 1))
                    v.tensor_copy(pT[:, 4:6, :].rearrange("p m c -> p (m c)"), ps[:, 7, 0:2 * P]).then_inc(pT_dve, 1)
                    if r + 1 < NT:
                        weights(r + 1)
                    dve.wait_ge(pv_mm, NT * h + r + 1)
                    v.tensor_copy(attT[:, bass.ds(h, 1), r:T:NT].rearrange("p a t -> p (a t)"), ps[:, r % 2, 0:P]).then_inc(att_ready, 1)

            dve.wait_ge(tables, made["amask"])
            own.begin(0, 11)
            att_head(0)
            own.end(1)
            dve.wait_ge(tables, made["sel"])
            dve.wait_ge(brow_in, 6 * DMA)
            hi, lo = slice(64, P), slice(96, P)
            own.mark(v.tensor_copy(bsp[0:E], brow[0:E]))
            own.step(v.tensor_copy(bsp[hi], brow[hi]))
            own.step(tt(brow[hi], brow[hi], bsp[hi], ALU.subtract))
            own.step(v.tensor_copy(bsp[hi], brow[hi]))
            own.step(tt(brow[lo], brow[lo], bsp[lo], ALU.subtract))
            v.tensor_copy(bsp[lo], brow[lo]).then_inc(bias_ready, 1)
            with dve.Fori(1, H) as h:
                own.begin(h - 1, 11)
                att_head(h)
                own.end(H - 1)

            def merge_step(b):
                for u in range(2):
                    for j in range(2):
                        dve.wait_ge(w_used, MRG0 + N_MRG * b + 4 * u + 2 + j + 1)
                        dve.wait_ge(sg_ready, 4 * b + 2 * u + j + 1)
                        own.mark(tt(mgt[:, u, j, :], ps[:, 4 * u + 2 + j, :], sgm[:, u, j, :], ALU.mult))
                    own.settle()
                    tt(mergedT[:, bass.ds(2 * b + u, 1), :].rearrange("p a t -> p (a t)"), mgt[:, u, 0, :], mgt[:, u, 1, :],
                       ALU.add).then_inc(merged, 1)

            dve.wait_ge(am_round, 1)
            tt(attL[:], attT[:], attR[:], ALU.subtract).then_inc(am_split, 1)
            for c in range(2):
                dve.wait_ge(am_round, c + 2)
                at = (slice(None), slice(4 * c, 4 * c + 4))
                tt(memL[at], memT[at], memR[at], ALU.subtract).then_inc(am_split, 1)
            own.begin(0, 4)
            merge_step(0)
            own.end(1)
            with dve.Fori(1, KD // 2) as b:
                own.begin(b - 1, 4)
                merge_step(b)
                own.end(KD // 2 - 1)
            for i in range(NT):
                for n in range(2):
                    dve.wait_ge(mix_mm, 2 * i + n + 1)
                    dve.wait_ge(x_in[i], 2 * DMA)
                    hn = hres[:, i, n * BANK:(n + 1) * BANK]
                    tt(hn, hn, ps[:, 4 + 2 * (i % 2) + n, :], ALU.add).then_inc(h_ready, 1)

            variance(1, h_square, h_var)
            dve.wait_ge(h_std, 1)
            own.step(v.reciprocal(rstd[:, 1, :], ssq[:, 1, :]))
            dve.wait_ge(router_in, 3 * DMA)
            for i in range(NT + 1):
                if i >= 2:
                    dve.wait_ge(hw_used, 2 * (i - 1))
                    if i < NT:
                        dve.wait_ge(xn_stored[i - 2], DMA)
                if i < NT:
                    stt(xw2[:, i % 2, :], hres[:, i, :], rstd[:, 1, i:i + 1], gffn[:], ALU.mult, ALU.mult).then_inc(hw_ready, 1)
                if i:
                    for n in (2 * i - 2, 2 * i - 1):
                        dve.wait_ge(hw_used, n + 1)
                        v.tensor_copy(xn2T[:, 4 * (n % 2):4 * (n % 2) + 4, (i - 1) * P:i * P],
                                      ps[:, n % 4, :].rearrange("p (k c) -> p k c", k=4)).then_inc(xn2T_ready, 1)
            dve.wait_ge(lg_mm, NT)
            own.step(tt(lg[:], ps[:, 4, 0:NT * E].rearrange("p (i e) -> p i e", i=NT), brt[:].unsqueeze(1).to_broadcast([P, NT, E]), ALU.add))
            for i in range(NT):
                own.step(v.max(v8[:, i, :], lg[:, i, :]))
                own.mark(v.max_index(i8[:, i, :], v8[:, i, :], lg[:, i, :]))
            own.settle()
            own.mark(v.tensor_copy(i8f[:], i8[:]))
            tt(gk[:], v8[:, :, 0:TOP_K], v8[:, :, 0:1].to_broadcast([P, NT, TOP_K]), ALU.subtract).then_inc(top_ready, 1)
            own.settle()
            dve.wait_ge(late_tables, 1)
            full = [P, NT, TOP_K, E]
            own.step(tt(oh, iota_e[:].unsqueeze(1).unsqueeze(1).to_broadcast(full), i8f[:, :, 0:TOP_K].unsqueeze(3).to_broadcast(full),
                        ALU.is_equal))
            over_k = lambda t: t.rearrange("p i k e -> p i e k")
            own.step(v.tensor_reduce(member, over_k(oh), AX.X, ALU.add))
            v.tensor_copy(memb[:], member).then_inc(memb_ready, 1)
            own.step(tt(oht, oh, iota_k[:].unsqueeze(1).unsqueeze(3).to_broadcast(full), ALU.mult))
            own.step(v.tensor_reduce(kth, over_k(oht), AX.X, ALU.add))
            dve.wait_ge(gk_ready, 1)
            own.step(v.tensor_reduce(gs[:, 0, :], gk[:], AX.X, ALU.add))
            own.step(v.reciprocal(gs[:, 1, :], gs[:, 0, :]))
            own.step(tt(gk[:], gk[:], gs[:, 1, :].unsqueeze(2).to_broadcast([P, NT, TOP_K]), ALU.mult))
            own.step(tt(oht, oh, gk[:].unsqueeze(3).to_broadcast(full), ALU.mult))
            own.step(v.tensor_reduce(gte, over_k(oht), AX.X, ALU.add))
            entry = lambda n: tbl[:, 0:E, :, n].rearrange("p e i -> p i e")
            per_tok = lambda n: tokf[:, n, :].unsqueeze(2).to_broadcast([P, NT, E])
            v.tensor_copy(entry(3), gte).then_inc(tbl_ready, 1)
            tt(entry(1), member, per_tok(0), ALU.mult).then_inc(tbl_ready, 1)
            own.step(tt(oht[:, :, 0, :], member, per_tok(1), ALU.mult))
            tt(entry(2), oht[:, :, 0, :], kth, ALU.add).then_inc(tbl_ready, 1)
            dve.wait_ge(pos_mm, 1)
            own.step(ts(pos1, ps[:, 5, 0:NT * E].rearrange("p (i e) -> p i e", i=NT), 1.0, None, ALU.add))
            own.step(tt(pos1, pos1, member, ALU.mult))
            ts(entry(0), pos1, -1.0, None, ALU.add).then_inc(tbl_ready, 1)
            own.step(v.tensor_reduce(ovf[:], ps[:, 5, NT * E:(NT + 1) * E], AX.X, ALU.max))
            ts(flag[:], ovf[:], float(P), None, ALU.is_gt).then_inc(flag_ready, 1)

            def select(m, slots):
                dve.wait_ge(te_ready, m + 1)
                dve.wait_ge(meta_mm, m)
                for i in range(NT):
                    ts(sels[:, i, :], slots[:], te[:, i, 0:1], None, ALU.is_equal).then_inc(sel_ready, 1)

            def selected(e, m):
                dve.wait_ge(meta_mm, m + 1)
                ts(idx_of[:, bass.ds(e, 1), :].rearrange("p a c -> p (a c)"), ps[:, 6, 1:3], float(ABSENT), None, ALU.add).then_inc(meta_ready, 1)
                v.tensor_copy(gate_of[:, bass.ds(e, 1)], ps[:, 6, 3:4]).then_inc(meta_ready, 1)

            def rows(xi):
                for b, bank in enumerate((7, 6)):
                    dve.wait_ge(xTh_ready, 2 * xi + b + 1)
                    part = (slice(None), slice(4 * b, 4 * b + 4))
                    tt(xTl[part], ps[:, bank, :].rearrange("p (k c) -> p k c", k=4), xTh[part], ALU.subtract).then_inc(xT_ready, 1)

            def chunk_rest(gi, k):
                dve.wait_ge(gu_rounded, KD * gi + k + 1)
                tt(gul[:, k, :], guw[:, k, :], guh[k % 4][:], ALU.subtract).then_inc(gu_split, 1)

            hg = ps[:, 0:4, :].rearrange("p b (n c) -> p c (b n)", c=2)

            def gates_in(gi):
                dve.wait_ge(gu_used, KD * (gi + 1))
                ts(gt[:], hg[:, 0, :], SWIGLU_LIMIT, None, ALU.min).then_inc(gt_ready, 1)

            def ups_in(gi):
                ts(up[:], hg[:, 1, :], SWIGLU_LIMIT, -SWIGLU_LIMIT, ALU.min, ALU.max).then_inc(up_read, 1)

            def swiglu(gi):
                dve.wait_ge(sg_ready2, gi + 1)
                own.step(tt(gt[:], gt[:], sg[:], ALU.mult))
                stt(act[:], up[:], 1.0, gt[:], ALU.add, ALU.mult).then_inc(act_ready, 1)

            def expert_turn(e, last=False):
                for k in range(4, KD):
                    chunk_rest(e, k)
                select(e + 2, iota_slot)
                if not last:
                    for k in range(2):
                        chunk_rest(e + 1, k)
                gates_in(e)
                selected(e + 2, e + 2)
                ups_in(e)
                rows(e + 1)
                swiglu(e)
                if not last:
                    for k in range(2, 4):
                        chunk_rest(e + 1, k)

            select(0, iota_slot)
            for k in range(4):
                chunk_rest(0, k)
            selected(0, 0)
            select(1, iota_slot)
            rows(0)
            selected(1, 1)
            own.begin(0, 1)
            expert_turn(0)
            own.end(1)
            with dve.Fori(1, E - 1) as e:
                own.begin(e - 1, 1)
                expert_turn(e)
                own.end(E - 2)
            own.begin(0, 1)
            expert_turn(E - 1, last=True)
            own.end(1)
            with dve.If(many(dve) > 0):
                common, own = own, Chain(dve, dve_over)
                v.tensor_copy(slot_b[:], iota_slot[:]).then_inc(slot_ready, 1)
                with dve.Fori(1, NT) as b:
                    dve.wait_ge(slot_ready, b)
                    ts(slot_b[:], slot_b[:], float(P), None, ALU.add).then_inc(slot_ready, 1)
                    dve.wait_ge(slot_ready, b + 1)
                    v.memset(tick[:], 0.0)
                    with dve.Fori(0, E) as e:
                        n = extra(b, e)
                        own.begin(n, 1)
                        select(E + 2 + n, slot_b)
                        selected(e, E + 2 + n)
                        rows(E + 1 + n)
                        for k in range(KD):
                            chunk_rest(E + n, k)
                        gates_in(E + n)
                        ups_in(E + n)
                        swiglu(E + n)
                        own.end((NT - 1) * E)
                own = common

            for i in range(NT):
                dve.wait_ge(y_in[i], DMA)
                y = yfin[:, i, :]
                own.mark(tt(y[:, 0:D], y[:, 0:D], y[:, D:2 * D], ALU.add))
                own.step(tt(y[:, 2 * D:3 * D], y[:, 2 * D:3 * D], y[:, 3 * D:4 * D], ALU.add))
                own.mark(tt(hres[:, i, :], hres[:, i, :], y[:, 0:D], ALU.add))
                own.settle()
                tt(hres[:, i, :], hres[:, i, :], y[:, 2 * D:3 * D], ALU.add).then_inc(f_sum, 1)
            variance(2, f_square, f_var)
            dve.wait_ge(f_std, 1)
            own.step(v.reciprocal(rstd[:, 2, :], ssq[:, 2, :]))
            dve.wait_ge(gfin_in, DMA)
            for i in range(NT):
                stt(hres[:, i, :], hres[:, i, :], rstd[:, 2, i:i + 1], gfin, ALU.mult, ALU.mult).then_inc(o_ready, 1)


_INS = ['x', 'positions', 'g_mix', 'w_in', 'conv_qk', 'b_if', 'g_mlstm_norm', 'w_attn_out', 'w_mlstm_out', 'w_mix_out', 'g_ffn',
        'w_router', 'b_router', 'w_gate_up', 'b_gate_up', 'w_down', 'b_down', 'g_final']


def kernel(**inputs):
    import concourse.bacc as _bacc
    from concourse.bass_utils import run_bass_kernel_spmd as _run

    nc = _bacc.Bacc("TRN2", target_bir_lowering=False, num_devices=1)
    arrays, args = {}, []
    for name in _INS:
        a = np.ascontiguousarray(inputs[name])
        arrays[f"in_{name}"] = a
        args.append(nc.dram_tensor(f"in_{name}", a.shape, mybir.dt.from_np(a.dtype), kind="ExternalInput").ap())
    shape = arrays["in_x"].shape
    args.append(nc.dram_tensor("out_0", shape, F32, kind="ExternalOutput").ap())
    hybrid_block(nc, *args)
    r = _run(nc, [arrays], core_ids=[0])
    return r.results[0]["out_0"]
```

```python
from contextlib import ExitStack

import numpy as np

import concourse.bass as bass
from concourse import mybir

F32 = mybir.dt.float32
F32R = mybir.dt.float32r
BF16 = mybir.dt.bfloat16
I32 = mybir.dt.int32
U32 = mybir.dt.uint32
ALU = mybir.AluOpType
ACT = mybir.ActivationFunctionType
AX = mybir.AxisListType

P = 128
BANK = 512
NEG = -1.0e30
RMS_EPS = 1e-5
LN_EPS = 1e-5
ROPE_THETA = 500000.0
WINDOW0 = 128
SWIGLU_LIMIT = 7.0
SWIGLU_ALPHA = 1.702
TOP_K = 4
ABSENT = 4096
DMA = 16


class Chain:

    def __init__(self, eng, sem):
        self.eng, self.sem, self.total, self.base, self.n = eng, sem, 0, 0, 0

    def begin(self, turn, per_turn):
        self.total += self.n
        self.per, self.base, self.n = per_turn, self.total + turn * per_turn, 0

    def end(self, turns):
        assert self.n == self.per, f"{self.n} steps in a turn, not {self.per}"
        self.total += turns * self.per
        self.base, self.n = self.total, 0

    def mark(self, ins):
        self.n += 1
        ins.then_inc(self.sem, 1)

    def settle(self):
        self.eng.wait_ge(self.sem, self.base + self.n)

    def step(self, ins):
        self.mark(ins)
        self.settle()


class Region:

    def __init__(self, nc, start, end):
        self.nc, self.at, self.end = nc, start, end

    def tensor(self, name, shape, dt=F32):
        size = 1
        for n in shape[1:]:
            size *= n
        size = -(-size * (2 if dt == BF16 else 4) // 32) * 32
        assert self.at + size <= self.end, f"{name}: {self.at + size} of {self.end}"
        t = self.nc.alloc_sbuf_tensor_at(name, shape, dt, offset=self.at)
        self.at += size
        return t


def hybrid_block(nc, x, positions, g_mix, w_in, conv_qk, b_if, g_mlstm_norm, w_attn_out, w_mlstm_out, w_mix_out,
                 g_ffn, w_router, b_router, w_gate_up, b_gate_up, w_down, b_down, g_final, out):
    _, T, D = x.shape
    NT = T // P
    KD = D // P
    E = w_router.shape[2]
    F = w_down.shape[2]
    F2 = 2 * F
    H = 4
    G = 3
    DH = 128
    MDH = D // H
    QK_SCALE = float(DH) ** -0.5
    MK_SCALE = float(MDH) ** -0.5
    TAPS = conv_qk.shape[1]
    CT = 2 * D // P
    ROT = DH // 4
    HALF = ROT // 2
    AW = G * H * DH
    AQ, AK, AV = 0, AW, 2 * AW
    MQ = 3 * AW
    MK, MV, MO, MI = MQ + D, MQ + 2 * D, MQ + 3 * D, MQ + 4 * D
    MF = MI + H
    GA = MF + H
    GM = GA + D
    assert T == BANK and DH == P and MDH == 2 * P and w_in.shape[2] == GM + D and F == D and E == 32

    def chunked(w):
        return w.rearrange("(k p) n -> p k n", p=P)

    w_in_v, wa_v, wm_v, wmix_v = chunked(w_in[0]), chunked(w_attn_out[0]), chunked(w_mlstm_out[0]), chunked(w_mix_out[0])
    gu_v = w_gate_up[0].rearrange("e (k p) n -> p e k n", p=P)
    dn_v = w_down[0].rearrange("e (k p) n -> p e k n", p=P)
    x_v = x[0].rearrange("(i p) d -> p i d", p=P)
    out_v = out[0].rearrange("(i p) d -> p i d", p=P)

    xn_rows = nc.dram_tensor("xn_rows", (T, D), F32).ap()
    y_rows = nc.dram_tensor("y_rows", (T * TOP_K, D), F32).ap()
    xn_v = xn_rows.rearrange("(i p) d -> p i d", p=P)
    y_v = y_rows.rearrange("(i p k) d -> p i (k d)", p=P, k=TOP_K)

    keep = Region(nc, -(-nc.sbuf_base // 64) * 64, nc.sbuf_usable_end)
    late_split = Region(nc, keep.at, keep.at + 4 * D * 4)
    hres = keep.tensor("hres", [P, NT, D])
    router_xT = Region(nc, keep.at, keep.at + KD * T * 4)
    xh = keep.tensor("xh", [P, KD, T], F32R)
    router = Region(nc, keep.at, keep.at + KD * T * 4)
    xl = keep.tensor("xl", [P, KD, T], F32R)
    sel = keep.tensor("sel", [P, E, P], BF16)
    bsp = keep.tensor("bsp", [P, F2 + D], BF16)
    ident = keep.tensor("ident", [P, P])
    vecT = keep.tensor("vecT", [P, 88])
    ssq = keep.tensor("ssq", [P, 3, NT])
    rstd = keep.tensor("rstd", [P, 3, NT])
    flag = keep.tensor("flag", [P, 1], I32)
    eps = keep.tensor("eps", [P, 1])
    tick = keep.tensor("tick", [P, 1])
    xn2T = router_xT.tensor("xn2T", [P, KD, T])
    xw2 = router.tensor("xw2", [P, 2, D])
    lg = router.tensor("lg", [P, NT, E])
    brt = router.tensor("brt", [P, E])
    wr = router.tensor("wr", [P, KD, E])
    iota_slot = router.tensor("iota_slot", [P, P])
    gffn = router.tensor("gffn", [P, D])
    iota_e = router.tensor("iota_e", [P, E])
    iota_k = router.tensor("iota_k", [P, TOP_K])
    tokf = router.tensor("tokf", [P, 2, NT])
    tri = router.tensor("tri", [P, P], BF16)
    onesb = router.tensor("onesb", [P, P], BF16)
    chunk_a = Region(nc, router_xT.at - KD * T * 4, router_xT.at)
    chunk_b = Region(nc, router_xT.at, router_xT.at + 2 * D * 4)
    GMIX, GFFN, GMEM = TAPS * CT, TAPS * CT + KD, TAPS * CT + 2 * KD

    RING = 12 * F2 * 4
    mixed = Region(nc, keep.at, keep.at + RING)
    attT = mixed.tensor("attT", [P, H, T])
    memT = mixed.tensor("memT", [P, KD, T])
    mem = Region(nc, mixed.at, mixed.end)
    raw = mem.tensor("raw", [P, 4, T + TAPS - 1])
    cv = mem.tensor("cv", [P, 4, T])
    qkf = mem.tensor("qkf", [P, 4, T])
    mvraw = mem.tensor("mvraw", [P, 2, T])
    VN = MDH + 2
    vN = mem.tensor("vN", [P, NT, VN])
    wexp = mem.tensor("wexp", [P, NT, T])
    AT = mem.tensor("AT", [P, NT, T])
    hh = mem.tensor("hh", [P, NT, MDH])
    sgo = mem.tensor("sgo", [P, 2, T])
    nmb = mem.tensor("nmb", [P, H, T])
    nmd = mem.tensor("nmd", [P, T])
    cmask = mem.tensor("cmask", [P, P])
    ceT = mem.tensor("ceT", [P, NT, 64])
    expE = mem.tensor("expE", [P, NT, H])
    cwh = mem.tensor("cwh", [P, TAPS, 4])
    gmh = mem.tensor("gmh", [P, 2])
    ch = mem.tensor("ch", [P, NT])
    eh = mem.tensor("eh", [P, NT])
    den = mem.tensor("den", [P, 2, NT])
    bst = mem.tensor("bst", [P, NT, 6])
    mv = mem.tensor("mv", [P, NT, 2])
    mrs = mem.tensor("mrs", [P, 2, NT])
    pre = Region(nc, mixed.at, mixed.end)
    pre.tensor("skip_to_wexp", [P, 4 * (T + TAPS - 1) + 8 * T + 2 * T + NT * VN])
    wif = pre.tensor("wif", [P, KD, 64])
    gat = pre.tensor("gat", [64, 3, T])
    ce = pre.tensor("ce", [64, T])
    ones_row = pre.tensor("ones_row", [H, T])
    head_sel = pre.tensor("head_sel", [H, H, P])
    bcol = pre.tensor("bcol", [64, 1])
    norm = Region(nc, mixed.at, mixed.end)
    norm.tensor("skip_to_qkf", [P, 4 * (T + TAPS - 1) + 4 * T])
    xw = norm.tensor("xw", [P, 2, D])
    xt = norm.tensor("xt", [P, 2, 4 * P])
    att = Region(nc, mixed.at, mixed.end)
    qk = att.tensor("qk", [P, 2 * G, T])
    avraw = att.tensor("avraw", [P, G, T])
    vh = att.tensor("vh", [P, G, NT, P])
    SC = T + 2 * P
    sm = att.tensor("sm", [P, 2, SC])
    pr = att.tensor("pr", [P, 2, SC])
    pT = att.tensor("pT", [P, 6, P])
    rs = att.tensor("rs", [ROT, 2 * G, T])
    smax = att.tensor("smax", [P, 2, 4])
    brow = att.tensor("brow", [P, F2 + D])
    mrg = Region(nc, mixed.at, mixed.end)
    attR = mrg.tensor("attR", [P, H, T], F32R)
    attL = mrg.tensor("attL", [P, H, T], F32R)
    memR = mrg.tensor("memR", [P, KD, T], F32R)
    memL = mrg.tensor("memL", [P, KD, T], F32R)
    mgt = mrg.tensor("mgt", [P, 2, 2, T])
    wmix1 = mrg.tensor("wmix1", [P, 2, D])
    assert att.at <= mrg.at
    sgm = mrg.tensor("sgm", [P, 2, 2, T])
    mixw = Region(nc, keep.at, mixed.at)
    wmix0 = mixw.tensor("wmix0", [P, KD - 2, D])
    tail = Region(nc, keep.at + RING, nc.sbuf_usable_end)
    mergedT = tail.tensor("mergedT", [P, KD, T])
    wraw = tail.tensor("wraw", [P, 4, D])
    split0 = tail.tensor("split0", [P, 2, 2, D], F32R)
    split1 = late_split.tensor("split1", [P, 2, 2, D], F32R)
    fcol = tail.tensor("fcol", [P, 2])
    masks = Region(nc, keep.at + RING, tail.end)
    amask = masks.tensor("amask", [P, NT, SC])
    rcos = masks.tensor("rcos", [ROT, T])
    rsin = masks.tensor("rsin", [ROT, T])
    start = Region(nc, pre.at, mixed.end)
    vrow = start.tensor("vrow", [88, P])
    frow = start.tensor("frow", [1, 2, P])
    post = start.tensor("post", [ROT, T], I32)
    ang = start.tensor("ang", [ROT, 3, T])
    m4 = start.tensor("m4", [P, P], I32)
    wifh = start.tensor("wifh", [P, KD, 64], F32R)
    wifl = start.tensor("wifl", [P, KD, 64], F32R)
    exp_ring = Region(nc, keep.at, keep.at + RING)
    rests = Region(nc, exp_ring.at, exp_ring.end)
    guw = exp_ring.tensor("guw", [P, KD, F2])
    gul = rests.tensor("gul", [P, KD, F2], F32R)
    dnw = exp_ring.tensor("dnw", [P, KD, D])
    ex = Region(nc, keep.at + RING, nc.sbuf_usable_end)
    xg = ex.tensor("xg", [P, D])
    xTh = ex.tensor("xTh", [P, KD, P], F32R)
    xTl = ex.tensor("xTl", [P, KD, P], F32R)
    gt = ex.tensor("gt", [P, F])
    sg = ex.tensor("sg", [P, F])
    up = ex.tensor("up", [P, F])
    actT = ex.tensor("actT", [P, KD, P])
    yw = ex.tensor("yw", [P, D])
    tbl = ex.tensor("tbl", [P, E + 2, NT, 4])
    te = ex.tensor("te", [P, NT, 4])
    sels = ex.tensor("sels", [P, NT, P])
    gate_of = ex.tensor("gate_of", [P, E + 2])
    idx_of = ex.tensor("idx_of", [P, E + 2, 2], I32)
    gcur = ex.tensor("gcur", [P, 1])
    gidx = ex.tensor("gidx", [P, 1], I32)
    sidx = ex.tensor("sidx", [P, 1], I32)
    pool_tick = ex.tensor("pool_tick", [P, 1])
    slot_b = ex.tensor("slot_b", [P, P])
    v8 = ex.tensor("v8", [P, NT, 8])
    i8 = ex.tensor("i8", [P, NT, 8], U32)
    i8f = ex.tensor("i8f", [P, NT, 8])
    gk = ex.tensor("gk", [P, NT, TOP_K])
    gs = ex.tensor("gs", [P, 2, NT])
    i_tmp = ex.tensor("i_tmp", [P, E], I32)
    oh = gt[:, 0:NT * TOP_K * E].rearrange("p (i k e) -> p i k e", i=NT, k=TOP_K)
    oht = sg[:, 0:NT * TOP_K * E].rearrange("p (i k e) -> p i k e", i=NT, k=TOP_K)
    member = up[:, 0:NT * E].rearrange("p (i e) -> p i e", i=NT)
    pos1 = up[:, NT * E:2 * NT * E].rearrange("p (i e) -> p i e", i=NT)
    kth = up[:, 2 * NT * E:3 * NT * E].rearrange("p (i e) -> p i e", i=NT)
    gte = up[:, 3 * NT * E:4 * NT * E].rearrange("p (i e) -> p i e", i=NT)
    memb = ex.tensor("memb", [P, NT, E], BF16)
    ovf = ex.tensor("ovf", [P, 1])
    act = sg
    guh = [chunk_a.tensor("guh0", [P, F2], F32R), chunk_a.tensor("guh1", [P, F2], F32R),
           chunk_b.tensor("guh2", [P, F2], F32R), ex.tensor("guh3", [P, F2], F32R)]

    ctx = ExitStack()
    with ctx:
        ps = ctx.enter_context(nc.psum_tensor("ps", [P, 8, BANK], F32))

        def sem(name):
            return ctx.enter_context(nc.semaphore(name))

        x_in = [sem(f"x_in{i}") for i in range(NT)]
        vec_in, pos_in, bif_in, wif_in, brow_in, router_in = (
            sem(n) for n in ("vec_in", "pos_in", "bif_in", "wif_in", "brow_in", "router_in"))
        w_in_slot = [sem(f"w_in_slot{s}") for s in range(4)]
        wmix_in = [sem(f"wmix_in{k}") for k in range(KD)]
        rounded, w_split, xt_ready, xh_ready, wif_round, wif_split, am_round, am_split = (
            sem(n) for n in ("rounded", "w_split", "xt_ready", "xh_ready", "wif_round", "wif_split", "am_round", "am_split"))
        pool_step, dve_step, act_step = sem("pool_step"), sem("dve_step"), sem("act_step")
        tables = sem("tables")
        x_square, x_std, xw_ready, xw_used, xnT_ready = (
            sem(n) for n in ("x_square", "x_std", "xw_ready", "xw_used", "xnT_ready"))
        vecT_done, angle_ready, sines_ready, m4_ready = (
            sem(n) for n in ("vecT_done", "angle_ready", "sines_ready", "m4_ready"))
        m4_made, sines_done, num_out = sem("m4_made"), sem("sines_done"), sem("num_out")
        gate_mm, gate_abs, gate_ln, gate_rows, gate_T, gate_cols, nmb_mm, nmb_ready = (
            sem(n) for n in ("gate_mm", "gate_abs", "gate_ln", "gate_rows", "gate_T", "gate_cols", "nmb_mm", "nmb_ready"))
        w_used, proj_out = sem("w_used"), sem("proj_out")
        conv_ready, qk_ready, cols_ready, wexp_ready, mv_T, vN_ready, at_mm, at_ready, num_mm, hvar_ready, hstd_ready, hn_ready, hn_T, mem_ready = (
            sem(n) for n in ("conv_ready", "qk_ready", "cols_ready", "wexp_ready", "mv_T", "vN_ready", "at_mm", "at_ready",
                             "num_mm", "hvar_ready", "hstd_ready", "hn_ready", "hn_T", "mem_ready"))
        rot_ready, av_T, vh_ready, s_mm, smax_ready, exp_ready, pr_ready, pr_T, pT_act, pT_dve, pv_mm, att_ready = (
            sem(n) for n in ("rot_ready", "av_T", "vh_ready", "s_mm", "smax_ready", "exp_ready", "pr_ready", "pr_T", "pT_act",
                             "pT_dve", "pv_mm", "att_ready"))
        sg_ready, merged, mix_mm, h_ready = (sem(n) for n in ("sg_ready", "merged", "mix_mm", "h_ready"))
        h_square, h_std, lg_read, late_ex, hw_ready, hw_used, xn2T_ready, lg_mm, top_ready, gk_ready, memb_ready, pos_mm, tbl_ready = (
            sem(n) for n in ("h_square", "h_std", "lg_read", "late_ex", "hw_ready", "hw_used", "xn2T_ready", "lg_mm",
                             "top_ready", "gk_ready", "memb_ready", "pos_mm", "tbl_ready"))
        late_tables, bias_ready, flag_ready, slot_ready = (sem(n) for n in ("late_tables", "bias_ready", "flag_ready", "slot_ready"))
        gu_rounded, gu_split, xTh_ready = sem("gu_rounded"), sem("gu_split"), sem("xTh_ready")
        gu_in = [sem(f"gu_in{s}") for s in range(KD)]
        dn_in = [sem(f"dn_in{s}") for s in range(KD // 2)]
        gu_used, dn_used, te_ready, sel_ready, meta_mm, meta_ready, gathered, xg_T, xT_ready, up_read, gt_ready, sg_ready2, act_ready, act_T, actT_ready, gcur_ready, y_ready, y_stored = (
            sem(n) for n in ("gu_used", "dn_used", "te_ready", "sel_ready", "meta_mm", "meta_ready", "gathered", "xg_T", "xT_ready",
                             "up_read", "gt_ready", "sg_ready2", "act_ready", "act_T", "actT_ready", "gcur_ready", "y_ready", "y_stored"))
        all_stored, gfin_in, f_sum, f_square, f_std, o_ready, o_stored = (
            sem(n) for n in ("all_stored", "gfin_in", "f_sum", "f_square", "f_std", "o_ready", "o_stored"))
        pool_over, dve_over, act_over = sem("pool_over"), sem("dve_over"), sem("act_over")
        y_in = [sem(f"y_in{i}") for i in range(NT)]
        xn_stored = [sem(f"xn_stored{i}") for i in range(NT)]

        TABLES = ("ident", "wif", "ce", "rows", "raw", "vN", "cmask", "amask", "sel")
        made = {name: n + 1 for n, name in enumerate(TABLES)}

        N_MEM, N_ATT, N_MRG = 8, 3 * G, 8
        ATT0 = N_MEM * H
        MRG0 = ATT0 + N_ATT * H
        MIX0 = MRG0 + N_MRG * (KD // 2)

        def mem_cols(h):
            return [c + MDH * h + P * u for c in (MQ, MK, MV, MO) for u in range(2)]

        def att_cols(h):
            return [c + H * DH * g + DH * h for c in (AQ, AK, AV) for g in range(G)]

        def split(slot):
            return (split0, split1)[slot // 2][:, slot % 2]

        def col(expr):
            return bass.ds(expr, P)

        yfin = guw[:].rearrange("p (i a) n -> p i (a n)", i=NT)
        gfin = dnw[:, 0, :]

        def many(eng):
            eng.wait_ge(flag_ready, 1)
            return eng.value_load(flag[0:1, 0:1], min_val=0, max_val=1)

        def extra(b, e):
            return (b - 1) * E + e

        block = ctx.enter_context(nc.Block())

        @block.sync
        def _(sp):
            nc.sync.dma_start(vrow[0:GMIX, :], conv_qk[0].rearrange("j (c p) -> (j c) p", p=P)).then_inc(vec_in, DMA)
            nc.sync.dma_start(vrow[GMIX:GFFN, :], g_mix.rearrange("a (c p) -> (a c) p", p=P)).then_inc(vec_in, DMA)
            nc.sync.dma_start(vrow[GFFN:GMEM, :], g_ffn.rearrange("a (c p) -> (a c) p", p=P)).then_inc(vec_in, DMA)
            nc.sync.dma_start(vrow[GMEM:GMEM + KD, :], g_mlstm_norm.rearrange("a (c p) -> (a c) p", p=P)).then_inc(vec_in, DMA)
            for i in range(NT):
                nc.sync.dma_start(hres[:, i, :], x_v[:, i, :]).then_inc(x_in[i], DMA)
            nc.sync.dma_start(bcol[0:H, :], b_if[:, 0:H].rearrange("a h -> h a")).then_inc(bif_in, DMA)
            nc.sync.dma_start(bcol[32:32 + H, :], b_if[:, H:2 * H].rearrange("a h -> h a")).then_inc(bif_in, DMA)
            sp.wait_ge(tables, made["wif"])
            nc.sync.dma_start(wif[:, :, 0:H], w_in_v[:, :, MI:MI + H]).then_inc(wif_in, DMA)
            nc.sync.dma_start(wif[:, :, 32:32 + H], w_in_v[:, :, MF:MF + H]).then_inc(wif_in, DMA)
            def load_tile(slot, c, w=w_in_v):
                nk = w.shape[1]
                nc.sync.dma_start(wraw[:, slot, 0:nk * P].rearrange("p (k n) -> p k n", n=P), w[:, :, col(c)]).then_inc(w_in_slot[slot], DMA)

            for j, c in enumerate(mem_cols(0)):
                if j >= 4:
                    sp.wait_ge(w_split, j - 3)
                load_tile(j % 4, c)
                if j == 0:
                    nc.sync.dma_start(post[:], positions[0:1, :].to_broadcast([ROT, T])).then_inc(pos_in, DMA)
            with sp.Fori(1, H) as h:
                for j, c in enumerate([sp.snap(c) for c in mem_cols(h)]):
                    sp.wait_ge(w_split, N_MEM * h + j - 3)
                    load_tile(j % 4, c)
            for j, c in enumerate(att_cols(0)):
                sp.wait_ge(w_split, ATT0 + j - (3 if j < 3 else 2))
                load_tile(j % 3, c)
            sp.wait_ge(mem_ready, 2 * H)
            for g in (0, 64, 96):
                nc.sync.dma_start(brow[g:g + E, 0:F2], b_gate_up[0]).then_inc(brow_in, DMA)
                nc.sync.dma_start(brow[g:g + E, F2:F2 + D], b_down[0]).then_inc(brow_in, DMA)
            with sp.Fori(1, H) as h:
                for j, c in enumerate([sp.snap(c) for c in att_cols(h)]):
                    sp.wait_ge(w_split, ATT0 + N_ATT * h + j - 2)
                    load_tile(j % 3, c)

            def merge_tiles(b, first=False):
                at = [P * (2 * b + u) + k0 for k0, u in ((GA, 0), (GM, 0), (GA, 1), (GM, 1))]
                if not first:
                    at = [sp.snap(a) for a in at]
                for t in range(N_MRG):
                    if not (first and t == 3):
                        sp.wait_ge(w_split, MRG0 + N_MRG * b + t - (2 if first and t < 3 else 3))
                    if t < 4:
                        load_tile(t, at[t])
                    else:
                        w, c = wm_v if t % 2 else wa_v, 2 * P * b + P * (t // 6 + 1)
                        load_tile(t % 4, (c if first else sp.snap(c)) - P, w)

            merge_tiles(0, first=True)
            sp.wait_ge(am_split, 3)
            for k in range(KD):
                nc.sync.dma_start(wmix0[:, k, :] if k < KD - 2 else wmix1[:, k - KD + 2, :], wmix_v[:, k, :]).then_inc(wmix_in[k], DMA)
            with sp.Fori(1, KD // 2) as b:
                merge_tiles(b)
            sp.wait_ge(w_used, MIX0)
            for i in range(NT):
                nc.sync.dma_start(hres[:, i, :], x_v[:, i, :]).then_inc(x_in[i], DMA)
            nc.sync.dma_start(brt[:], b_router[0:1, :].to_broadcast([P, E])).then_inc(router_in, DMA)
            nc.sync.dma_start(wr[:], chunked(w_router[0])).then_inc(router_in, DMA)
            nc.sync.dma_start(gffn[:], g_ffn[0:1, :].to_broadcast([P, D])).then_inc(router_in, DMA)
            sp.wait_ge(merged, KD)

            def load_gu(e, s):
                nc.sync.dma_start(guw[:, s, :], gu_v[:, bass.ds(e, 1), s, :].rearrange("p a n -> p (a n)")).then_inc(gu_in[s], DMA)

            def load_dn(e, s):
                nc.sync.dma_start(dnw[:, 2 * s:2 * s + 2, :],
                                  dn_v[:, bass.ds(e, 1), 2 * s:2 * s + 2, :].rearrange("p a k n -> p (a k) n")).then_inc(dn_in[s], DMA)

            for s in range(3, KD):
                load_gu(0, s)
            for s in (0, 1, 3):
                load_dn(0, s)
            sp.wait_ge(mix_mm, 2 * NT)
            for s in range(3):
                load_gu(0, s)
            load_dn(0, 2)
            for s in range(KD):
                sp.wait_ge(gu_used, s + 1)
                load_gu(1, s)
            with sp.Fori(2, E) as e:
                before = sp.snap(e - 1)
                for s in range(KD):
                    sp.wait_ge(gu_used, KD * (e - 1) + s + 1)
                    load_gu(e, s)
                for s in range(KD // 2):
                    sp.wait_ge(dn_used, (KD // 2) * (e - 2) + s + 1)
                    load_dn(before, s)
            for s in range(KD // 2):
                sp.wait_ge(dn_used, (KD // 2) * (E - 2) + s + 1)
                load_dn(E - 1, s)
            with sp.If(many(sp) > 0):
                with sp.Fori(1, NT) as b:
                    with sp.Fori(0, E) as e:
                        g_idx = extra(b, e) + E
                        for s in range(KD):
                            sp.wait_ge(gu_used, KD * (g_idx - 1) + s + 1)
                            load_gu(e, s)
                        for s in range(KD // 2):
                            sp.wait_ge(dn_used, (KD // 2) * (g_idx - 1) + s + 1)
                            load_dn(e, s)
            sp.wait_ge(all_stored, 1)
            sp.wait_ge(dn_used, KD // 2 * E)
            nc.sync.dma_start(gfin[:], g_final.rearrange("(a d) -> a d", a=1).to_broadcast([P, D])).then_inc(gfin_in, DMA)
            for i in range(NT):
                nc.sync.dma_start(yfin[:, i, :], y_v[:, i, :]).then_inc(y_in[i], DMA)
            for i in range(NT):
                sp.wait_ge(o_ready, i + 1)
                nc.sync.dma_start(out_v[:, i, :], hres[:, i, :]).then_inc(o_stored, DMA)
            sp.wait_ge(o_stored, DMA * NT)

        @block.gpsimd
        def _(pool):
            own = Chain(pool, pool_step)
            g = nc.gpsimd

            def table(name, ins):
                ins.then_inc(tables, 1)
                pool.wait_ge(tables, made[name])

            own.step(g.memset(eps[:], RMS_EPS))
            own.step(g.memset(ident[:], 0.0))
            table("ident", g.affine_select(out=ident[:], in_=ident[:], compare_op=ALU.not_equal, fill=1.0, base=0,
                                  pattern=[[-1, P]], channel_multiplier=1))
            table("wif", g.memset(wif[:], 0.0))
            table("ce", g.memset(ce[:], 0.0))
            own.step(g.memset(ones_row[:], 1.0))
            own.step(g.memset(frow[:], -1.0))
            for j in range(HALF):
                freq = float(np.float32(ROPE_THETA) ** np.float32(-j / HALF))
                own.step(g.memset(frow[0:1, 0, j:j + HALF + 1:HALF], freq))
            own.step(g.memset(frow[0:1, 1, HALF:ROT], 1.0))
            own.step(g.memset(head_sel[:], 0.0))
            table("rows", g.affine_select(out=head_sel[:], in_=head_sel[:], compare_op=ALU.not_equal, fill=1.0, base=0,
                                  pattern=[[-1, H], [0, P]], channel_multiplier=1))
            table("raw", g.memset(raw[:, :, 0:TAPS - 1], 0.0))
            table("vN", g.memset(vN[:, :, MDH:VN], 1.0))
            g.iota(m4[:], pattern=[[-1, P]], base=P, channel_multiplier=1).then_inc(m4_made, 1)
            pool.wait_ge(m4_made, 1)
            own.step(g.memset(cmask[:], 0.0))
            table("cmask", g.affine_select(out=cmask[:], in_=cmask[:], compare_op=ALU.is_ge, fill=NEG, base=0,
                                  pattern=[[1, P]], channel_multiplier=-1))

            def rest(n, slot, nk=KD):
                pool.wait_ge(rounded, n + 1)
                g.tensor_tensor(split(slot)[:, 1, 0:nk * P], wraw[:, slot, 0:nk * P], split(slot)[:, 0, 0:nk * P], ALU.subtract).then_inc(w_split, 1)

            for j in range(N_MEM):
                rest(j, j % 4)
            pool.wait_ge(w_split, N_MEM)
            own.step(g.memset(amask[:, :, 0:T + P], 0.0))
            m0, m1, m2 = amask[:, :, 0:T], amask[:, :, T:T + P], amask[:, :, T + P:SC]
            own.step(g.affine_select(out=m0, in_=m0, compare_op=ALU.is_ge, fill=NEG, base=0,
                                     pattern=[[1, NT], [-1, T]], channel_multiplier=NT))
            own.step(g.affine_select(out=m0, in_=m0, compare_op=ALU.is_ge, fill=NEG, base=WINDOW0,
                                     pattern=[[-1, NT], [1, T]], channel_multiplier=-NT))
            own.step(g.affine_select(out=m1, in_=m1, compare_op=ALU.is_ge, fill=NEG, base=0,
                                     pattern=[[0, NT], [-1, P]], channel_multiplier=1))
            pool.wait_ge(m4_ready, 1)
            table("amask", g.affine_select(out=m2, in_=m2, compare_op=ALU.is_ge, fill=NEG, base=0,
                                  pattern=[[0, NT], [-1, P]], channel_multiplier=1))
            with pool.Fori(1, H) as h:
                for j in range(N_MEM):
                    rest(N_MEM * h + j, j % 4)
            for j in range(N_ATT):
                rest(ATT0 + j, j % 3)
            pool.wait_ge(w_split, ATT0 + N_ATT)
            own.step(g.memset(bsp[32:64], 0.0))
            own.step(g.memset(sel[:], 0.0))
            for q in (0, 64):
                own.step(g.affine_select(out=sel[q:q + E], in_=sel[q:q + E], compare_op=ALU.not_equal, fill=1.0, base=0,
                                         pattern=[[-1, E], [0, P]], channel_multiplier=1))
            table("sel", g.affine_select(out=sel[96:P], in_=sel[96:P], compare_op=ALU.not_equal, fill=1.0, base=0,
                                  pattern=[[-1, E], [0, P]], channel_multiplier=1))
            own.settle()
            with pool.Fori(1, H) as h:
                for j in range(N_ATT):
                    rest(ATT0 + N_ATT * h + j, j % 3)
            with pool.Fori(0, KD // 2) as b:
                for t in range(N_MRG):
                    rest(MRG0 + N_MRG * b + t, t % 4, H if t in (4, 6) else KD)
            pool.wait_ge(w_used, MIX0)
            own.step(g.iota(iota_slot[:], pattern=[[1, P]], base=0, channel_multiplier=0, allow_small_or_imprecise_dtypes=True))
            own.step(g.iota(iota_e[:], pattern=[[1, E]], base=0, channel_multiplier=0, allow_small_or_imprecise_dtypes=True))
            own.step(g.iota(iota_k[:], pattern=[[1, TOP_K]], base=0, channel_multiplier=0, allow_small_or_imprecise_dtypes=True))
            own.step(g.iota(tokf[:, 0, :], pattern=[[P, NT]], base=-ABSENT, channel_multiplier=1,
                            allow_small_or_imprecise_dtypes=True))
            own.step(g.iota(tokf[:, 1, :], pattern=[[TOP_K * P, NT]], base=-ABSENT, channel_multiplier=TOP_K,
                            allow_small_or_imprecise_dtypes=True))
            own.step(g.memset(onesb[:], 1.0))
            g.affine_select(out=tri[:], in_=onesb[:], compare_op=ALU.is_gt, fill=0.0, base=0,
                            pattern=[[1, P]], channel_multiplier=-1).then_inc(late_tables, 1)
            pool.wait_ge(late_tables, 1)
            pool.wait_ge(mix_mm, 2 * NT)
            own.step(g.memset(tbl[:, E:E + 2, :, 0], -1.0))
            own.step(g.memset(pool_tick[:], 0.0))
            own.step(g.memset(tbl[:, E:E + 2, :, 1:4], 0.0))
            g.memset(xg[:], 0.0).then_inc(late_ex, 1)
            pool.wait_ge(late_ex, 1)
            pool.wait_ge(tbl_ready, 4)
            for i in range(NT):
                pool.wait_ge(xn_stored[i], DMA)

            def table_of(e, m):
                pool.wait_ge(meta_mm, m)
                g.tensor_copy(te[:], tbl[:, bass.ds(e, 1), :, :].rearrange("p a i v -> p (a i) v")).then_inc(te_ready, 1)

            def gather(e, m, xi):
                pool.wait_ge(meta_ready, 2 * (m + 1))
                pool.wait_ge(gathered, DMA * xi)
                pool.wait_ge(xg_T, 2 * xi)
                own.step(g.tensor_copy(gidx[:], idx_of[:, bass.ds(e, 1), 0]))
                g.tensor_tensor(pool_tick[:], pool_tick[:], pool_tick[:], ALU.mult)
                g.indirect_dma_start(out=xg[:], out_offset=None, in_=xn_rows,
                                     in_offset=bass.IndirectOffsetOnAxis(ap=gidx[:, 0:1], axis=0),
                                     bounds_check=T - 1, oob_is_err=False).then_inc(gathered, DMA)

            def scatter(e, gi):
                pool.wait_ge(y_ready, 2 * (gi + 1))
                pool.wait_ge(y_stored, DMA * gi)
                own.step(g.tensor_copy(sidx[:], idx_of[:, bass.ds(e, 1), 1]))
                g.tensor_tensor(pool_tick[:], pool_tick[:], pool_tick[:], ALU.mult)
                g.indirect_dma_start(out=y_rows, out_offset=bass.IndirectOffsetOnAxis(ap=sidx[:, 0:1], axis=0),
                                     in_=yw[:], in_offset=None,
                                     bounds_check=T * TOP_K - 1, oob_is_err=False).then_inc(y_stored, DMA)

            table_of(0, 0)
            gather(0, 0, 0)
            table_of(1, 1)
            gather(1, 1, 1)
            table_of(2, 2)

            def expert_turn(e):
                gather(e + 1, e + 1, e + 1)
                table_of(e + 2, e + 2)
                scatter(e - 1, e - 1)

            expert_turn(1)
            with pool.Fori(2, E) as e:
                own.begin(e - 2, 2)
                expert_turn(e)
                own.end(E - 2)
            scatter(E - 1, E - 1)
            pool.wait_ge(y_stored, DMA * E)
            with pool.If(many(pool) > 0):
                common, own = own, Chain(pool, pool_over)
                with pool.Fori(1, NT) as b:
                    with pool.Fori(0, E) as e:
                        n = extra(b, e)
                        own.begin(n, 2)
                        table_of(e, E + 2 + n)
                        gather(e, E + 2 + n, E + 1 + n)
                        scatter(e, E + n)
                        pool.wait_ge(y_stored, DMA * (E + 1 + n))
                        own.end((NT - 1) * E)
                own = common
            g.engine_nop().then_inc(all_stored, 1)

        @block.tensor
        def _(pe):
            mm, tr = nc.tensor.matmul, nc.tensor.transpose

            pe.wait_ge(tables, made["ident"])
            pe.wait_ge(vec_in, 4 * DMA)
            tr(ps[:, 7, 0:88], vrow[:, :], ident[0:88, 0:88]).then_inc(vecT_done, 1)
            pe.wait_ge(tables, made["rows"])
            tr(ps[:, 6, 0:1], frow[0:1, 0, :], ident[0:1, 0:1])
            tr(ps[:, 6, 1:2], frow[0:1, 1, :], ident[0:1, 0:1]).then_inc(vecT_done, 1)

            def transpose_rows(xw, ready, used, done, i):
                pe.wait_ge(ready, i + 1)
                for b in range(2):
                    if i >= 2:
                        pe.wait_ge(done, 2 * (i - 2) + b + 1)
                    for k in range(4):
                        last = tr(ps[:, 2 * (i % 2) + b, k * P:(k + 1) * P], xw[:, i % 2, (4 * b + k) * P:(4 * b + k + 1) * P], ident[:])
                    last.then_inc(used, 1)

            for i in range(NT):
                transpose_rows(xw, xw_ready, xw_used, xnT_ready, i)
            def product(out, wh, wl, rh, rl, nk):
                for k in range(nk):
                    mm(out, wh(k), rh[:, k, :], start=(k == 0), stop=False)
                    mm(out, wh(k), rl[:, k, :], start=False, stop=False)
                    last = mm(out, wl(k), rh[:, k, :], start=False, stop=(k == nk - 1))
                return last

            pe.wait_ge(wif_split, 1)
            pe.wait_ge(xnT_ready, 2 * NT)
            product(ps[0:64, 4, :], lambda k: wifh[:, k, :], lambda k: wifl[:, k, :], xh, xl, KD).then_inc(gate_mm, 1)

            def project(n, slot, bank, rh=xh, rl=xl, nk=KD):
                pe.wait_ge(w_split, n + 1)
                product(ps[:, bank, :], lambda k: split(slot)[:, 0, k * P:(k + 1) * P], lambda k: split(slot)[:, 1, k * P:(k + 1) * P],
                        rh, rl, nk).then_inc(w_used, 1)

            def mem_tile(h, j):
                n = N_MEM * h + j
                if not isinstance(h, int) or n >= 2:
                    pe.wait_ge(proj_out, n - 1)
                project(n, j % 4, j % 2)

            def mem_gates():
                pe.wait_ge(tables, made["ce"])
                pe.wait_ge(gate_rows, 2)
                for i in range(NT):
                    last = tr(ps[:, 5, i * 64:(i + 1) * 64], ce[:, i * P:(i + 1) * P], ident[0:64, 0:64])
                last.then_inc(gate_T, 1)
                for h in range(H):
                    if h >= 2:
                        pe.wait_ge(nmb_ready, h - 1)
                    mm(ps[:, 6 + h % 2, :], head_sel[:, h, :], gat[0:H, 1, :], start=True, stop=True).then_inc(nmb_mm, 1)

            def mem_core(h, following):
                pe.wait_ge(proj_out, N_MEM * h + 6)
                pe.wait_ge(mem_ready, 2 * h)
                for i in range(NT):
                    for u in range(2):
                        last = tr(ps[:, 2 + i // 2, (i % 2) * MDH + u * P:(i % 2) * MDH + (u + 1) * P],
                                  mvraw[:, u, i * P:(i + 1) * P], ident[:])
                    if i % 2:
                        last.then_inc(mv_T, 1)
                pe.wait_ge(qk_ready, h + 1)
                for j in range(NT):
                    pe.wait_ge(at_ready, NT * h + j - 1 if j > 0 else NT * h)
                    for c in range(2):
                        last = mm(ps[:, 4 + j % 2, j * P:T], qkf[:, 2 + c, j * P:(j + 1) * P], qkf[:, c, j * P:T],
                                  start=(c == 0), stop=(c == 1))
                    last.then_inc(at_mm, 1)
                    if j == 1:
                        following(0)
                pe.wait_ge(vN_ready, 2 * (h + 1))
                for i in range(NT):
                    pe.wait_ge(at_ready, NT * h + i + 1)
                    if i >= 2:
                        pe.wait_ge(num_out, NT * h + i - 1)
                    for j in range(i + 1):
                        last = mm(ps[:, 6 + i % 2, 0:VN], AT[:, j, i * P:(i + 1) * P], vN[:, j, :], start=(j == 0), stop=(j == i))
                    last.then_inc(num_mm, 1)
                following(1)
                for i in range(NT):
                    pe.wait_ge(hn_ready, NT * h + i + 1)
                    for c in range(2):
                        last = tr(ps[:, 2 + c, i * P:(i + 1) * P], hh[:, i, c * P:(c + 1) * P], ident[:])
                last.then_inc(hn_T, 1)

            for j in range(4):
                mem_tile(0, j)
            mem_gates()
            for j in range(4, N_MEM):
                mem_tile(0, j)
            pe.wait_ge(nmb_ready, H)
            pe.wait_ge(gate_cols, 2)
            mem_core(0, lambda n: mem_tile(1, n))
            with pe.Fori(1, H - 1) as h:
                for j in range(2, N_MEM):
                    mem_tile(h, j)
                mem_core(h, lambda n: mem_tile(h + 1, n))
            for j in range(2, N_MEM):
                mem_tile(H - 1, j)

            def att_tile(h, j):
                pe.wait_ge(proj_out, ATT0 + N_ATT * h + j - (1 if j else 0))
                project(ATT0 + N_ATT * h + j, j % 3, j % 2)

            def att_head(h, following):
                def scores(r):
                    b = 2 + 2 * (r % 2)
                    pe.wait_ge(smax_ready, NT * h + r - 1 if r else NT * h)
                    q = lambda g: qk[:, g, r:T:NT]
                    mm(ps[:, b, :], q(0), qk[:, G, :], start=True, stop=True)
                    mm(ps[:, b + 1, 0:P], q(1), qk[:, G + 1, r:T:NT], start=True, stop=True)
                    mm(ps[:, b + 1, P:2 * P], q(2), qk[:, G + 2, r:T:NT], start=True, stop=True).then_inc(s_mm, 1)

                for j in range(4, N_ATT - 1):
                    att_tile(h, j)
                pe.wait_ge(rot_ready, 2 * (h + 1))
                scores(0)
                pe.wait_ge(smax_ready, NT * h)
                scores(1)
                att_tile(h, N_ATT - 1)
                pe.wait_ge(pT_act, NT * h)
                pe.wait_ge(att_ready, NT * h)
                for g, bank in enumerate((6, 7, 6)):
                    pe.wait_ge(proj_out, ATT0 + N_ATT * h + 2 * G + g + 1)
                    if g == 2:
                        pe.wait_ge(vh_ready, G * h + 1)
                    for i in range(NT):
                        src = avraw[:, g, i * P:(i + 1) * P] if g == 0 else avraw[:, g, i:T:NT]
                        last = tr(ps[:, bank, i * P:(i + 1) * P], src, ident[:])
                    last.then_inc(av_T, 1)
                    if g == 1:
                        scores(2)
                scores(3)
                pe.wait_ge(vh_ready, G * (h + 1))
                for r in range(NT):
                    pe.wait_ge(pr_ready, NT * h + r + 1)
                    for m in range(6):
                        if m == 4:
                            pe.wait_ge(att_ready, NT * h + r)
                        last = tr(ps[:, 6 + m // 4, (m % 4) * P:(m % 4 + 1) * P], pr[:, r % 2, m * P:(m + 1) * P], ident[:])
                        if m == 3:
                            last.then_inc(pr_T, 1)
                    last.then_inc(pr_T, 1)
                    following(r)
                    pe.wait_ge(pT_act, NT * h + r + 1)
                    pe.wait_ge(pT_dve, NT * h + r + 1)
                    for m in range(6):
                        v = vh[:, 0, m, :] if m < NT else vh[:, m - NT + 1, r, :]
                        last = mm(ps[:, 7, (2 + r % 2) * P:(3 + r % 2) * P], v, pT[:, m, :], start=(m == 0), stop=(m == 5))
                    last.then_inc(pv_mm, 1)

            def first_gates(r):
                if r < 2:
                    pe.wait_ge(proj_out, ATT0 + N_ATT * H)
                    project(MRG0 + r, r, r)

            mem_core(H - 1, lambda n: att_tile(0, n))
            att_tile(0, 2)
            att_tile(0, 3)
            pe.wait_ge(mem_ready, 2 * H)
            pe.wait_ge(at_ready, NT * H)
            pe.wait_ge(num_out, NT * H)
            att_head(0, lambda r: att_tile(1, r))
            with pe.Fori(1, H - 1) as h:
                att_head(h, lambda r: att_tile(h + 1, r))
            att_head(H - 1, first_gates)

            def merge_step(b, first=False):
                for t in range(2 if first else 0, N_MRG):
                    if t < 4:
                        pe.wait_ge(sg_ready, 4 * b)
                        rh, rl, nk = xh, xl, KD
                    else:
                        pe.wait_ge(merged, 2 * b)
                        rh, rl, nk = (memR, memL, KD) if t % 2 else (attR, attL, H)
                        pe.wait_ge(am_split, 3 if t % 2 else 1)
                    project(MRG0 + N_MRG * b + t, t % 4, t, rh, rl, nk)

            pe.wait_ge(att_ready, NT * H)
            merge_step(0, first=True)
            with pe.Fori(1, KD // 2) as b:
                merge_step(b)
            pe.wait_ge(merged, KD)

            def mix(i):
                for n in range(2):
                    if i >= 2:
                        pe.wait_ge(h_ready, 2 * (i - 2) + n + 1)
                    cols = slice(n * BANK, (n + 1) * BANK)
                    for k in range(KD):
                        if i == 0 and n == 0:
                            pe.wait_ge(wmix_in[k], DMA)
                        w = wmix0[:, k, cols] if k < KD - 2 else wmix1[:, k - KD + 2, cols]
                        last = mm(ps[:, 4 + 2 * (i % 2) + n, :], mergedT[:, k, i * P:(i + 1) * P], w, start=(k == 0), stop=(k == KD - 1))
                    last.then_inc(mix_mm, 1)

            def normed_T(i):
                pe.wait_ge(hw_ready, i + 1)
                for b in range(2):
                    if i:
                        pe.wait_ge(xn2T_ready, 2 * (i - 1) + b + 1)
                    for k in range(4):
                        last = tr(ps[:, b, k * P:(k + 1) * P], xw2[:, i % 2, (4 * b + k) * P:(4 * b + k + 1) * P], ident[:])
                    last.then_inc(hw_used, 1)

            def logits(i):
                if i == 0:
                    pe.wait_ge(router_in, 3 * DMA)
                pe.wait_ge(xn2T_ready, 2 * (i + 1))
                if i >= 2:
                    pe.wait_ge(lg_read, i - 1)
                for k in range(KD):
                    last = mm(ps[:, 2 + i % 2, 0:E], xn2T[:, k, i * P:(i + 1) * P], wr[:, k, :], start=(k == 0), stop=(k == KD - 1))
                last.then_inc(lg_mm, 1)

            mix(0)
            mix(1)
            normed_T(0)
            mix(2)
            normed_T(1)
            logits(0)
            mix(3)
            normed_T(2)
            logits(1)
            normed_T(3)
            logits(2)
            logits(3)
            pe.wait_ge(late_tables, 1)
            pe.wait_ge(memb_ready, 1)
            pe.wait_ge(h_ready, 2 * NT)
            for i in range(NT):
                for j in range(i):
                    mm(ps[:, 5, i * E:(i + 1) * E], onesb[:], memb[:, j, :], start=(j == 0), stop=False)
                mm(ps[:, 5, i * E:(i + 1) * E], tri[:], memb[:, i, :], start=(i == 0), stop=True)
            for j in range(NT):
                last = mm(ps[:, 5, NT * E:(NT + 1) * E], onesb[:], memb[:, j, :], start=(j == 0), stop=(j == NT - 1))
            last.then_inc(pos_mm, 1)

            GUB, DNB, TB0, TB1 = 0, 4, 7, 6

            def slots_of(m):
                pe.wait_ge(sel_ready, NT * (m + 1))
                for i in range(NT):
                    last = mm(ps[:, TB1, 0:4], sels[:, i, :], te[:, i, :], start=(i == 0), stop=(i == NT - 1))
                last.then_inc(meta_mm, 1)

            def rows_T(m, xi):
                pe.wait_ge(gathered, DMA * (xi + 1))
                for b, bank in enumerate((TB0, TB1)):
                    if b == 1:
                        pe.wait_ge(meta_ready, 2 * (m + 1))
                    for k in range(4):
                        last = tr(ps[:, bank, k * P:(k + 1) * P], xg[:, (4 * b + k) * P:(4 * b + k + 1) * P], ident[:])
                    last.then_inc(xg_T, 1)

            def gate_up(e, xi, gi):
                pe.wait_ge(xT_ready, 2 * (xi + 1))
                pe.wait_ge(up_read, gi)
                for n in range(4):
                    mm(ps[:, GUB + n, :], sel[:, bass.ds(e, 1), :].rearrange("p a s -> p (a s)"), bsp[:, n * BANK:(n + 1) * BANK],
                       start=True, stop=False)
                for k in range(KD):
                    pe.wait_ge(gu_split, KD * gi + k + 1)
                    for n in range(4):
                        cols = slice(n * BANK, (n + 1) * BANK)
                        mm(ps[:, GUB + n, :], xTh[:, k, :], guh[k % 4][:, cols], start=False, stop=False)
                        mm(ps[:, GUB + n, :], xTh[:, k, :], gul[:, k, cols], start=False, stop=False)
                    for n in range(4):
                        last = mm(ps[:, GUB + n, :], xTl[:, k, :], guh[k % 4][:, n * BANK:(n + 1) * BANK], start=False, stop=(k == KD - 1))
                    last.then_inc(gu_used, 1)

            def down(e, gi):
                pe.wait_ge(actT_ready, 2 * (gi + 1))
                pe.wait_ge(y_ready, 2 * gi)
                for n in range(2):
                    mm(ps[:, DNB + n, :], sel[:, bass.ds(e, 1), :].rearrange("p a s -> p (a s)"),
                       bsp[:, F2 + n * BANK:F2 + (n + 1) * BANK], start=True, stop=False)
                for k in range(KD):
                    if k % 2 == 0:
                        pe.wait_ge(dn_in[k // 2], DMA * (gi + 1))
                    for n in range(2):
                        last = mm(ps[:, DNB + n, :], actT[:, k, :], dnw[:, k, n * BANK:(n + 1) * BANK], start=False, stop=(k == KD - 1))
                    if k % 2:
                        last.then_inc(dn_used, 1)

            def act_rows_T(gi, xi):
                pe.wait_ge(act_ready, gi + 1)
                pe.wait_ge(xT_ready, 2 * (xi + 1))
                for b, bank in enumerate((TB0, TB1)):
                    for k in range(4):
                        last = tr(ps[:, bank, k * P:(k + 1) * P], act[:, (4 * b + k) * P:(4 * b + k + 1) * P], ident[:])
                    last.then_inc(act_T, 1)

            pe.wait_ge(bias_ready, 1)
            slots_of(0)
            rows_T(0, 0)
            pe.wait_ge(xT_ready, 2)
            slots_of(1)
            gate_up(0, 0, 0)
            pe.wait_ge(meta_ready, 4)
            slots_of(2)
            rows_T(2, 1)
            act_rows_T(0, 1)

            def expert_turn(e):
                gate_up(e, e, e)
                pe.wait_ge(actT_ready, 2 * e)
                slots_of(e + 2)
                rows_T(e + 2, e + 1)
                down(e - 1, e - 1)
                act_rows_T(e, e + 1)

            expert_turn(1)
            with pe.Fori(2, E) as e:
                expert_turn(e)
            down(E - 1, E - 1)
            with pe.If(many(pe) > 0):
                with pe.Fori(1, NT) as b:
                    with pe.Fori(0, E) as e:
                        n = extra(b, e)
                        slots_of(E + 2 + n)
                        rows_T(E + 2 + n, E + 1 + n)
                        gate_up(e, E + 1 + n, E + n)
                        act_rows_T(E + n, E + 1 + n)
                        down(e, E + n)

        @block.scalar
        def _(sc):
            own = Chain(sc, act_step)
            a = nc.scalar.activation

            def std(n, i, ready, count, junk, square, done):
                sc.wait_ge(ready, count)
                if i:
                    sc.wait_ge(square, i)
                a(junk, hres[:, i, :], ACT.Square, accum_out=ssq[:, n, i:i + 1]).then_inc(square, 1)
                sc.wait_ge(square, i + 1)
                a(ssq[:, n, i:i + 1], ssq[:, n, i:i + 1], ACT.Sqrt, scale=1.0 / D, bias=eps[:, 0:1]).then_inc(done, 1)

            sc.wait_ge(tables, made["ident"])
            for i in range(NT):
                std(0, i, x_in[i], DMA, ps[:, 4:6, :].rearrange("p b n -> p (b n)"), x_square, x_std)
            sc.wait_ge(wif_in, 2 * DMA)
            nc.scalar.copy(wifh[:], wif[:]).then_inc(wif_round, 1)
            for n in range(2 * NT):
                sc.wait_ge(xt_ready, n + 1)
                nc.scalar.copy(xh[:, 4 * (n % 2):4 * (n % 2) + 4, (n // 2) * P:(n // 2 + 1) * P],
                               xt[:, n % 2, :].rearrange("p (k c) -> p k c", k=4)).then_inc(xh_ready, 1)

            def round_tile(slot, uses):
                sc.wait_ge(w_in_slot[slot], DMA * uses)
                nc.scalar.copy(split(slot)[:, 0, :], wraw[:, slot, :]).then_inc(rounded, 1)

            def next_of_mem(h, j):
                j = j + 3
                if j < N_MEM:
                    round_tile(j % 4, 2 * h + j // 4 + 1)
                else:
                    round_tile(j - N_MEM, 2 * h + 3)

            def next_of_att(h, j):
                j = j + 3
                if j < N_ATT:
                    round_tile(j % 3, 2 * H + 3 * h + j // 3 + 1)
                else:
                    round_tile(j - N_ATT, 2 * H + 3 * h + 4)

            def next_of_merge(b, t, last):
                t = t + 3
                if t >= N_MRG and last:
                    return
                if t >= N_MRG:
                    b, t = b + 1, t - N_MRG
                s = t % 4
                round_tile(s, (2 * H if s == 3 else 5 * H) + 2 * b + t // 4 + 1)

            round_tile(0, 1)
            round_tile(1, 1)
            sc.wait_ge(xw_ready, NT)
            round_tile(2, 1)
            sc.wait_ge(angle_ready, 2)
            a(rcos[:], ang[:, 1, :], ACT.Sin).then_inc(sines_ready, 1)
            a(rsin[:], ang[:, 2, :], ACT.Sin).then_inc(sines_ready, 1)
            sc.wait_ge(gate_abs, 1)
            own.step(a(gat[0:H, 2, :], gat[0:H, 2, :], ACT.Exp))
            a(gat[0:H, 2, :], gat[0:H, 2, :], ACT.Ln, bias=1.0).then_inc(gate_ln, 1)

            def mem_out(h, j):
                sc.wait_ge(w_used, N_MEM * h + j + 1)
                if j < 4:
                    sc.wait_ge(conv_ready, 4 * h)
                    nc.scalar.copy(raw[:, j, TAPS - 1:], ps[:, j % 2, :]).then_inc(proj_out, 1)
                elif j < 6:
                    sc.wait_ge(mv_T, 2 * h)
                    nc.scalar.copy(mvraw[:, j - 4, :], ps[:, j % 2, :]).then_inc(proj_out, 1)
                else:
                    sc.wait_ge(mem_ready, 2 * h)
                    a(sgo[:, j - 6, :], ps[:, j % 2, :], ACT.Sigmoid).then_inc(proj_out, 1)
                next_of_mem(h, j)

            def mem_head(h, following, first=False):
                for j in range(2, 4):
                    mem_out(h, j)
                if first:
                    sc.wait_ge(gate_cols, 1)
                    a(expE[:], ceT[:, :, 32:32 + H], ACT.Exp).then_inc(gate_cols, 1)
                    sc.wait_ge(sines_done, 1)
                    for n in range(H):
                        sc.wait_ge(nmb_mm, n + 1)
                        nc.scalar.copy(nmb[:, n, :], ps[:, 6 + n % 2, :]).then_inc(nmb_ready, 1)
                for j in range(4, 6):
                    mem_out(h, j)
                sc.wait_ge(conv_ready, 4 * (h + 1))
                sc.wait_ge(at_mm, NT * h)
                a(qkf[:], cv[:], ACT.Silu).then_inc(qk_ready, 1)
                for j in range(6, 8):
                    mem_out(h, j)
                sc.wait_ge(cols_ready, 3 * (h + 1))
                sc.wait_ge(at_ready, NT * h)
                for j in range(NT):
                    a(wexp[:, j, j * P:(j + 1) * P], nmd[:, j * P:(j + 1) * P], ACT.Exp, bias=ch[:, j:j + 1]).then_inc(wexp_ready, 1)
                    if j < NT - 1:
                        a(wexp[:, j, (j + 1) * P:T], nmb[:, bass.ds(h, 1), (j + 1) * P:T].rearrange("p a t -> p (a t)"),
                          ACT.Exp, bias=ch[:, j:j + 1]).then_inc(wexp_ready, 1)
                for b in range(2):
                    sc.wait_ge(mv_T, 2 * h + b + 1)
                    sc.wait_ge(num_mm, NT * h)
                    nc.scalar.copy(vN[:, 2 * b:2 * b + 2, 0:MDH], ps[:, 2 + b, :].rearrange("p (i c) -> p i c", i=2)).then_inc(vN_ready, 1)
                following(0)
                sc.wait_ge(hvar_ready, h + 1)
                a(mrs[:, 0, :], mrs[:, 0, :], ACT.Sqrt).then_inc(hstd_ready, 1)
                following(1)

            def att_out(h, j):
                sc.wait_ge(w_used, ATT0 + N_ATT * h + j + 1)
                dst = qk[:, j, :] if j < 2 * G else avraw[:, j - 2 * G, :]
                nc.scalar.copy(dst, ps[:, j % 2, :]).then_inc(proj_out, 1)
                next_of_att(h, j)

            def att_head(h, following):
                def weights(r):
                    sc.wait_ge(smax_ready, NT * h + r + 1)
                    a(pr[:, r % 2, :], sm[:, r % 2, :], ACT.Exp, bias=smax[:, r % 2, 1:2], scale=QK_SCALE,
                      accum_out=smax[:, r % 2, 2:3]).then_inc(exp_ready, 1)

                for j in range(4, N_ATT - 1):
                    att_out(h, j)
                weights(0)
                att_out(h, N_ATT - 1)
                weights(1)
                for g, bank in enumerate((6, 7, 6)):
                    sc.wait_ge(av_T, G * h + g + 1)
                    nc.scalar.copy(vh[:, g, :, :].rearrange("p i c -> p (i c)"), ps[:, bank, :]).then_inc(vh_ready, 1)
                for r in range(NT):
                    sc.wait_ge(pr_T, 2 * (NT * h + r) + 1)
                    nc.scalar.copy(pT[:, 0:4, :].rearrange("p m c -> p (m c)"), ps[:, 6, :]).then_inc(pT_act, 1)
                    if r + 2 < NT:
                        sc.wait_ge(pr_T, 2 * (NT * h + r + 1))
                        weights(r + 2)
                    following(r)

            def gate_out(b, t, last=False):
                sc.wait_ge(w_used, MRG0 + N_MRG * b + t + 1)
                sc.wait_ge(merged, 2 * b)
                a(sgm[:, t // 2, t % 2, :], ps[:, t, :], ACT.Sigmoid).then_inc(sg_ready, 1)
                next_of_merge(b, t, last)

            def merge_step(b, first=False, last=False):
                for t in range(2 if first else 0, 4):
                    gate_out(b, t, last)
                for t in range(4, N_MRG):
                    sc.wait_ge(w_used, MRG0 + N_MRG * b + t)
                    next_of_merge(b, t, last)

            for j in range(2):
                mem_out(0, j)
            mem_head(0, lambda n: mem_out(1, n), first=True)
            with sc.Fori(1, H - 1) as h:
                mem_head(h, lambda n: mem_out(h + 1, n))
            mem_head(H - 1, lambda n: att_out(0, n))
            for j in range(2, 4):
                att_out(0, j)
            att_head(0, lambda r: att_out(1, r))
            with sc.Fori(1, H - 1) as h:
                att_head(h, lambda r: att_out(h + 1, r))
            att_head(H - 1, lambda r: gate_out(0, r) if r < 2 else None)
            sc.wait_ge(att_ready, NT * H)
            nc.scalar.copy(attR[:], attT[:]).then_inc(am_round, 1)
            for c in range(2):
                nc.scalar.copy(memR[:, 4 * c:4 * c + 4, :], memT[:, 4 * c:4 * c + 4, :]).then_inc(am_round, 1)
            merge_step(0, first=True)
            with sc.Fori(1, KD // 2 - 1) as b:
                merge_step(b)
            merge_step(KD // 2 - 1, last=True)

            for i in range(NT):
                std(1, i, h_ready, 2 * (i + 1), yw[:], h_square, h_std)
                sc.wait_ge(hw_ready, i + 1)
                nc.scalar.dma_start(xn_v[:, i, :], xw2[:, i % 2, :]).then_inc(xn_stored[i], DMA)
            sc.wait_ge(top_ready, 1)
            a(gk[:], gk[:], ACT.Exp).then_inc(gk_ready, 1)

            def round_chunk(gi, k):
                sc.wait_ge(gu_in[k], DMA * (gi + 1))
                if not isinstance(gi, int) or gi or k >= 4:
                    sc.wait_ge(gu_used, KD * gi + k - 3)
                nc.scalar.copy(guh[k % 4][:], guw[:, k, :]).then_inc(gu_rounded, 1)

            def rows(xi):
                for b, bank in enumerate((7, 6)):
                    sc.wait_ge(xg_T, 2 * xi + b + 1)
                    nc.scalar.copy(xTh[:, 4 * b:4 * b + 4, :].rearrange("p k c -> p (k c)"), ps[:, bank, :]).then_inc(xTh_ready, 1)

            def sigmoid(gi):
                sc.wait_ge(gt_ready, gi + 1)
                a(sg[:], gt[:], ACT.Sigmoid, scale=SWIGLU_ALPHA).then_inc(sg_ready2, 1)

            def weighted(e, gi):
                sc.wait_ge(y_ready, 2 * gi)
                own.step(nc.scalar.copy(gcur[:], gate_of[:, bass.ds(e, 1)]))
                sc.wait_ge(dn_used, (KD // 2) * (gi + 1))
                sc.wait_ge(y_stored, DMA * gi)
                for n in range(2):
                    nc.scalar.mul(yw[:, n * BANK:(n + 1) * BANK], ps[:, 4 + n, :], gcur[:, 0:1]).then_inc(y_ready, 1)

            def act_rows(gi):
                for b, bank in enumerate((7, 6)):
                    sc.wait_ge(act_T, 2 * gi + b + 1)
                    nc.scalar.copy(actT[:, 4 * b:4 * b + 4, :].rearrange("p k c -> p (k c)"), ps[:, bank, :]).then_inc(actT_ready, 1)

            def expert_turn(e, first=False, last=False):
                for k in range(4, KD):
                    round_chunk(e, k)
                if not last:
                    for k in range(3):
                        round_chunk(e + 1, k)
                sigmoid(e)
                rows(e + 1)
                if not last:
                    round_chunk(e + 1, 3)
                if not first:
                    weighted(e - 1, e - 1)
                act_rows(e)

            sc.wait_ge(lg_mm, NT)
            for i in range(NT):
                sc.wait_ge(xn_stored[i], DMA)
            for k in range(4):
                round_chunk(0, k)
            rows(0)
            expert_turn(0, first=True)
            expert_turn(1)
            with sc.Fori(2, E - 1) as e:
                own.begin(e - 2, 1)
                expert_turn(e)
                own.end(E - 3)
            expert_turn(E - 1, last=True)
            weighted(E - 1, E - 1)
            with sc.If(many(sc) > 0):
                common, own = own, Chain(sc, act_over)
                with sc.Fori(1, NT) as b:
                    with sc.Fori(0, E) as e:
                        n = extra(b, e)
                        own.begin(n, 1)
                        rows(E + 1 + n)
                        for k in range(KD):
                            round_chunk(E + n, k)
                        sigmoid(E + n)
                        act_rows(E + n)
                        weighted(e, E + n)
                        own.end((NT - 1) * E)
                own = common
            for i in range(NT):
                std(2, i, f_sum, i + 1, ps[:, 0:2, :].rearrange("p b n -> p (b n)"), f_square, f_std)

        @block.vector
        def _(dve):
            own = Chain(dve, dve_step)
            v = nc.vector
            tt, ts, stt = v.tensor_tensor, v.tensor_scalar, v.scalar_tensor_tensor

            dve.wait_ge(vecT_done, 2)
            own.mark(v.tensor_copy(vecT[:], ps[:, 7, 0:88]))
            own.mark(v.tensor_copy(fcol[:], ps[:, 6, 0:2]))
            own.settle()
            four = lambda t: t.rearrange("p (k c) -> p k c", k=4)

            def x_rest(n):
                dve.wait_ge(xh_ready, n + 1)
                at = (slice(None), slice(4 * (n % 2), 4 * (n % 2) + 4), slice((n // 2) * P, (n // 2 + 1) * P))
                tt(xl[at], four(xt[:, n % 2, :]), xh[at], ALU.subtract).then_inc(xnT_ready, 1)

            for i in range(NT + 1):
                if i >= 2:
                    dve.wait_ge(xw_used, 2 * (i - 1))
                if i < NT:
                    dve.wait_ge(x_std, i + 1)
                    own.step(v.reciprocal(rstd[:, 0, i:i + 1], ssq[:, 0, i:i + 1]))
                    ts(xw[:, i % 2, :], hres[:, i, :], rstd[:, 0, i:i + 1], None, ALU.mult).then_inc(xw_ready, 1)
                if i == 0:
                    continue
                for n in (2 * i - 2, 2 * i - 1):
                    dve.wait_ge(xw_used, n + 1)
                    if n >= 2:
                        dve.wait_ge(xnT_ready, n - 1)
                    tt(four(xt[:, n % 2, :]), ps[:, n % 4, :].rearrange("p (k c) -> p k c", k=4),
                       vecT[:, GMIX + 4 * (n % 2):GMIX + 4 * (n % 2) + 4].unsqueeze(2).to_broadcast([P, 4, P]), ALU.mult).then_inc(xt_ready, 1)
                    if n == 0:
                        dve.wait_ge(wif_round, 1)
                        tt(wifl[:], wif[:], wifh[:], ALU.subtract).then_inc(wif_split, 1)
                    else:
                        x_rest(n - 1)
            x_rest(2 * NT - 1)
            TWO_PI = 2.0 * float(np.pi)
            C1 = 6.28125
            C2 = float(np.float32(np.round((TWO_PI - C1) * 2 ** 21) / 2 ** 21))
            C3 = TWO_PI - C1 - C2
            MAGIC = 1.5 * 2 ** 23
            TOP = 3.1415925
            dve.wait_ge(pos_in, DMA)
            own.step(ts(ang[:, 0, :], post[:], fcol[0:ROT, 0:1], None, ALU.mult))
            turns = rcos
            for n, (shift, offset) in enumerate(((0.25, float(np.pi) / 2), (0.0, 0.0))):
                a1 = ang[:, n + 1, :]
                own.step(ts(turns[:], ang[:, 0, :], 1.0 / TWO_PI, shift, ALU.mult, ALU.add))
                own.step(ts(turns[:], turns[:], MAGIC, None, ALU.add))
                own.step(ts(turns[:], turns[:], MAGIC, None, ALU.subtract))
                own.step(stt(a1, turns[:], -C1, ang[:, 0, :], ALU.mult, ALU.add))
                own.step(stt(a1, turns[:], -C2, a1, ALU.mult, ALU.add))
                own.step(stt(a1, turns[:], -C3, a1, ALU.mult, ALU.add))
                own.step(ts(a1, a1, offset, TOP, ALU.add, ALU.min))
                ts(a1, a1, -TOP, None, ALU.max).then_inc(angle_ready, 1)

            R = slice(0, H)
            R2 = slice(32, 32 + H)
            dve.wait_ge(gate_mm, 1)
            dve.wait_ge(bif_in, 2 * DMA)
            own.mark(ts(gat[R, 0, :], ps[R, 4, :], bcol[R, 0:1], None, ALU.add))
            own.step(ts(gat[R, 1, :], ps[R2, 4, :], bcol[R2, 0:1], None, ALU.add))
            stt(gat[R, 2, :], gat[R, 1, :], -1.0, gat[R, 1, :], ALU.mult, ALU.min).then_inc(gate_abs, 1)
            dve.wait_ge(gate_ln, 1)
            own.step(stt(gat[R, 1, :], gat[R, 1, :], 0.0, gat[R, 2, :], ALU.min, ALU.subtract))
            own.step(v.tensor_tensor_scan(gat[R, 2, :], ones_row[:], gat[R, 1, :], 0.0, ALU.mult, ALU.add))
            dve.wait_ge(tables, made["ce"])
            own.step(tt(ce[R, :], gat[R, 0, :], gat[R, 2, :], ALU.subtract))
            own.step(v.tensor_tensor_scan(gat[R, 0, :], ones_row[:], ce[R, :], 0.0, ALU.mult, ALU.max))
            stt(ce[R2, :], gat[R, 2, :], -1.0, gat[R, 0, :], ALU.mult, ALU.subtract).then_inc(gate_rows, 1)
            ts(gat[R, 1, :], gat[R, 0, :], -1.0, None, ALU.mult).then_inc(gate_rows, 1)
            dve.wait_ge(sines_ready, 2)
            ts(rsin[:], rsin[:], fcol[0:ROT, 1:2], None, ALU.mult).then_inc(sines_done, 1)

            dve.wait_ge(m4_made, 1)
            own.step(ts(m4[:], m4[:], 3, None, ALU.bitwise_and))
            ts(amask[:, :, T + P:SC], m4[:].unsqueeze(1).to_broadcast([P, NT, P]), NEG, None, ALU.mult).then_inc(m4_ready, 1)
            WEXPS = 2 * NT - 1

            def mem_head(h, first=False):
                dve.wait_ge(wexp_ready, WEXPS * h)
                dve.wait_ge(mem_ready, 2 * h)
                cols = vecT[:, 0:GMIX].rearrange("p (t c) -> p t c", t=TAPS)
                own.mark(v.tensor_copy(cwh[:, :, 0:2], cols[:, :, bass.ds(2 * h, 2)]))
                own.mark(v.tensor_copy(cwh[:, :, 2:4], cols[:, :, bass.ds(KD + 2 * h, 2)]))
                own.mark(v.tensor_copy(gmh[:], vecT[:, bass.ds(GMEM + 2 * h, 2)]))
                own.settle()
                dve.wait_ge(qk_ready, h)
                for j in range(4):
                    dve.wait_ge(proj_out, N_MEM * h + j + 1)
                    own.step(ts(cv[:, j, :], raw[:, j, 0:T], cwh[:, 0, j:j + 1], None, ALU.mult))
                    for t in range(1, TAPS):
                        ins = stt(cv[:, j, :], raw[:, j, t:t + T], cwh[:, t, j:j + 1], cv[:, j, :], ALU.mult, ALU.add)
                        if t < TAPS - 1:
                            own.step(ins)
                        else:
                            ins.then_inc(conv_ready, 1)
                if first:
                    dve.wait_ge(gate_T, 1)
                    v.tensor_copy(ceT[:].rearrange("p i c -> p (i c)"), ps[:, 5, 0:NT * 64]).then_inc(gate_cols, 1)
                    dve.wait_ge(gate_cols, 2)
                    dve.wait_ge(nmb_ready, H)
                    dve.wait_ge(tables, made["cmask"])
                v.tensor_copy(ch[:], ceT[:, :, bass.ds(h, 1)].rearrange("p i a -> p (i a)")).then_inc(cols_ready, 1)
                v.tensor_copy(eh[:], expE[:, :, bass.ds(h, 1)].rearrange("p i a -> p (i a)")).then_inc(cols_ready, 1)
                tt(nmd[:].rearrange("p (i t) -> p i t", i=NT), nmb[:, bass.ds(h, 1), :].rearrange("p a (i t) -> p (a i) t", i=NT),
                   cmask[:].unsqueeze(1).to_broadcast([P, NT, P]), ALU.add).then_inc(cols_ready, 1)
                dve.wait_ge(cols_ready, 3 * (h + 1))
                dve.wait_ge(wexp_ready, WEXPS * (h + 1))
                for j in range(NT):
                    dve.wait_ge(at_mm, NT * h + j + 1)
                    stt(AT[:, j, j * P:T], ps[:, 4 + j % 2, j * P:T], MK_SCALE, wexp[:, j, j * P:T],
                        ALU.mult, ALU.mult).then_inc(at_ready, 1)
                for i in range(NT):
                    dve.wait_ge(num_mm, NT * h + i + 1)
                    num = ps[:, 6 + i % 2, :]
                    own.step(ts(den[:, 0, i:i + 1], num[:, MDH:MDH + 1], eh[:, i:i + 1], None, ALU.max))
                    own.step(stt(den[:, 0, i:i + 1], num[:, MDH:MDH + 1], -1.0, den[:, 0, i:i + 1], ALU.mult, ALU.max))
                    own.step(v.reciprocal(den[:, 1, i:i + 1], den[:, 0, i:i + 1]))
                    ts(hh[:, i, :], num[:, 0:MDH], den[:, 1, i:i + 1], None, ALU.mult).then_inc(num_out, 1)
                    dve.wait_ge(num_out, NT * h + i + 1)
                    own.mark(v.bn_stats(bst[:, i, :], hh[:, i, :]))
                own.settle()
                v.memset(mrs[:], 0.0)
                for i in range(NT):
                    own.mark(v.bn_aggr(mv[:, i, :], bst[:, i, :]))
                own.settle()
                ts(mrs[:, 0, :], mv[:, :, 1], LN_EPS, None, ALU.add).then_inc(hvar_ready, 1)
                dve.wait_ge(hstd_ready, h + 1)
                own.step(v.reciprocal(mrs[:, 1, :], mrs[:, 0, :]))
                for i in range(NT):
                    ts(hh[:, i, :], hh[:, i, :], mv[:, i, 0:1], mrs[:, 1, i:i + 1], ALU.subtract, ALU.mult).then_inc(hn_ready, 1)
                dve.wait_ge(hn_T, h + 1)
                for c in range(2):
                    stt(memT[:, bass.ds(2 * h + c, 1), :].rearrange("p a t -> p (a t)"), ps[:, 2 + c, :], gmh[:, c:c + 1], sgo[:, c, :],
                        ALU.mult, ALU.mult).then_inc(mem_ready, 1)

            own.begin(0, 36)
            mem_head(0, first=True)
            own.end(1)
            with dve.Fori(1, H) as h:
                own.begin(h - 1, 36)
                mem_head(h)
                own.end(H - 1)

            def att_head(h, beside=lambda r: None):
                swap = [(i + HALF) % ROT for i in range(ROT)]
                flat = lambda t: t.rearrange("p g t -> p (g t)")

                def rotate(j0, j1):
                    dve.wait_ge(proj_out, ATT0 + N_ATT * h + j1)
                    rows, turned = qk[0:ROT, j0:j1, :], rs[:, j0:j1, :]
                    v.memset(tick[:], 0.0)
                    own.step(v.stream_shuffle(flat(turned), flat(rows), swap))
                    own.mark(tt(turned, turned, rsin[:].unsqueeze(1).to_broadcast([ROT, j1 - j0, T]), ALU.mult))
                    own.step(tt(rows, rows, rcos[:].unsqueeze(1).to_broadcast([ROT, j1 - j0, T]), ALU.mult))
                    tt(rows, rows, turned, ALU.add).then_inc(rot_ready, 1)

                rotate(0, 4)
                rotate(4, 2 * G)

                def masked(r):
                    dve.wait_ge(s_mm, NT * h + r + 1)
                    b = 2 + 2 * (r % 2)
                    v.memset(tick[:], 0.0)
                    own.step(v.tensor_tensor_reduce(out=sm[:, r % 2, :], in0=ps[:, b:b + 2, :].rearrange("p b t -> p (b t)")[:, 0:SC],
                                                    in1=amask[:, r, :], scale=1.0, scalar=NEG, op0=ALU.add, op1=ALU.max,
                                                    accum_out=smax[:, r % 2, 0:1]))
                    ts(smax[:, r % 2, 1:2], smax[:, r % 2, 0:1], -QK_SCALE, None, ALU.mult).then_inc(smax_ready, 1)

                def weights(r):
                    dve.wait_ge(exp_ready, NT * h + r + 1)
                    own.step(v.reciprocal(smax[:, r % 2, 3:4], smax[:, r % 2, 2:3]))
                    ts(pr[:, r % 2, :], pr[:, r % 2, :], smax[:, r % 2, 3:4], None, ALU.mult).then_inc(pr_ready, 1)

                def probs_T(r):
                    dve.wait_ge(pr_T, 2 * (NT * h + r + 1))
                    v.tensor_copy(pT[:, 4:6, :].rearrange("p m c -> p (m c)"), ps[:, 7, 0:2 * P]).then_inc(pT_dve, 1)

                def out(r):
                    dve.wait_ge(pv_mm, NT * h + r + 1)
                    v.tensor_copy(attT[:, bass.ds(h, 1), r:T:NT].rearrange("p a t -> p (a t)"),
                                  ps[:, 7, (2 + r % 2) * P:(3 + r % 2) * P]).then_inc(att_ready, 1)

                masked(0)
                masked(1)
                weights(0)
                masked(2)
                weights(1)
                masked(3)
                for r in range(NT):
                    probs_T(r)
                    out(r)
                    if r + 2 < NT:
                        weights(r + 2)
                    beside(r)

            def split_bias(r):
                hi, lo = slice(64, P), slice(96, P)
                if r == 0:
                    dve.wait_ge(tables, made["sel"])
                    dve.wait_ge(brow_in, 6 * DMA)
                    own.mark(v.tensor_copy(bsp[0:E], brow[0:E]))
                    own.step(v.tensor_copy(bsp[hi], brow[hi]))
                if r == 1:
                    own.step(tt(brow[hi], brow[hi], bsp[hi], ALU.subtract))
                if r == 2:
                    own.step(v.tensor_copy(bsp[hi], brow[hi]))
                    own.step(tt(brow[lo], brow[lo], bsp[lo], ALU.subtract))
                if r == 3:
                    v.tensor_copy(bsp[lo], brow[lo]).then_inc(bias_ready, 1)

            dve.wait_ge(tables, made["amask"])
            own.begin(0, 19)
            att_head(0, split_bias)
            own.end(1)
            with dve.Fori(1, H) as h:
                own.begin(h - 1, 14)
                att_head(h)
                own.end(H - 1)

            def merge_step(b):
                for u in range(2):
                    for j in range(2):
                        dve.wait_ge(w_used, MRG0 + N_MRG * b + 4 + 2 * u + j + 1)
                        dve.wait_ge(sg_ready, 4 * b + 2 * u + j + 1)
                        own.mark(tt(mgt[:, u, j, :], ps[:, 4 + 2 * u + j, :], sgm[:, u, j, :], ALU.mult))
                    own.settle()
                    tt(mergedT[:, bass.ds(2 * b + u, 1), :].rearrange("p a t -> p (a t)"), mgt[:, u, 0, :], mgt[:, u, 1, :],
                       ALU.add).then_inc(merged, 1)

            dve.wait_ge(am_round, 1)
            tt(attL[:], attT[:], attR[:], ALU.subtract).then_inc(am_split, 1)
            for c in range(2):
                dve.wait_ge(am_round, c + 2)
                at = (slice(None), slice(4 * c, 4 * c + 4))
                tt(memL[at], memT[at], memR[at], ALU.subtract).then_inc(am_split, 1)
            own.begin(0, 4)
            merge_step(0)
            own.end(1)
            with dve.Fori(1, KD // 2) as b:
                own.begin(b - 1, 4)
                merge_step(b)
                own.end(KD // 2 - 1)

            def add_mix(i):
                for n in range(2):
                    dve.wait_ge(mix_mm, 2 * i + n + 1)
                    dve.wait_ge(x_in[i], 2 * DMA)
                    hn = hres[:, i, n * BANK:(n + 1) * BANK]
                    tt(hn, hn, ps[:, 4 + 2 * (i % 2) + n, :], ALU.add).then_inc(h_ready, 1)

            def normed(i):
                dve.wait_ge(h_std, i + 1)
                own.step(v.reciprocal(rstd[:, 1, i:i + 1], ssq[:, 1, i:i + 1]))
                if i >= 2:
                    dve.wait_ge(hw_used, 2 * (i - 1))
                    dve.wait_ge(xn_stored[i - 2], DMA)
                stt(xw2[:, i % 2, :], hres[:, i, :], rstd[:, 1, i:i + 1], gffn[:], ALU.mult, ALU.mult).then_inc(hw_ready, 1)

            def normed_T(i):
                for b in range(2):
                    dve.wait_ge(hw_used, 2 * i + b + 1)
                    v.tensor_copy(xn2T[:, 4 * b:4 * b + 4, i * P:(i + 1) * P],
                                  ps[:, b, :].rearrange("p (k c) -> p k c", k=4)).then_inc(xn2T_ready, 1)

            def top(i):
                dve.wait_ge(lg_mm, i + 1)
                tt(lg[:, i, :], ps[:, 2 + i % 2, 0:E], brt[:], ALU.add).then_inc(lg_read, 1)
                if i == 0:
                    dve.wait_ge(mix_mm, 2 * NT)
                dve.wait_ge(lg_read, i + 1)
                own.step(v.max(v8[:, i, :], lg[:, i, :]))
                own.mark(v.max_index(i8[:, i, :], v8[:, i, :], lg[:, i, :]))

            add_mix(0)
            dve.wait_ge(router_in, 3 * DMA)
            normed(0)
            add_mix(1)
            normed(1)
            normed_T(0)
            add_mix(2)
            normed(2)
            normed_T(1)
            add_mix(3)
            normed(3)
            normed_T(2)
            top(0)
            normed_T(3)
            top(1)
            top(2)
            top(3)
            own.settle()
            own.mark(v.tensor_copy(i8f[:], i8[:]))
            tt(gk[:], v8[:, :, 0:TOP_K], v8[:, :, 0:1].to_broadcast([P, NT, TOP_K]), ALU.subtract).then_inc(top_ready, 1)
            own.settle()
            dve.wait_ge(late_tables, 1)
            full = [P, NT, TOP_K, E]
            own.step(tt(oh, iota_e[:].unsqueeze(1).unsqueeze(1).to_broadcast(full), i8f[:, :, 0:TOP_K].unsqueeze(3).to_broadcast(full),
                        ALU.is_equal))
            over_k = lambda t: t.rearrange("p i k e -> p i e k")
            own.step(v.tensor_reduce(member, over_k(oh), AX.X, ALU.add))
            v.tensor_copy(memb[:], member).then_inc(memb_ready, 1)
            own.step(tt(oht, oh, iota_k[:].unsqueeze(1).unsqueeze(3).to_broadcast(full), ALU.mult))
            own.step(v.tensor_reduce(kth, over_k(oht), AX.X, ALU.add))
            dve.wait_ge(gk_ready, 1)
            own.step(v.tensor_reduce(gs[:, 0, :], gk[:], AX.X, ALU.add))
            own.step(v.reciprocal(gs[:, 1, :], gs[:, 0, :]))
            own.step(tt(gk[:], gk[:], gs[:, 1, :].unsqueeze(2).to_broadcast([P, NT, TOP_K]), ALU.mult))
            own.step(tt(oht, oh, gk[:].unsqueeze(3).to_broadcast(full), ALU.mult))
            own.step(v.tensor_reduce(gte, over_k(oht), AX.X, ALU.add))
            entry = lambda n: tbl[:, 0:E, :, n].rearrange("p e i -> p i e")
            per_tok = lambda n: tokf[:, n, :].unsqueeze(2).to_broadcast([P, NT, E])
            v.tensor_copy(entry(3), gte).then_inc(tbl_ready, 1)
            tt(entry(1), member, per_tok(0), ALU.mult).then_inc(tbl_ready, 1)
            own.step(tt(oht[:, :, 0, :], member, per_tok(1), ALU.mult))
            tt(entry(2), oht[:, :, 0, :], kth, ALU.add).then_inc(tbl_ready, 1)
            dve.wait_ge(pos_mm, 1)
            own.step(ts(pos1, ps[:, 5, 0:NT * E].rearrange("p (i e) -> p i e", i=NT), 1.0, None, ALU.add))
            own.step(tt(pos1, pos1, member, ALU.mult))
            ts(entry(0), pos1, -1.0, None, ALU.add).then_inc(tbl_ready, 1)
            own.step(v.tensor_reduce(ovf[:], ps[:, 5, NT * E:(NT + 1) * E], AX.X, ALU.max))
            ts(flag[:], ovf[:], float(P), None, ALU.is_gt).then_inc(flag_ready, 1)

            def select(m, slots):
                dve.wait_ge(te_ready, m + 1)
                dve.wait_ge(meta_mm, m)
                for i in range(NT):
                    ts(sels[:, i, :], slots[:], te[:, i, 0:1], None, ALU.is_equal).then_inc(sel_ready, 1)

            def selected(e, m):
                dve.wait_ge(meta_mm, m + 1)
                ts(idx_of[:, bass.ds(e, 1), :].rearrange("p a c -> p (a c)"), ps[:, 6, 1:3], float(ABSENT), None, ALU.add).then_inc(meta_ready, 1)
                v.tensor_copy(gate_of[:, bass.ds(e, 1)], ps[:, 6, 3:4]).then_inc(meta_ready, 1)

            def rows(xi):
                for b, bank in enumerate((7, 6)):
                    dve.wait_ge(xTh_ready, 2 * xi + b + 1)
                    part = (slice(None), slice(4 * b, 4 * b + 4))
                    tt(xTl[part], ps[:, bank, :].rearrange("p (k c) -> p k c", k=4), xTh[part], ALU.subtract).then_inc(xT_ready, 1)

            def chunk_rest(gi, k):
                dve.wait_ge(gu_rounded, KD * gi + k + 1)
                tt(gul[:, k, :], guw[:, k, :], guh[k % 4][:], ALU.subtract).then_inc(gu_split, 1)

            hg = ps[:, 0:4, :].rearrange("p b (n c) -> p c (b n)", c=2)

            def gates_in(gi):
                dve.wait_ge(gu_used, KD * (gi + 1))
                ts(gt[:], hg[:, 0, :], SWIGLU_LIMIT, None, ALU.min).then_inc(gt_ready, 1)

            def ups_in(gi):
                ts(up[:], hg[:, 1, :], SWIGLU_LIMIT, -SWIGLU_LIMIT, ALU.min, ALU.max).then_inc(up_read, 1)

            def swiglu(gi):
                dve.wait_ge(sg_ready2, gi + 1)
                own.step(tt(gt[:], gt[:], sg[:], ALU.mult))
                stt(act[:], up[:], 1.0, gt[:], ALU.add, ALU.mult).then_inc(act_ready, 1)

            def expert_turn(e, last=False):
                for k in range(4, KD):
                    chunk_rest(e, k)
                select(e + 2, iota_slot)
                if not last:
                    for k in range(2):
                        chunk_rest(e + 1, k)
                gates_in(e)
                selected(e + 2, e + 2)
                ups_in(e)
                rows(e + 1)
                swiglu(e)
                if not last:
                    for k in range(2, 4):
                        chunk_rest(e + 1, k)

            select(0, iota_slot)
            selected(0, 0)
            for k in range(2):
                chunk_rest(0, k)
            select(1, iota_slot)
            rows(0)
            selected(1, 1)
            for k in range(2, 4):
                chunk_rest(0, k)
            own.begin(0, 1)
            expert_turn(0)
            own.end(1)
            with dve.Fori(1, E - 1) as e:
                own.begin(e - 1, 1)
                expert_turn(e)
                own.end(E - 2)
            own.begin(0, 1)
            expert_turn(E - 1, last=True)
            own.end(1)
            with dve.If(many(dve) > 0):
                common, own = own, Chain(dve, dve_over)
                v.tensor_copy(slot_b[:], iota_slot[:]).then_inc(slot_ready, 1)
                with dve.Fori(1, NT) as b:
                    dve.wait_ge(slot_ready, b)
                    ts(slot_b[:], slot_b[:], float(P), None, ALU.add).then_inc(slot_ready, 1)
                    dve.wait_ge(slot_ready, b + 1)
                    v.memset(tick[:], 0.0)
                    with dve.Fori(0, E) as e:
                        n = extra(b, e)
                        own.begin(n, 1)
                        select(E + 2 + n, slot_b)
                        selected(e, E + 2 + n)
                        rows(E + 1 + n)
                        for k in range(KD):
                            chunk_rest(E + n, k)
                        gates_in(E + n)
                        ups_in(E + n)
                        swiglu(E + n)
                        own.end((NT - 1) * E)
                own = common

            dve.wait_ge(gfin_in, DMA)

            def scaled_out(i):
                dve.wait_ge(f_std, i + 1)
                own.step(v.reciprocal(rstd[:, 2, i:i + 1], ssq[:, 2, i:i + 1]))
                stt(hres[:, i, :], hres[:, i, :], rstd[:, 2, i:i + 1], gfin, ALU.mult, ALU.mult).then_inc(o_ready, 1)

            for i in range(NT):
                dve.wait_ge(y_in[i], DMA)
                y = yfin[:, i, :]
                own.mark(tt(y[:, 0:D], y[:, 0:D], y[:, D:2 * D], ALU.add))
                own.step(tt(y[:, 2 * D:3 * D], y[:, 2 * D:3 * D], y[:, 3 * D:4 * D], ALU.add))
                own.step(tt(y[:, 0:D], y[:, 0:D], y[:, 2 * D:3 * D], ALU.add))
                tt(hres[:, i, :], hres[:, i, :], y[:, 0:D], ALU.add).then_inc(f_sum, 1)
                if i:
                    scaled_out(i - 1)
            scaled_out(NT - 1)


_INS = ['x', 'positions', 'g_mix', 'w_in', 'conv_qk', 'b_if', 'g_mlstm_norm', 'w_attn_out', 'w_mlstm_out', 'w_mix_out', 'g_ffn',
        'w_router', 'b_router', 'w_gate_up', 'b_gate_up', 'w_down', 'b_down', 'g_final']


def kernel(**inputs):
    import concourse.bacc as _bacc
    from concourse.bass_utils import run_bass_kernel_spmd as _run

    nc = _bacc.Bacc("TRN2", target_bir_lowering=False, num_devices=1)
    arrays, args = {}, []
    for name in _INS:
        a = np.ascontiguousarray(inputs[name])
        arrays[f"in_{name}"] = a
        args.append(nc.dram_tensor(f"in_{name}", a.shape, mybir.dt.from_np(a.dtype), kind="ExternalInput").ap())
    shape = arrays["in_x"].shape
    args.append(nc.dram_tensor("out_0", shape, F32, kind="ExternalOutput").ap())
    hybrid_block(nc, *args)
    r = _run(nc, [arrays], core_ids=[0])
    return r.results[0]["out_0"]
```
